# Optimizing a Trainium2 kernel written in Bass

```python
import math
import jax, jax.numpy as jnp
from jax import lax
import numpy as np

D_MODEL = 1024
BATCH = 1
SEQ = 256
DEPTH = 2

SSD_HEADS = 16
SSD_HEAD_DIM = 64
SSD_WIDTH = SSD_HEADS * SSD_HEAD_DIM
SSD_GROUPS = 4
SSD_STATE = 128
CONV_K = 4
SSD_CHUNK = 128
CONV_DIM = SSD_WIDTH + 2 * SSD_GROUPS * SSD_STATE

ATT_HEADS = 16
ATT_HEAD_DIM = 64
ATT_WIDTH = ATT_HEADS * ATT_HEAD_DIM
ATT_BRANCHES = ((128, 1), (512, 4), (2048, 16))
BAND_BLOCK = 128

MIX_WIDTH = SSD_WIDTH + ATT_WIDTH
IN_PROJ = SSD_WIDTH + CONV_DIM + SSD_HEADS + 3 * ATT_WIDTH
D_FF = 2816
EPS = 1e-6


def rms_norm(x, w):
    xf = x.astype(jnp.float32)
    y = xf * lax.rsqrt(jnp.mean(xf * xf, axis=-1, keepdims=True) + EPS)
    return (y * w.astype(jnp.float32)).astype(x.dtype)

def swiglu(x, w_gate, w_up, w_down):
    return (jax.nn.silu(x @ w_gate) * (x @ w_up)) @ w_down

def causal_depthwise_conv(x, w, b):
    c = x.shape[-1]
    y = lax.conv_general_dilated(
        x, w[:, None, :], window_strides=(1,), padding=[(CONV_K - 1, 0)],
        dimension_numbers=("NWC", "WIO", "NWC"), feature_group_count=c)
    return y + b

def ssd_mixer(xbc, dt_raw, z, dt_bias, a_log, d_skip, norm_w):
    out_dtype = z.dtype
    b, s, _ = xbc.shape
    H, P, G, N, L = SSD_HEADS, SSD_HEAD_DIM, SSD_GROUPS, SSD_STATE, SSD_CHUNK
    R = H // G
    nc = s // L
    xbc = xbc.astype(jnp.float32)
    xs, bm, cm = jnp.split(xbc, [SSD_WIDTH, SSD_WIDTH + G * N], axis=-1)
    dt = jax.nn.softplus(dt_raw.astype(jnp.float32) + dt_bias.astype(jnp.float32))
    a = -jnp.exp(a_log.astype(jnp.float32))
    xh = xs.reshape(b, s, H, P)
    X = (xh * dt[..., None]).reshape(b, nc, L, G, R, P)
    adt = (dt * a).reshape(b, nc, L, G, R).transpose(0, 3, 4, 1, 2)
    a_cum = jnp.cumsum(adt, axis=-1)
    Bc = bm.reshape(b, nc, L, G, N)
    Cc = cm.reshape(b, nc, L, G, N)
    causal = jnp.tril(jnp.ones((L, L), dtype=bool))
    seg = a_cum[..., :, None] - a_cum[..., None, :]
    lmat = jnp.where(causal, jnp.exp(jnp.where(causal, seg, 0.0)), 0.0)
    cb = jnp.einsum("bclgn,bcsgn->bgcls", Cc, Bc)
    y_diag = jnp.einsum("bgcls,bgrcls,bcsgrp->bclgrp", cb, lmat, X)
    decay_states = jnp.exp(a_cum[..., -1:] - a_cum)
    states = jnp.einsum("bclgn,bgrcl,bclgrp->bcgrpn", Bc, decay_states, X)
    chunk_decay = jnp.exp(a_cum[..., -1])

    def step(h, inp):
        st, dec = inp
        return h * dec[..., None, None] + st, h

    h0 = jnp.zeros((b, G, R, P, N), jnp.float32)
    _, prev = lax.scan(step, h0, (states.transpose(1, 0, 2, 3, 4, 5),
                                  chunk_decay.transpose(3, 0, 1, 2)))
    y_off = jnp.einsum("bclgn,cbgrpn,bgrcl->bclgrp", Cc, prev, jnp.exp(a_cum))
    y = (y_diag + y_off).reshape(b, s, H, P) + xh * d_skip.astype(jnp.float32)[:, None]
    y = y.reshape(b, s, SSD_WIDTH) * jax.nn.silu(z.astype(jnp.float32))
    yg = y.reshape(b, s, G, SSD_WIDTH // G)
    yg = yg * lax.rsqrt(jnp.mean(yg * yg, axis=-1, keepdims=True) + EPS)
    y = yg.reshape(b, s, SSD_WIDTH) * norm_w.astype(jnp.float32)
    return y.astype(out_dtype)

def dilated_branch(q, k, v, dilation, back):
    b, s, h, e = q.shape
    n = s // dilation
    nb = -(-n // BAND_BLOCK)
    npad = nb * BAND_BLOCK
    blk = BAND_BLOCK

    def blocks(t):
        t = t.reshape(b, n, dilation, h, e)
        t = jnp.pad(t, ((0, 0), (0, npad - n), (0, 0), (0, 0), (0, 0)))
        return t.reshape(b, nb, blk, dilation, h, e)

    def with_prev(t):
        prev = jnp.pad(t[:, :-1], ((0, 0), (1, 0), (0, 0), (0, 0), (0, 0), (0, 0)))
        return jnp.concatenate([prev, t], axis=2)

    qb = blocks(q)
    kk = with_prev(blocks(k))
    vv = with_prev(blocks(v))
    scores = jnp.einsum("bnqrhe,bnkrhe->bnrhqk", qb, kk).astype(jnp.float32)
    scores = scores * (1.0 / math.sqrt(e))
    qi = jnp.arange(blk)[:, None]
    kj = jnp.arange(2 * blk)[None, :]
    dist = qi + blk - kj
    bidx = jnp.arange(nb)[:, None, None]
    valid = (dist >= 0) & (dist <= back) & (bidx * blk - blk + kj >= 0)
    scores = jnp.where(valid[None, :, None, None], scores, -jnp.inf)
    m = jnp.max(scores, axis=-1, keepdims=True)
    p = jnp.exp(scores - m)
    den = jnp.sum(p, axis=-1, keepdims=True)
    o = jnp.einsum("bnrhqk,bnkrhe->bnqrhe", (p / den).astype(v.dtype), vv)
    lse = (m + jnp.log(den))[..., 0]
    o = o.reshape(b, npad, dilation, h, e)[:, :n].reshape(b, s, h, e)
    lse = lse.transpose(0, 1, 4, 2, 3).reshape(b, npad, dilation, h)[:, :n].reshape(b, s, h)
    return o, lse

def dilated_attention(q, k, v):
    outs, lses = [], []
    for window, dilation in ATT_BRANCHES:
        o, lse = dilated_branch(q, k, v, dilation, window // dilation)
        outs.append(o)
        lses.append(lse)
    wts = jax.nn.softmax(jnp.stack(lses, axis=0), axis=0)
    y = jnp.einsum("kbsh,kbshe->bshe", wts.astype(q.dtype), jnp.stack(outs, axis=0))
    return y

def first_inputs(seed: int = 0) -> dict:
    key = jax.random.key(seed)
    ks = jax.random.split(key, 24)
    f = jnp.float32

    def normal(k, shape, scale):
        return jax.random.normal(k, shape, f) * scale

    def gain(k, shape):
        return 1.0 + 0.02 * jax.random.normal(k, shape, f)

    dt = jnp.exp(jax.random.uniform(ks[10], (DEPTH, SSD_HEADS), f)
                 * (math.log(0.1) - math.log(0.001)) + math.log(0.001))
    return {
        "x": jax.random.normal(ks[0], (BATCH, SEQ, D_MODEL), f),
        "ffn1_norm": gain(ks[1], (DEPTH, D_MODEL)),
        "ffn1_w_gate": normal(ks[2], (DEPTH, D_MODEL, D_FF), D_MODEL ** -0.5),
        "ffn1_w_up": normal(ks[3], (DEPTH, D_MODEL, D_FF), D_MODEL ** -0.5),
        "ffn1_w_down": normal(ks[4], (DEPTH, D_FF, D_MODEL), D_FF ** -0.5),
        "mix_norm": gain(ks[5], (DEPTH, D_MODEL)),
        "w_in": normal(ks[6], (DEPTH, D_MODEL, IN_PROJ), D_MODEL ** -0.5),
        "conv_w": normal(ks[7], (DEPTH, CONV_K, CONV_DIM), CONV_K ** -0.5),
        "conv_b": normal(ks[8], (DEPTH, CONV_DIM), 0.02),
        "dt_bias": dt + jnp.log(-jnp.expm1(-dt)),
        "a_log": jnp.log(jax.random.uniform(ks[11], (DEPTH, SSD_HEADS), f, 1.0, 16.0)),
        "d_skip": gain(ks[12], (DEPTH, SSD_HEADS)),
        "ssd_norm": gain(ks[13], (DEPTH, SSD_WIDTH)),
        "q_norm": gain(ks[14], (DEPTH, ATT_HEAD_DIM)),
        "k_norm": gain(ks[15], (DEPTH, ATT_HEAD_DIM)),
        "w_out": normal(ks[16], (DEPTH, MIX_WIDTH, D_MODEL), MIX_WIDTH ** -0.5),
        "ffn2_norm": gain(ks[17], (DEPTH, D_MODEL)),
        "ffn2_w_gate": normal(ks[18], (DEPTH, D_MODEL, D_FF), D_MODEL ** -0.5),
        "ffn2_w_up": normal(ks[19], (DEPTH, D_MODEL, D_FF), D_MODEL ** -0.5),
        "ffn2_w_down": normal(ks[20], (DEPTH, D_FF, D_MODEL), D_FF ** -0.5),
    }

def first_block(x, ffn1_norm, ffn1_w_gate, ffn1_w_up, ffn1_w_down, mix_norm, w_in,
              conv_w, conv_b, dt_bias, a_log, d_skip, ssd_norm, q_norm, k_norm,
              w_out, ffn2_norm, ffn2_w_gate, ffn2_w_up, ffn2_w_down):
    b, s, _ = x.shape
    splits = np.cumsum([SSD_WIDTH, CONV_DIM, SSD_HEADS, ATT_WIDTH, ATT_WIDTH]).tolist()
    for i in range(DEPTH):
        x = x + 0.5 * swiglu(rms_norm(x, ffn1_norm[i]), ffn1_w_gate[i], ffn1_w_up[i], ffn1_w_down[i])
        h = rms_norm(x, mix_norm[i])
        proj = h @ w_in[i]
        z, xbc, dt_raw, q, k, v = jnp.split(proj, splits, axis=-1)
        xbc = jax.nn.silu(causal_depthwise_conv(xbc, conv_w[i], conv_b[i]))
        y_ssd = ssd_mixer(xbc, dt_raw, z, dt_bias[i], a_log[i], d_skip[i], ssd_norm[i])
        q = rms_norm(q.reshape(b, s, ATT_HEADS, ATT_HEAD_DIM), q_norm[i])
        k = rms_norm(k.reshape(b, s, ATT_HEADS, ATT_HEAD_DIM), k_norm[i])
        v = v.reshape(b, s, ATT_HEADS, ATT_HEAD_DIM)
        y_att = dilated_attention(q, k, v).reshape(b, s, ATT_WIDTH)
        x = x + jnp.concatenate([y_ssd, y_att], axis=-1) @ w_out[i]
        x = x + 0.5 * swiglu(rms_norm(x, ffn2_norm[i]), ffn2_w_gate[i], ffn2_w_up[i], ffn2_w_down[i])
    return x


DEPTH_2 = 1

CONV_DIM_2 = 512
CONV_WIDTH = 31
GLA_HEADS = 4
GLA_DK = 128
GLA_DV = 256
GLA_LOWRANK = 16
GLA_TAU = 16.0
GLA_CHUNK = 64
QK_DIM = GLA_HEADS * GLA_DK
V_DIM = GLA_HEADS * GLA_DV
N_BRANCH = 2
N_GROUPS = 4
EXPERTS_PER_GROUP = 8
N_EXPERTS = N_GROUPS * EXPERTS_PER_GROUP
TOP_K = 2
D_EXPERT = 512
N_MOD = 6
IN_SIZES = (2 * CONV_DIM_2, QK_DIM, QK_DIM, V_DIM, V_DIM, GLA_LOWRANK, N_BRANCH * D_MODEL)
IN_DIM = 2 * CONV_DIM_2 + 2 * QK_DIM + 2 * V_DIM + GLA_LOWRANK + N_BRANCH * D_MODEL


def rmsnorm(x, g):
    x32 = x.astype(jnp.float32)
    y = x32 * lax.rsqrt(jnp.mean(x32 * x32, axis=-1, keepdims=True) + EPS)
    return (y * g.astype(jnp.float32)).astype(x.dtype)

def layernorm(x, g, b):
    x32 = x.astype(jnp.float32)
    mu = jnp.mean(x32, axis=-1, keepdims=True)
    xc = x32 - mu
    var = jnp.mean(xc * xc, axis=-1, keepdims=True)
    y = xc * lax.rsqrt(var + EPS) * g.astype(jnp.float32) + b.astype(jnp.float32)
    return y.astype(x.dtype)

def modulate(x, shift, scale):
    return x * (1.0 + scale[:, None, :]) + shift[:, None, :]

def conv_module(u, w_dw, b_dw, ln_g, ln_b, w_pw, b_pw):
    a, gt = jnp.split(u, 2, axis=-1)
    z = a * jax.nn.sigmoid(gt)
    z = lax.conv_general_dilated(
        z, w_dw, window_strides=(1,), padding=[(CONV_WIDTH - 1, 0)],
        dimension_numbers=("NWC", "WIO", "NWC"), feature_group_count=CONV_DIM_2) + b_dw
    z = jax.nn.silu(layernorm(z, ln_g, ln_b))
    return z @ w_pw + b_pw

def gla_chunked(q, k, v, logg):
    B, S, H, _ = q.shape
    n_chunks = S // GLA_CHUNK

    def to_chunks(t):
        return t.reshape(B, n_chunks, GLA_CHUNK, H, t.shape[-1]).transpose(1, 0, 3, 2, 4)

    causal = jnp.tril(jnp.ones((GLA_CHUNK, GLA_CHUNK), dtype=bool))[:, :, None]

    def step(state, inp):
        qc, kc, vc, gc = inp
        b = jnp.cumsum(gc, axis=2)
        o_inter = jnp.einsum("bhcd,bhde->bhce", qc * jnp.exp(b), state)
        diff = b[:, :, :, None, :] - b[:, :, None, :, :]
        decay = jnp.exp(jnp.where(causal, diff, -jnp.inf))
        attn = jnp.einsum("bhid,bhijd,bhjd->bhij", qc, decay, kc)
        o_intra = jnp.einsum("bhij,bhje->bhie", attn, vc)
        b_last = b[:, :, -1:, :]
        new_state = (jnp.exp(b_last[:, :, 0, :])[..., None] * state
                     + jnp.einsum("bhcd,bhce->bhde", kc * jnp.exp(b_last - b), vc))
        return new_state, o_inter + o_intra

    state0 = jnp.zeros((B, H, q.shape[-1], v.shape[-1]), jnp.float32)
    _, outs = lax.scan(step, state0, (to_chunks(q), to_chunks(k), to_chunks(v), to_chunks(logg)))
    return outs.transpose(1, 0, 3, 2, 4).reshape(B, S, H, v.shape[-1])

def hybrid_mixer(u, w_in, w_dw, b_dw, g_conv_ln, b_conv_ln, w_conv_pw, b_conv_pw,
                 w_a2, b_a2, g_gla_norm, w_gla_o, w_out):
    B, S, _ = u.shape
    proj = u @ w_in
    offs = np.cumsum(IN_SIZES)[:-1].tolist()
    p_conv, q, k, v, r, a1, gates = jnp.split(proj, offs, axis=-1)
    y_conv = conv_module(p_conv, w_dw, b_dw, g_conv_ln, b_conv_ln, w_conv_pw, b_conv_pw)
    q = q.reshape(B, S, GLA_HEADS, GLA_DK).astype(jnp.float32) * (GLA_DK ** -0.5)
    k = k.reshape(B, S, GLA_HEADS, GLA_DK).astype(jnp.float32)
    v = v.reshape(B, S, GLA_HEADS, GLA_DV).astype(jnp.float32)
    logg = jax.nn.log_sigmoid((a1 @ w_a2 + b_a2).astype(jnp.float32)) / GLA_TAU
    logg = logg.reshape(B, S, GLA_HEADS, GLA_DK)
    o = gla_chunked(q, k, v, logg)
    o = rmsnorm(o, g_gla_norm.reshape(GLA_HEADS, GLA_DV)).reshape(B, S, V_DIM).astype(u.dtype)
    y_gla = (o * jax.nn.silu(r)) @ w_gla_o
    gt = jax.nn.sigmoid(gates).reshape(B, S, N_BRANCH, D_MODEL)
    merged = gt[:, :, 0, :] * y_conv + gt[:, :, 1, :] * y_gla
    return merged @ w_out

def hierarchical_moe(h, w_rg, b_rg, w_re, b_re, w1, w3, w2):
    B, S, D = h.shape
    t = h.reshape(B * S, D)
    lg = (t @ w_rg + b_rg).astype(jnp.float32)
    pg = jax.nn.softmax(lg, axis=-1)
    _, gsel = lax.top_k(lg, 1)
    wg = jnp.take_along_axis(pg, gsel, axis=1)
    le = (t @ w_re + b_re).astype(jnp.float32).reshape(-1, N_GROUPS, EXPERTS_PER_GROUP)
    le_sel = jnp.take_along_axis(le, gsel[:, :, None], axis=1)[:, 0, :]
    top_v, top_i = lax.top_k(le_sel, TOP_K)
    w = jax.nn.softmax(top_v, axis=-1) * wg
    eid = gsel * EXPERTS_PER_GROUP + top_i
    comb = jnp.einsum("tk,tke->te", w, jax.nn.one_hot(eid, N_EXPERTS, dtype=jnp.float32))
    y = jnp.zeros((B * S, D), jnp.float32)
    for e in range(N_EXPERTS):
        hid = jax.nn.silu(t @ w1[e]) * (t @ w3[e])
        y = y + comb[:, e:e + 1] * (hid @ w2[e]).astype(jnp.float32)
    return y.astype(h.dtype).reshape(B, S, D)

def second_inputs(seed: int = 0) -> dict:
    key = jax.random.key(seed)
    ks = jax.random.split(key, 32)
    f32 = jnp.float32
    L, D = DEPTH_2, D_MODEL

    def nrm(k, shape, scale):
        return jax.random.normal(k, shape, f32) * scale

    def gain(k, shape):
        return 1.0 + 0.05 * jax.random.normal(k, shape, f32)

    return {
        "x": jax.random.normal(ks[0], (BATCH, SEQ, D), f32),
        "c": jax.random.normal(ks[1], (BATCH, D), f32),
        "w_ada": nrm(ks[2], (L, D, N_MOD * D), 0.5 * D ** -0.5),
        "b_ada": nrm(ks[3], (L, N_MOD * D), 0.02),
        "g_norm1": gain(ks[4], (L, D)),
        "w_in": nrm(ks[5], (L, D, IN_DIM), D ** -0.5),
        "w_dw": nrm(ks[6], (L, CONV_WIDTH, 1, CONV_DIM_2), CONV_WIDTH ** -0.5),
        "b_dw": nrm(ks[7], (L, CONV_DIM_2), 0.02),
        "g_conv_ln": gain(ks[8], (L, CONV_DIM_2)),
        "b_conv_ln": nrm(ks[9], (L, CONV_DIM_2), 0.02),
        "w_conv_pw": nrm(ks[10], (L, CONV_DIM_2, D), CONV_DIM_2 ** -0.5),
        "b_conv_pw": nrm(ks[11], (L, D), 0.02),
        "w_a2": nrm(ks[12], (L, GLA_LOWRANK, QK_DIM), GLA_LOWRANK ** -0.5),
        "b_a2": nrm(ks[13], (L, QK_DIM), 0.02),
        "g_gla_norm": gain(ks[14], (L, V_DIM)),
        "w_gla_o": nrm(ks[15], (L, V_DIM, D), V_DIM ** -0.5),
        "w_out": nrm(ks[16], (L, D, D), D ** -0.5),
        "g_norm2": gain(ks[17], (L, D)),
        "w_router_g": nrm(ks[18], (L, D, N_GROUPS), D ** -0.5),
        "b_router_g": nrm(ks[19], (L, N_GROUPS), 0.01),
        "w_router_e": nrm(ks[20], (L, D, N_EXPERTS), D ** -0.5),
        "b_router_e": nrm(ks[21], (L, N_EXPERTS), 0.01),
        "w1": nrm(ks[22], (L, N_EXPERTS, D, D_EXPERT), D ** -0.5),
        "w3": nrm(ks[23], (L, N_EXPERTS, D, D_EXPERT), D ** -0.5),
        "w2": nrm(ks[24], (L, N_EXPERTS, D_EXPERT, D), D_EXPERT ** -0.5),
        "w_ada_f": nrm(ks[25], (D, 2 * D), 0.5 * D ** -0.5),
        "b_ada_f": nrm(ks[26], (2 * D,), 0.02),
        "g_final": gain(ks[27], (D,)),
    }

def second_block(x, c, w_ada, b_ada, g_norm1, w_in, w_dw, b_dw, g_conv_ln, b_conv_ln,
              w_conv_pw, b_conv_pw, w_a2, b_a2, g_gla_norm, w_gla_o, w_out, g_norm2,
              w_router_g, b_router_g, w_router_e, b_router_e, w1, w3, w2,
              w_ada_f, b_ada_f, g_final):
    h = x
    c_act = jax.nn.silu(c)
    for l in range(DEPTH_2):
        mod = c_act @ w_ada[l] + b_ada[l]
        sh1, sc1, ga1, sh2, sc2, ga2 = jnp.split(mod, N_MOD, axis=-1)
        u = modulate(rmsnorm(h, g_norm1[l]), sh1, sc1)
        y = hybrid_mixer(u, w_in[l], w_dw[l], b_dw[l], g_conv_ln[l], b_conv_ln[l],
                         w_conv_pw[l], b_conv_pw[l], w_a2[l], b_a2[l], g_gla_norm[l],
                         w_gla_o[l], w_out[l])
        h = h + ga1[:, None, :] * y
        u2 = modulate(rmsnorm(h, g_norm2[l]), sh2, sc2)
        y2 = hierarchical_moe(u2, w_router_g[l], b_router_g[l], w_router_e[l], b_router_e[l],
                              w1[l], w3[l], w2[l])
        h = h + ga2[:, None, :] * y2
    modf = c_act @ w_ada_f + b_ada_f
    shf, scf = jnp.split(modf, 2, axis=-1)
    return modulate(rmsnorm(h, g_final), shf, scf)


def setup_inputs(seed=0):
    out = dict(first_inputs(seed))
    for name, value in second_inputs(seed + 1).items():
        if name != "x":
            out[name + "_2"] = value
    return out


def reference(
    x, ffn1_norm, ffn1_w_gate, ffn1_w_up, ffn1_w_down, mix_norm, w_in, conv_w, conv_b, dt_bias,
    a_log, d_skip, ssd_norm, q_norm, k_norm, w_out, ffn2_norm, ffn2_w_gate, ffn2_w_up,
    ffn2_w_down, c_2, w_ada_2, b_ada_2, g_norm1_2, w_in_2, w_dw_2, b_dw_2, g_conv_ln_2,
    b_conv_ln_2, w_conv_pw_2, b_conv_pw_2, w_a2_2, b_a2_2, g_gla_norm_2, w_gla_o_2, w_out_2,
    g_norm2_2, w_router_g_2, b_router_g_2, w_router_e_2, b_router_e_2, w1_2, w3_2, w2_2,
    w_ada_f_2, b_ada_f_2, g_final_2,
):
    x = first_block(
        x, ffn1_norm, ffn1_w_gate, ffn1_w_up, ffn1_w_down, mix_norm, w_in, conv_w, conv_b,
        dt_bias, a_log, d_skip, ssd_norm, q_norm, k_norm, w_out, ffn2_norm, ffn2_w_gate,
        ffn2_w_up, ffn2_w_down,
    )
    return second_block(
        x, c_2, w_ada_2, b_ada_2, g_norm1_2, w_in_2, w_dw_2, b_dw_2, g_conv_ln_2, b_conv_ln_2,
        w_conv_pw_2, b_conv_pw_2, w_a2_2, b_a2_2, g_gla_norm_2, w_gla_o_2, w_out_2, g_norm2_2,
        w_router_g_2, b_router_g_2, w_router_e_2, b_router_e_2, w1_2, w3_2, w2_2, w_ada_f_2,
        b_ada_f_2, g_final_2,
    )


_drawn_inputs = setup_inputs


def setup_inputs(seed=0):
    import zlib

    import numpy as np

    out = dict(_drawn_inputs(seed))
    spreads = {}
    factors = {'ffn1_norm': 3.5,
     'd_skip': 5.963,
     'ssd_norm': 3.205,
     'q_norm': 8.0,
     'k_norm': 8.0,
     'ffn2_norm': 5.293,
     'b_ada_2': 4.612,
     'g_norm1_2': 6.376,
     'b_dw_2': 64.0,
     'g_conv_ln_2': 64.0,
     'b_conv_ln_2': 200.0,
     'b_conv_pw_2': 157.92,
     'w_a2_2': 3.524,
     'b_a2_2': 34.582,
     'g_gla_norm_2': 8.0,
     'g_norm2_2': 5.044,
     'b_router_g_2': 22.965,
     'b_router_e_2': 80.078}
    for name, (base, spread) in spreads.items():
        noise = np.random.default_rng([zlib.crc32(name.encode()), seed]).standard_normal(out[name].shape)
        drawn = base * np.exp(spread * noise) if base else spread * noise
        out[name] = __import__('jax').numpy.asarray(drawn.astype(out[name].dtype))
    for name, factor in factors.items():
        out[name] = (out[name] * factor).astype(out[name].dtype)
    return out
```

```python
from contextlib import ExitStack

import concourse.bass as bass
from concourse import mybir
import numpy as np

F32 = mybir.dt.float32
F32R = mybir.dt.float32r
U32 = mybir.dt.uint32
ALU = mybir.AluOpType
ACT = mybir.ActivationFunctionType
AX_X = mybir.AxisListType.X

P = 128
SEQ = 256
NT = SEQ // P
D = 1024
KD = D // P
DEPTH = 2
D_FF = 2816
NF = D_FF // P
EPS = 1e-6
HEADS = 16
HD = 64
GROUPS = 4
HPG = HEADS // GROUPS
CONV_K = 4
XBC = 2048
NX = XBC // P
BLK = 256
BACK = 128
DILATIONS = (1, 4, 16)
NEG = -1e30

ARENA = 32512
SLOTS = 4
SLOT = KD * BLK
SLOT_D = D
LOAD = 16

C_FFN1, C_MIX, C_FFN2, C_CW, C_CB, C_SSD, C_QN, C_KN = 0, 8, 16, 24, 88, 104, 112, 113
N_COLA = 114


CW2 = 512
NC2 = CW2 // P
CONV_W = 31
GH = 4
DK = 128
DV = 256
RANK = 16
TAU = 16.0
QK0, V0, R0, A0, G0 = 1024, 2048, 3072, 4096, 4112
N_PROJ2 = 24
N_GROUPS = 4
PER_GROUP = 8
EXPERTS = N_GROUPS * PER_GROUP
D_EXPERT = 512
CPE = D_EXPERT // P
CAP = 64
LEVELS = (64, 32, 16, 8, 4, 2, 1)
PIECES = 8
SH1, SC1, GA1, SH2, SC2, GA2, SHF, SCF = range(PIECES)

B_ADA, B_C, B_N1, B_N2, B_NF, B_PW, B_GLA, B_DW, B_LG, B_LB, B_A2 = 0, 64, 72, 80, 88, 96, 104, 112, 116, 120, 124
N_COLC = CONV_W * NC2

K_ID, K_TRI, K_NEG, K_CNT, K_IOTA = 0, 128, 256, 640, 1024
N_CONST = 1088


def constants():
    t = np.arange(P)[:, None]
    out = [np.eye(P), (np.arange(P)[:, None] <= np.arange(P)[None, :])]
    cnts = []
    for tile, keys in ((0, P), (1, 2 * P)):
        d = t + tile * P - np.arange(keys)[None, :]
        cnts.append(sum(((d >= 0) & (d % r == 0) & (d // r <= BACK)).astype(np.float32) for r in DILATIONS))
    cnt = np.concatenate(cnts, 1)
    iota = np.broadcast_to(np.arange(CAP), (P, CAP))
    return np.ascontiguousarray(np.concatenate(out + [np.where(cnt > 0, 0.0, NEG), cnt, iota], 1).astype(np.float32))


def pair_masks():
    j, i = np.arange(P)[:, None], np.arange(P)[None, :]
    out = [(j // (2 * s) == i // (2 * s)) & (j % (2 * s) < s) & (i % (2 * s) >= s) for s in LEVELS] + [j == i]
    return np.ascontiguousarray(np.concatenate(out, 1).astype(np.float32))


class Order:

    def __init__(self, phases):
        self.first, n = {}, 0
        for name, uses in phases:
            self.first[name] = n
            n += uses
        self.total = n

    def __getitem__(self, name):
        return self.first[name]


def attention_fills():
    order = []
    for h in range(HEADS + 2):
        if h < HEADS:
            order.append(("S", h))
        if h >= 2:
            order.append(("T", h - 2))
    return {step: i for i, step in enumerate(order)}


def two_blocks(nc, d, out):
    fills = [("params", 4)]
    slots, rows_d = [], []
    for l in range(DEPTH):
        fills += [(("norm", 3 * l), 4), (("ffn", 2 * l), NF), (("mod", 4 * l), 1), (("norm", 3 * l + 1), 4),
                  (("xbc", l), 8), (("dt", l), 1), (("z", l), 4), (("qkv", l), 12), (("mod", 4 * l + 1), 1),
                  (("acum", l), 1), (("xt", l), 4), (("bt", l), 1), (("qkt", l), 8), (("cb", l), 2),
                  (("bc", l), 8), (("state", l), 2), (("off", l), 2), (("att", l), 2 * HEADS),
                  (("yt", l), 8), (("mod", 4 * l + 2), 1), (("norm", 3 * l + 2), 4), (("ffn", 2 * l + 1), NF),
                  (("mod", 4 * l + 3), 1)]
        slots += [(("ffn", 2 * l), NF), (("win", l), 24), (("wout", l), 8), (("ffn", 2 * l + 1), NF)]
        rows_d += [(("ffn", 2 * l), NF), (("ffn", 2 * l + 1), NF)]
    U1 = 3 * DEPTH
    A1 = 5 * DEPTH
    fills += [(("norm", U1), 4), ("a1", 1), ("a2", 2), ("qk2", 4), ("v2", 4), ("pc", 4), ("r", 4), ("gates", 8),
              ("pairs", 2 * len(LEVELS) + 2), ("cross", 1), ("o", GH), ("osum", 2),
              ("mean", 1), ("var", 1), (("pwa", 0), 1), (("pwb", 0), 1), (("pwa", 1), 1), (("pwb", 1), 1), ("ygla", 4), ("garow", 2), (("norm", U1 + 1), 4), ("router", 1),
              ("rows", 10), ("count", 1), ("moe", EXPERTS * CPE)]
    slots += [("win2", N_PROJ2), ("pw", 2), ("glao", 4), ("wout2", 4), ("moe", EXPERTS * CPE // 2)]
    rows_d += [("moe", EXPERTS * CPE // 2)]
    BLOCKS = ("xbc", "z", "qkv", "qk2", "v2", "pc", "r", "gates", "ygla", "pwb")
    FILL, RING, ROWD = Order(fills), Order(slots), Order(rows_d)
    AF = attention_fills()

    ctx = ExitStack()
    with ctx:
        def sb(name, shape, dt=F32):
            return ctx.enter_context(nc.sbuf_tensor(name, shape, dt))

        def sem(name):
            return ctx.enter_context(nc.semaphore(name))

        with nc.sbuf_tensor("ring", [P, SLOTS, SLOT], F32) as ring, \
                nc.sbuf_tensor("ring_d", [P, SLOTS, SLOT_D], F32) as ring_d, \
                nc.sbuf_tensor("arena", [P, ARENA], F32) as arena:
            pass
        ring_low = sb("ring_low", [P, SLOTS, SLOT], F32R)
        ring_d_low = sb("ring_d_low", [P, SLOTS, SLOT_D], F32R)
        low_at = [0]

        def beside(to):
            if to > low_at[0]:
                sb(f"pad{to}", [P, to - low_at[0]])
            low_at[0] = to

        def over(name, shape):
            low_at[0] += int(np.prod(shape))
            return sb(name, [P] + shape, F32R)

        A_HIGH = 2 * 2 * SEQ + NT * D
        A_HID = A_HIGH + NX * (SEQ + CONV_K - 1) + NX * SEQ + 3 * NT * D
        A_X = A_HIGH + NX * (SEQ + CONV_K - 1) + NX * SEQ + 4 * NT * D
        beside(A_HIGH)
        high_b = over("high_b", [SLOTS, SLOT])
        high_r = over("high_r", [SLOTS, SLOT_D])
        beside(A_HID)
        hidh, hidl = over("hidh", [2, SEQ]), over("hidl", [2, SEQ])
        beside(A_X)
        xh, xl = over("xh", [KD, SEQ]), over("xl", [KD, SEQ])
        beside(ARENA)
        x = sb("x", [P, NT, D])
        xnT = sb("xnT", [P, KD, SEQ])
        konst = sb("konst", [P, N_CONST])
        ones = sb("ones", [P, P])
        cola = sb("cola", [P, 2, N_COLA])
        heads3 = sb("heads3", [P, 3, DEPTH, HEADS])
        wdt = sb("wdt", [P, DEPTH, KD, HEADS])
        colb = sb("colb", [P, P])
        colc = sb("colc", [P, N_COLC])
        wa1 = sb("wa1", [P, KD, RANK])
        wa2 = sb("wa2", [RANK, GH * DK])
        wr = sb("wr", [P, KD, N_GROUPS + EXPERTS])
        br = sb("br", [P, N_GROUPS + EXPERTS])
        mod = sb("mod", [P, PIECES, KD])
        gains = sb("gains", [P, 3, KD])
        cact = sb("cact", [P, KD])
        N_PARAMS = 1 + 3 + 1 + DEPTH * 8 + 12 + 1 + 1 + 1 + 2 + 2
        at = [0]

        def part(shape):
            n = int(np.prod(shape))
            v = arena[:, at[0]:at[0] + n]
            at[0] += n
            if len(shape) == 2:
                v = v.rearrange("p (a b) -> p a b", a=shape[0])
            elif len(shape) == 3:
                v = v.rearrange("p (a b c) -> p a b c", a=shape[0], b=shape[1])
            return v

        stat = sb("stat", [P, 64])
        ss, std, rstd = stat[:, 0:2], stat[:, 2:4], stat[:, 4:6]
        gate_s = part([2, SEQ])
        hid = part([2, SEQ])
        xsc = part([NT, D])
        yatt = xsc
        here = at[0]
        xraw = part([NX, SEQ + CONV_K - 1])
        after = at[0]
        at[0] = here
        xtok = part([NT, D])
        xdt = part([NT, D])
        at[0] = max(after, at[0])
        here = at[0]
        xc = part([NX, SEQ])
        after = at[0]
        at[0] = here
        xdec = part([D])
        prev = part([GROUPS, BLK])
        at[0] = after
        z = part([NT, D])
        here = at[0]
        qk = part([NT, 2 * D])
        v = part([NT, D])
        at[0] = here
        yT = part([2 * KD, SEQ])
        at[0] = here + 3 * NT * D
        assert at[0] == A_X
        qT = part([KD, SEQ])
        kT = part([KD, SEQ])
        btok = part([GROUPS, P])
        seg = part([2, HPG * P])
        cbm = part([2, GROUPS, P])
        sp3 = part([3, 3 * P])
        pT = part([2, 3 * P])
        small = part([768])
        sm = [0]

        def tiny(n):
            sm[0] += n
            return small[:, sm[0] - n:sm[0]]

        dr, dn, de, dl, dtv, ea, adt, nac, ex, dd, dec = (tiny(32) for _ in range(11))
        rq, rqs, rqr = tiny(64), tiny(64), tiny(64)
        gs, gss, gsr = tiny(8), tiny(8), tiny(8)
        mx, nmx, den, rden = tiny(32), tiny(32), tiny(32), tiny(32)
        w_ada = part([2, D])
        ada = part([D])
        assert at[0] <= ARENA, at[0]

        at[0] = 2 * 2 * SEQ + NT * D
        masks = part([len(LEVELS) + 1, P])
        q2k2 = part([2 * GH, SEQ])
        v2 = part([NT, D])
        pc = part([2 * NC2, SEQ])
        rT = part([KD, SEQ])
        gT = part([2 * KD, SEQ])
        a1T = part([SEQ])
        graw = part([GH, SEQ])
        bcum = part([GH, SEQ])
        here = at[0]
        lev_e = part([2, GH * SEQ])
        lev_qk = part([2, GH * SEQ])
        at[0] = here
        merged = part([KD, SEQ])
        at[0] = here + 4 * GH * SEQ
        attn = part([2 * GH, P])
        across = part([GH, P])
        oT = part([KD, SEQ])
        osq = part([KD, SEQ])
        zpad = part([NC2, SEQ + CONV_W - 1])
        zc = part([NC2, SEQ])
        zsq = part([NC2, SEQ])
        mean = part([SEQ])
        assert at[0] <= ARENA, at[0]
        rg = graw
        rgs = bcum
        onesr = lev_e
        diag = osq.rearrange("p a b -> p (a b)")[:, 0:D]
        garow = pc.rearrange("p a b -> p (a b)")[:, 0:D]
        y2 = v2
        rt = [0]

        def route(n, t=NT):
            rt[0] += t * n
            return rT.rearrange("p a b -> p (a b)")[:, rt[0] - t * n:rt[0]].rearrange("p (t e) -> p t e", t=t)

        row2 = q2k2.rearrange("p a b -> p (a b)").rearrange("p (a b) -> p a b", a=2)
        EP = EXPERTS + 2
        comb, place = route(EP), route(EP)
        logit = route(N_GROUPS + EXPERTS)
        number = route(1)
        at[0] = here
        u2 = part([NT, D])
        sel = part([2, NT, CAP])
        selw = part([NT, 2 * CAP])
        selT = part([SEQ])
        ueT = part([2, KD, CAP])
        gate_e = part([4, 2 * CAP])
        hid_e = part([CPE, 2 * CAP])
        out_e = part([D])
        late = at[0]
        more = [arena[:, late + q * SLOT:late + (q + 1) * SLOT] for q in range(3)]
        more.append(pc.rearrange("p a b -> p (a b)"))
        spare = late + 3 * SLOT
        assert spare + SLOT_D <= ARENA
        flat2 = row2.rearrange("p a b -> p (a b)")
        more_d = [arena[:, spare:spare + SLOT_D], flat2[:, 0:SLOT_D], flat2[:, SLOT_D:2 * SLOT_D],
                  masks.rearrange("p a b -> p (a b)")]
        flag = sb("flag", [P, 1], mybir.dt.int32)
        cand, mark1, mark2 = route(EXPERTS), route(EXPERTS), route(EXPERTS)
        rt_og, rt_gd, rt_ge, rt_pen = (route(N_GROUPS) for _ in range(4))
        rt_mg, rt_m1, rt_m2, rt_m, rt_r, rt_pd, rt_pe = (route(1) for _ in range(7))
        rank = route(EXPERTS, 1)[:, 0, :]
        rows = gT.rearrange("p a b -> p (a b)")[:, 0:4 * P].rearrange("p (a b) -> p a b", a=4)
        rowf = gT.rearrange("p a b -> p (a b)")[:, 0:3 * D].rearrange("p (a b) -> p a b", a=3)

        acc = ctx.enter_context(nc.psum_tensor("acc", [P, NT, D], F32))
        misc = ctx.enter_context(nc.psum_tensor("misc", [P, 4, 512], F32))
        ident = konst[:, K_ID:K_ID + P]
        tri = konst[:, K_TRI:K_TRI + P]

        params_in = sem("params_in")
        x_in = sem("x_in")
        loaded = [sem(f"loaded{s}") for s in range(SLOTS)]
        loaded_d = [sem(f"loaded_d{s}") for s in range(SLOTS)]
        freed_d = [sem(f"freed_d{s}") for s in range(SLOTS)]
        freed = [sem(f"freed{s}") for s in range(SLOTS)]
        filled = sem("filled")
        drained = [sem(f"drained{b}") for b in range(4)]
        acc_free = sem("acc_free")
        ones_set = sem("ones_set")
        var_ready = sem("var_ready")
        std_ready = sem("std_ready")
        xsc_ready = sem("xsc_ready")
        std_ready2 = sem("std_ready2")
        gate_ready = sem("gate_ready")
        conv_done = sem("conv_done")
        xc_ready = sem("xc_ready")
        z_ready = sem("z_ready")
        dn_ready = sem("dn_ready")
        dl_ready = sem("dl_ready")
        adt_ready = sem("adt_ready")
        nac_ready = sem("nac_ready")
        decay_ready = sem("decay_ready")
        sq_ready = sem("sq_ready")
        qk_ready = sem("qk_ready")
        seg_ready = sem("seg_ready")
        seg_exp = sem("seg_exp")
        mix_ready = sem("mix_ready")
        y_done = sem("y_done")
        xdt_ready = sem("xdt_ready")
        ysd_ready = sem("ysd_ready")
        smax_ready = sem("smax_ready")
        p_exp = sem("p_exp")
        p_ready = sem("p_ready")
        av_done = sem("av_done")
        yatt_ready = sem("yatt_ready")
        out_done = sem("out_done")
        masks_in = sem("masks_in")
        cact_ready = sem("cact_ready")
        ada_in = [sem("ada_in0"), sem("ada_in1")]
        ada_used = sem("ada_used")
        pool_step = sem("pool_step")
        ada_ready = sem("ada_ready")
        gl_ready = sem("gl_ready")
        gl_log = sem("gl_log")
        lev_ready = sem("lev_ready")
        lev_exp = sem("lev_exp")
        lev_qk_ready = sem("lev_qk_ready")
        o_sq = sem("o_sq")
        z_out = sem("z_out")
        pc_in = sem("pc_in")
        var2 = sem("var2")
        std2 = sem("std2")
        zn_ready = sem("zn_ready")
        zs_ready = sem("zs_ready")
        og_ready = sem("og_ready")
        merged_ready = sem("merged_ready")
        diag_ready = sem("diag_ready")
        rt_in = sem("rt_in")
        rt_exp = sem("rt_exp")
        y_final = sem("y_final")
        mask_ready = sem("mask_ready")
        flag_ready = sem("flag_ready")
        sel_ready = sem("sel_ready")
        selw_ready = sem("selw_ready")
        zero_ready = sem("zero_ready")
        loaded_more = [sem(f"loaded_more{s}") for s in range(SLOTS)]
        freed_more = [sem(f"freed_more{s}") for s in range(SLOTS)]
        loaded_more_d = [sem(f"loaded_more_d{s}") for s in range(SLOTS)]
        freed_more_d = [sem(f"freed_more_d{s}") for s in range(SLOTS)]
        high_in = [sem(f"high_in{s}") for s in range(SLOTS)]
        low_in = [sem(f"low_in{s}") for s in range(SLOTS)]
        high_in_d = [sem(f"high_in_d{s}") for s in range(SLOTS)]
        low_in_d = [sem(f"low_in_d{s}") for s in range(SLOTS)]
        hid_high = sem("hid_high")
        hid_low = sem("hid_low")
        xh_ready = sem("xh_ready")
        more_free = sem("more_free")
        y_ready = sem("y_ready")
        scattered = sem("scattered")
        dve_step = sem("dve_step")
        act_step = sem("act_step")

        def fill_count(m):
            return m + 1 - sum(min(max(m + 1 - FILL[k], 0), uses) for k, uses in fills
                               if (k[0] if isinstance(k, tuple) else k) in BLOCKS)

        def wait_filled(eng, m):
            eng.wait_ge(filled, fill_count(m))

        def wait_slot_read(eng, n0, i=0, j=0):
            n = n0 + j
            eng.wait_ge(freed[n % SLOTS], i + (n // SLOTS + 1))

        def wait_drained(eng, m0, i=0, j=0):
            m = m0 + j
            eng.wait_ge(drained[m % 4], i + (m // 4 + 1))

        def bank_of(m):
            return misc[:, m % 4, :]

        def wait_summed(eng, n0, i, j):
            n = n0 + j
            eng.wait_ge(freed_d[n % SLOTS], i + (n // SLOTS + 1))

        def block_part(n):
            return ring[:, n % SLOTS, :].rearrange("p (k f) -> p k f", k=KD)

        SPLIT = [(RING[k], uses) for k, uses in slots if k[0] == "ffn"]

        def split_count(n):
            return sum(1 for n0, uses in SPLIT for u in range(n0, n0 + uses) if u <= n and u % SLOTS == n % SLOTS)

        def wait_split(eng, sems, n0, i=0, j=0):
            eng.wait_ge(sems[(n0 + j) % SLOTS], i + split_count(n0 + j))

        def wait_split_d(eng, sems, n0, i=0, j=0):
            eng.wait_ge(sems[(n0 + j) % SLOTS], i + ((n0 + j) // SLOTS + 1))

        def low_part(n):
            return ring_low[:, n % SLOTS, :].rearrange("p (k f) -> p k f", k=KD)

        def high_part(n):
            return high_b[:, n % SLOTS, :].rearrange("p (k f) -> p k f", k=KD)

        def pw_part(n):
            return ring[:, n % SLOTS, :].rearrange("p (k f) -> p k f", k=NC2)

        def pair_part(half, x):
            return (block_part(RING["moe"] + x) if half == 0
                    else more[x].rearrange("p (k f) -> p k f", k=KD))

        def pair_rows(half, c):
            return ring_d[:, (ROWD["moe"] + c) % SLOTS, :] if half == 0 else more_d[c]

        def pair_freed(half, x):
            return freed[(RING["moe"] + x) % SLOTS] if half == 0 else freed_more[x]

        def pair_freed_d(half, c):
            return freed_d[(ROWD["moe"] + c) % SLOTS] if half == 0 else freed_more_d[c]

        def wait_pair(eng, half, i, x):
            n = RING["moe"] + x
            if half == 0:
                eng.wait_ge(loaded[n % SLOTS], i * LOAD + LOAD * (n // SLOTS + 1))
            else:
                eng.wait_ge(loaded_more[x], i * LOAD + LOAD)

        def wait_pair_d(eng, half, i, c):
            n = ROWD["moe"] + c
            if half == 0:
                eng.wait_ge(loaded_d[n % SLOTS], i * LOAD + LOAD * (n // SLOTS + 1))
            else:
                eng.wait_ge(loaded_more_d[c], i * LOAD + LOAD)

        def wait_pair_summed(eng, half, i, c):
            if half == 0:
                wait_summed(eng, ROWD["moe"], i, c)
            else:
                eng.wait_ge(freed_more_d[c], i + 1)

        def rows_part(n):
            return ring[:, n % SLOTS, :].rearrange("p (a f) -> p a f", a=2)

        block = ctx.enter_context(nc.Block())

        @block.sync
        def _(sp):
            def claim(n0, i, j):
                n = n0 + j
                if n >= SLOTS or not isinstance(i, int):
                    sp.wait_ge(freed[n % SLOTS], i + n // SLOTS)

            def claim_d(n0, i, j):
                n = n0 + j
                if n >= SLOTS or not isinstance(i, int):
                    sp.wait_ge(freed_d[n % SLOTS], i + n // SLOTS)

            def load_pair(n0, i, q, gate, up, col):
                for g, w in enumerate((gate, up)):
                    load_block(n0, i, 2 * q + g, w, col)

            def load_down(n0, i, j, down, row):
                claim_d(n0, i, j)
                s = (n0 + j) % SLOTS
                sp.dma_start(ring_d[:, s, :], down[bass.ds(row, P), :]).then_inc(loaded_d[s], LOAD)

            def load_block(n0, i, j, w, col):
                claim(n0, i, j)
                n = n0 + j
                sp.dma_start(block_part(n), w[:, bass.ds(col, BLK)].rearrange("(k p) f -> p k f", p=P))\
                    .then_inc(loaded[n % SLOTS], LOAD)

            def load_rows(n0, i, j, w, r):
                claim(n0, i, j)
                n = n0 + j
                sp.dma_start(rows_part(n), w[bass.ds(r * 2 * P, 2 * P), :].rearrange("(a p) f -> p a f", p=P))\
                    .then_inc(loaded[n % SLOTS], LOAD)

            def ffn(f):
                l, which = divmod(f, 2)
                w = [d[f"ffn{which + 1}_w_{s}"][l] for s in ("gate", "up", "down")]
                n0, d0 = RING["ffn", f], ROWD["ffn", f]

                def four(n, dn, i, c):
                    for q in range(2):
                        load_pair(n, i, q, w[0], w[1], c * P + q * BLK)
                        for j in range(2 * q, 2 * q + 2):
                            load_down(dn, i, j, w[2], c * P + j * P)

                if not f:
                    four(n0, d0, 0, 0)
                with sp.Fori(0 if f else 1, NF // 4) as i:
                    four(n0, d0, i, i * 4)
                c = NF // 4 * 4
                load_pair(n0 + c, 0, 0, w[0], w[1], c * P)
                for j in range(2):
                    load_down(d0 + c, 0, j, w[2], (c + j) * P)

            for l in range(DEPTH):
                ffn(2 * l)
                n0 = RING["win", l]
                w_in = d["w_in"][l]
                with sp.Fori(0, 2) as i:
                    for j in range(4):
                        load_block(n0, i, j, w_in, (i * 4 + j) * BLK + D)
                for j in range(4):
                    load_block(n0 + 8 + j, 0, 0, w_in, j * BLK)
                with sp.Fori(0, 3) as i:
                    for j in range(4):
                        load_block(n0 + 12, i, j, w_in, (i * 4 + j) * BLK + (D + XBC + HEADS))
                n0 = RING["wout", l]
                with sp.Fori(0, 2) as i:
                    for j in range(4):
                        load_rows(n0, i, j, d["w_out"][l], i * 4 + j)
                ffn(2 * l + 1)
            w_in = d["w_in_2"][0]
            n0 = RING["win2"]
            for j in range(4):
                load_block(n0 + j, 0, 0, w_in, QK0 + j * BLK)
            for j in range(4):
                load_block(n0 + 4 + j, 0, 0, w_in, V0 + j * BLK)
            for j in range(4):
                load_block(n0 + 8 + j, 0, 0, w_in, j * BLK)
            for j in range(4):
                load_block(n0 + 12 + j, 0, 0, w_in, R0 + j * BLK)
            with sp.Fori(0, 2) as i:
                for j in range(4):
                    load_block(n0 + 16, i, j, w_in, (i * 4 + j) * BLK + G0)
            n0 = RING["pw"]
            for j in range(2):
                claim(n0 + j, 0, 0)
                sp.dma_start(pw_part(n0 + j), d["w_conv_pw_2"][0][:, j * 512:(j + 1) * 512]
                             .rearrange("(k p) f -> p k f", p=P)).then_inc(loaded[(n0 + j) % SLOTS], LOAD)
            for j in range(4):
                load_block(RING["glao"] + j, 0, 0, d["w_gla_o_2"][0], j * BLK)
            for j in range(4):
                load_rows(RING["wout2"] + j, 0, 0, d["w_out_2"][0], j)
            w1, w3 = (d[k][0].rearrange("e m f -> (e m) f") for k in ("w1_2", "w3_2"))
            w2 = d["w2_2"][0].rearrange("e f m -> (e f) m")

            def load_expert(i, half, first=False):
                e = i * 2 + half
                for x in range(4):
                    w = w1 if x % 2 == 0 else w3
                    if half == 0:
                        load_block(RING["moe"], i, x, w[bass.ds(e * D, D), :], x // 2 * BLK)
                    else:
                        if not first:
                            sp.wait_ge(freed_more[x], i)
                        sp.dma_start(pair_part(1, x), w[bass.ds(e * D, D), x // 2 * BLK:(x // 2 + 1) * BLK]
                                     .rearrange("(k p) f -> p k f", p=P)).then_inc(loaded_more[x], LOAD)
                for c in range(CPE):
                    if half == 0:
                        load_down(ROWD["moe"], i, c, w2, e * D_EXPERT + c * P)
                    else:
                        if not first:
                            sp.wait_ge(freed_more_d[c], i)
                        sp.dma_start(more_d[c], w2[bass.ds(e * D_EXPERT + c * P, P), :])\
                            .then_inc(loaded_more_d[c], LOAD)

            load_expert(0, 0)
            sp.wait_ge(more_free, 1)
            load_expert(0, 1, first=True)
            with sp.Fori(1, EXPERTS // 2) as i:
                load_expert(i, 0)
                load_expert(i, 1)
            sp.wait_ge(out_done, 16)

        @block.tensor
        def _(pe):
            def three(dst, wh, wl, mh, ml, start, stop, **kw):
                pe.matmul(dst, wh, ml, start=start, stop=False, **kw)
                pe.matmul(dst, wl, mh, start=False, stop=False, **kw)
                return pe.matmul(dst, wh, mh, start=False, stop=stop, **kw)

            def claim_bank(m0, i=0, j=0):
                m = m0 + j
                if m >= 4 or not isinstance(i, int):
                    pe.wait_ge(drained[m % 4], i + m // 4)
                return bank_of(m)

            def wait_slot(n0, i=0, j=0):
                n = n0 + j
                pe.wait_ge(loaded[n % SLOTS], i * LOAD + LOAD * (n // SLOTS + 1))

            def turn(m0, src, groups):
                for q in groups:
                    b = claim_bank(m0 + q)
                    for kk in range(2):
                        for t in range(NT):
                            k = 2 * q + kk
                            mm = pe.transpose(b[:, kk * SEQ + t * P:kk * SEQ + (t + 1) * P],
                                              src[:, t, k * P:(k + 1) * P], ident)
                    mm.then_inc(filled, 1)

            def norm(u):
                pe.wait_ge(xsc_ready, u + 1)
                turn(FILL["norm", u], xsc, range(4))
                for q in range(4):
                    wait_drained(pe, FILL["norm", u] + q)

            def gate_up(m0, n0, i, c):
                b = claim_bank(m0, i, c)
                for g in range(2):
                    n = n0 + c // 2 * 2 + g
                    if c % 2 == 0:
                        wait_split(pe, low_in, n, i)
                    cs = slice(c % 2 * P, (c % 2 + 1) * P)
                    for k in range(KD):
                        mm = three(b[:, g * SEQ:(g + 1) * SEQ], high_part(n)[:, k, cs], low_part(n)[:, k, cs],
                                   xh[:, k, :], xl[:, k, :], k == 0, k == KD - 1)
                mm.then_inc(filled, 1)

            def down(m0, n0, d0, g0, i, c, start, stop):
                pe.wait_ge(hid_low, i * 4 + (g0 + c + 1))
                dn = d0 + c
                wait_split_d(pe, low_in_d, d0, i, c)
                q = (m0 + c) % 2
                for t in range(NT):
                    ts = slice(t * P, (t + 1) * P)
                    for cc in range(2):
                        cs = slice(cc * 512, (cc + 1) * 512)
                        mm = three(acc[:, t, cs], hidh[:, q, ts], hidl[:, q, ts], high_r[:, dn % SLOTS, cs],
                                   ring_d_low[:, dn % SLOTS, cs], start, stop, skip_group_check=True)
                        if c % 2 == 0 and t == 0:
                            mm.then_inc(freed[(n0 + c + cc) % SLOTS], 1)
                mm.then_inc(freed_d[dn % SLOTS], 1)

            def ffn(f, a):
                m0, n0, d0 = FILL["ffn", f], RING["ffn", f], ROWD["ffn", f]
                gate_up(m0, n0, 0, 0)
                if a:
                    pe.wait_ge(acc_free, a)
                gate_up(m0, n0, 0, 1)
                down(m0, n0, d0, NF * f, 0, 0, True, False)
                with pe.Fori(0, (NF - 2) // 4) as i:
                    for j in range(4):
                        gate_up(m0, n0, i, j + 2)
                        down(m0, n0, d0, NF * f, i, j + 1, False, False)
                down(m0, n0, d0, NF * f, 0, NF - 1, False, True)

            def cols_out(m0, n0, i, j, src=xnT):
                wait_slot(n0, i, j)
                b = claim_bank(m0, i, j)
                w = block_part(n0 + j)
                for c in range(2):
                    for k in range(KD):
                        mm = pe.matmul(b[:, c * SEQ:(c + 1) * SEQ], w[:, k, c * P:(c + 1) * P], src[:, k, :],
                                       start=(k == 0), stop=(k == KD - 1))
                mm.then_inc(freed[(n0 + j) % SLOTS], 1)

            def toks_out(m0, n0, i, j):
                wait_slot(n0, i, j)
                b = claim_bank(m0, i, j)
                w = block_part(n0 + j)
                for t in range(NT):
                    for k in range(KD):
                        mm = pe.matmul(b[:, t * BLK:(t + 1) * BLK], xnT[:, k, t * P:(t + 1) * P], w[:, k, :],
                                       start=(k == 0), stop=(k == KD - 1))
                mm.then_inc(freed[(n0 + j) % SLOTS], 1)

            def w_in(l):
                n0 = RING["win", l]
                with pe.Fori(0, 2) as i:
                    for j in range(4):
                        cols_out(FILL["xbc", l], n0, i, j)
                b = claim_bank(FILL["dt", l])
                for t in range(NT):
                    for k in range(KD):
                        mm = pe.matmul(b[:, t * HEADS:(t + 1) * HEADS], xnT[:, k, t * P:(t + 1) * P],
                                       wdt[:, l, k, :], start=(k == 0), stop=(k == KD - 1))
                mm.then_inc(filled, 1)
                for j in range(4):
                    toks_out(FILL["z", l] + j, n0 + 8 + j, 0, 0)
                with pe.Fori(0, 3) as i:
                    for j in range(4):
                        toks_out(FILL["qkv", l], n0 + 12, i, j)

            def ssd(l, a):
                pe.wait_ge(adt_ready, l + 1)
                b = claim_bank(FILL["acum", l])
                pe.matmul(b[:, 0:32], tri, adt, start=True, stop=True)
                pe.matmul(b[:, 32:48], ones[:, :], adt[:, 0:HEADS], start=True, stop=True).then_inc(filled, 1)
                pe.wait_ge(xc_ready, 4 * (l + 1))
                for q in range(4):
                    t, half = divmod(q, 2)
                    b = claim_bank(FILL["xt", l] + q)
                    for c in range(4):
                        mm = pe.transpose(b[:, c * P:(c + 1) * P], xc[:, half * 4 + c, t * P:(t + 1) * P], ident)
                    mm.then_inc(filled, 1)
                b = claim_bank(FILL["bt", l])
                for g in range(GROUPS):
                    mm = pe.transpose(b[:, g * P:(g + 1) * P], xc[:, 8 + g, 0:P], ident)
                mm.then_inc(filled, 1)
                pe.wait_ge(qk_ready, l + 1)
                turn(FILL["qkt", l], qk[:, :, 0:D], range(4))
                turn(FILL["qkt", l] + 4, qk[:, :, D:2 * D], range(4))
                for c in range(NT):
                    b = claim_bank(FILL["cb", l] + c)
                    for g in range(GROUPS):
                        mm = pe.matmul(b[:, g * P:(g + 1) * P], xc[:, 8 + g, c * P:(c + 1) * P],
                                       xc[:, 12 + g, c * P:(c + 1) * P], start=True, stop=True)
                    mm.then_inc(filled, 1)
                pe.wait_ge(xdt_ready, l + 1)
                pe.wait_ge(acc_free, a)

                def y_diag(s):
                    pe.wait_ge(mix_ready, 8 * l + s + 1)
                    c, g = divmod(s, GROUPS)
                    for r in range(HPG):
                        h = g * HPG + r
                        mm = pe.matmul(acc[:, c, h * HD:(h + 1) * HD], seg[:, s % 2, r * P:(r + 1) * P],
                                       xdt[:, c, h * HD:(h + 1) * HD], start=True, stop=True,
                                       skip_group_check=True)
                    mm.then_inc(y_done, 1)

                for s in range(8):
                    c, g = divmod(s, GROUPS)
                    b = claim_bank(FILL["bc", l] + s)
                    for r in range(HPG):
                        col = c * HEADS + g * HPG + r
                        mm = pe.matmul(b[:, r * P:(r + 1) * P], adt[:, col:col + 1].to_broadcast([P, P]), tri,
                                       start=True, stop=True)
                    mm.then_inc(filled, 1)
                    if s >= 1:
                        y_diag(s - 1)
                y_diag(7)
                for q in range(2):
                    b = claim_bank(FILL["state", l] + q)
                    for gg in range(2):
                        g = 2 * q + gg
                        mm = pe.matmul(b[:, gg * BLK:(gg + 1) * BLK], btok[:, g, :], xdec[:, g * BLK:(g + 1) * BLK],
                                       start=True, stop=True)
                    mm.then_inc(filled, 1)
                for q in range(2):
                    wait_drained(pe, FILL["state", l] + q)
                for q in range(2):
                    b = claim_bank(FILL["off", l] + q)
                    for gg in range(2):
                        g = 2 * q + gg
                        mm = pe.matmul(b[:, gg * BLK:(gg + 1) * BLK], xc[:, 12 + g, P:SEQ], prev[:, g, :],
                                       start=True, stop=True)
                    mm.then_inc(filled, 1)

            def attention(l, a):
                m0 = FILL["att", l]

                def scores(h):
                    rows64 = slice(h % 2 * HD, h % 2 * HD + HD)
                    b = claim_bank(m0 + AF["S", h])
                    pe.matmul(b[:, 0:P], qT[rows64, h // 2, 0:P], kT[rows64, h // 2, 0:P], start=True, stop=True)
                    pe.matmul(b[:, P:3 * P], qT[rows64, h // 2, P:SEQ], kT[rows64, h // 2, :],
                              start=True, stop=True).then_inc(filled, 1)

                def turn_weights(h):
                    pe.wait_ge(p_ready, HEADS * l + h + 1)
                    b = claim_bank(m0 + AF["T", h])
                    for c in range(3):
                        mm = pe.transpose(b[:, c * P:(c + 1) * P], sp3[:, h % 3, c * P:(c + 1) * P], ident)
                    mm.then_inc(filled, 1)

                def values(h):
                    wait_drained(pe, m0 + AF["T", h])
                    if h == 0:
                        pe.wait_ge(acc_free, a)
                    for t, c, key in ((0, 0, 0), (1, 1, 0), (1, 2, 1)):
                        mm = pe.matmul(acc[:, t, h * HD:(h + 1) * HD], pT[:, h % 2, c * P:(c + 1) * P],
                                       v[:, key, h * HD:(h + 1) * HD], start=(key == 0), stop=(key == t),
                                       skip_group_check=True)
                    mm.then_inc(av_done, 1)

                for q in range(8):
                    wait_drained(pe, FILL["qkt", l] + q)
                for h in range(HEADS + 3):
                    if h < HEADS:
                        scores(h)
                    if 2 <= h < HEADS + 2:
                        turn_weights(h - 2)
                    if h >= 3:
                        values(h - 3)

            def w_out(l, a):
                pe.wait_ge(ysd_ready, l + 1)
                turn(FILL["yt", l], xtok, range(4))
                pe.wait_ge(yatt_ready, l + 1)
                turn(FILL["yt", l] + 4, yatt, range(4))
                for q in range(8):
                    wait_drained(pe, FILL["yt", l] + q)
                pe.wait_ge(acc_free, a)
                n0 = RING["wout", l]
                for r in range(8):
                    wait_slot(n0 + r)
                    w = rows_part(n0 + r)
                    for kk in range(2):
                        k = 2 * r + kk
                        for t in range(NT):
                            for c in range(2):
                                mm = pe.matmul(acc[:, t, c * 512:(c + 1) * 512], yT[:, k, t * P:(t + 1) * P],
                                               w[:, kk, c * 512:(c + 1) * 512], start=(k == 0), stop=(k == 15),
                                               skip_group_check=True)
                    mm.then_inc(freed[(n0 + r) % SLOTS], 1)

            def modulation(p):
                pe.wait_ge(ada_ready, p + 1)
                b = claim_bank(FILL["mod", p])
                for k in range(KD):
                    mm = pe.matmul(b[:, k:k + 1], ada[:, k * P:(k + 1) * P], ones[:, 0:1], start=True, stop=True)
                mm.then_inc(filled, 1)

            def w_in2():
                n0 = RING["win2"]
                b = claim_bank(FILL["a1"])
                for k in range(KD):
                    mm = pe.matmul(b[0:RANK, 0:SEQ], wa1[:, k, :], xnT[:, k, :], start=(k == 0), stop=(k == KD - 1))
                mm.then_inc(filled, 1)
                for j in range(4):
                    cols_out(FILL["qk2"] + j, n0 + j, 0, 0)
                    if j == 0:
                        wait_drained(pe, FILL["a1"])
                        for q in range(2):
                            b = claim_bank(FILL["a2"] + q)
                            for hh in range(2):
                                h = 2 * q + hh
                                mm = pe.matmul(b[:, hh * SEQ:(hh + 1) * SEQ], wa2[:, h * DK:(h + 1) * DK],
                                               a1T[0:RANK, :], start=True, stop=True)
                            mm.then_inc(filled, 1)
                for j in range(4):
                    toks_out(FILL["v2"] + j, n0 + 4 + j, 0, 0)
                for j in range(4):
                    cols_out(FILL["pc"] + j, n0 + 8 + j, 0, 0)
                for j in range(4):
                    cols_out(FILL["r"] + j, n0 + 12 + j, 0, 0)
                with pe.Fori(0, 2) as i:
                    for j in range(4):
                        cols_out(FILL["gates"], n0 + 16, i, j)

            def gla():
                for s in range(len(LEVELS) + 1):
                    if s < len(LEVELS):
                        pe.wait_ge(lev_qk_ready, s + 1)
                    for t in range(NT):
                        b = claim_bank(FILL["pairs"] + 2 * s + t)
                        for h in range(GH):
                            if s < len(LEVELS):
                                keys = lev_qk[:, s % 2, h * SEQ + t * P:h * SEQ + (t + 1) * P]
                                queries = keys
                            else:
                                keys = q2k2[:, GH + h, t * P:(t + 1) * P]
                                queries = q2k2[:, h, t * P:(t + 1) * P]
                            mm = pe.matmul(b[:, h * P:(h + 1) * P], keys, queries, start=True, stop=True)
                        mm.then_inc(filled, 1)
                pe.wait_ge(lev_qk_ready, len(LEVELS) + 1)
                b = claim_bank(FILL["cross"])
                lq = lev_qk[:, len(LEVELS) % 2, :]
                for h in range(GH):
                    mm = pe.matmul(b[:, h * P:(h + 1) * P], lq[:, h * SEQ:h * SEQ + P],
                                   lq[:, h * SEQ + P:(h + 1) * SEQ], start=True, stop=True)
                mm.then_inc(filled, 1)
                for i in range(2 * len(LEVELS) + 2):
                    if i >= 2 * len(LEVELS) - 2:
                        wait_drained(pe, FILL["pairs"] + i)
                wait_drained(pe, FILL["cross"])
                for h in range(GH):
                    b = claim_bank(FILL["o"] + h)
                    for c in range(2):
                        ch = slice(h * DV + c * P, h * DV + (c + 1) * P)
                        pe.matmul(b[:, c * SEQ:c * SEQ + P], v2[:, 0, ch], attn[:, h, :], start=True, stop=True)
                        pe.matmul(b[:, c * SEQ + P:(c + 1) * SEQ], v2[:, 1, ch], attn[:, GH + h, :],
                                  start=True, stop=False)
                        mm = pe.matmul(b[:, c * SEQ + P:(c + 1) * SEQ], v2[:, 0, ch], across[:, h, :],
                                       start=False, stop=True)
                    mm.then_inc(filled, 1)
                pe.wait_ge(o_sq, 1)
                for q in range(2):
                    b = claim_bank(FILL["osum"] + q)
                    for hh in range(2):
                        for c in range(2):
                            mm = pe.matmul(b[:, hh * SEQ:(hh + 1) * SEQ], ones[:, :], osq[:, 2 * (2 * q + hh) + c, :],
                                           start=(c == 0), stop=(c == 1))
                    mm.then_inc(filled, 1)

            def conv_branch():
                for k, (name, src) in enumerate((("mean", zc), ("var", zsq))):
                    pe.wait_ge(z_out, k + 1)
                    b = claim_bank(FILL[name])
                    for c in range(NC2):
                        mm = pe.matmul(b[:, 0:SEQ], ones[:, :], src[:, c, :], start=(c == 0), stop=(c == NC2 - 1))
                    mm.then_inc(filled, 1)
                pe.wait_ge(zs_ready, 1)
                for j in range(2):
                    n = RING["pw"] + j
                    wait_slot(n)
                    w = pw_part(n)
                    for q in range(2):
                        b = claim_bank(FILL["pwa", 0] + 2 * j + q)
                        for c in range(2):
                            cc = (2 * q + c) * P
                            for k in range(NC2):
                                mm = pe.matmul(b[:, c * SEQ:(c + 1) * SEQ], w[:, k, cc:cc + P], zc[:, k, :],
                                               start=(k == 0), stop=(k == NC2 - 1))
                        mm.then_inc(freed[n % SLOTS] if q else filled, 1)
                pe.wait_ge(og_ready, 1)
                for j in range(4):
                    cols_out(FILL["ygla"] + j, RING["glao"] + j, 0, 0, src=oT)

            def row_fill(m0, which):
                pe.wait_ge(diag_ready, which)
                for q in range(2):
                    b = claim_bank(m0 + q)
                    mm = pe.matmul(b, ones[:, :], diag[:, q * 512:(q + 1) * 512], start=True, stop=True)
                    mm.then_inc(filled, 1)

            def w_out2():
                pe.wait_ge(merged_ready, 1)
                pe.wait_ge(acc_free, A1)
                for r in range(4):
                    n = RING["wout2"] + r
                    wait_slot(n)
                    w = rows_part(n)
                    for kk in range(2):
                        k = 2 * r + kk
                        for t in range(NT):
                            for c in range(2):
                                mm = pe.matmul(acc[:, t, c * 512:(c + 1) * 512], merged[:, k, t * P:(t + 1) * P],
                                               w[:, kk, c * 512:(c + 1) * 512], start=(k == 0), stop=(k == KD - 1),
                                               skip_group_check=True)
                    mm.then_inc(freed[n % SLOTS], 1)
                row_fill(FILL["garow"], 1)

            def router():
                b = claim_bank(FILL["router"])
                for t in range(NT):
                    for k in range(KD):
                        mm = pe.matmul(b[:, t * 36:(t + 1) * 36], xnT[:, k, t * P:(t + 1) * P], wr[:, k, :],
                                       start=(k == 0), stop=(k == KD - 1))
                mm.then_inc(filled, 1)

            def count():
                pe.wait_ge(mask_ready, 1)
                b = claim_bank(FILL["count"])
                pe.matmul(b[:, 0:EXPERTS], tri, mark1[:, 0, :], start=True, stop=True)
                pe.matmul(b[:, EXPERTS:2 * EXPERTS], tri, mark1[:, 1, :], start=True, stop=False)
                pe.matmul(b[:, EXPERTS:2 * EXPERTS], ones[:, :], mark1[:, 0, :], start=False, stop=True)
                pe.matmul(b[:, 2 * EXPERTS:3 * EXPERTS], ones[:, :], mark1[:, 0, :], start=True, stop=False)
                pe.matmul(b[:, 2 * EXPERTS:3 * EXPERTS], ones[:, :], mark1[:, 1, :], start=False, stop=True)\
                    .then_inc(filled, 1)

            def gathered_experts():
                m0 = FILL["moe"] + 1

                def claim3(i, j):
                    m = m0 + j
                    pe.wait_ge(drained[m % 4], i * 3 + m // 4)
                    return bank_of(m)

                def drained3(i, j):
                    m = m0 + j
                    pe.wait_ge(drained[m % 4], i * 3 + (m // 4 + 1))

                def gather(b, half, frees=()):
                    for k in range(KD):
                        for t in range(NT):
                            mm = pe.matmul(b[:, k * CAP:(k + 1) * CAP], u2[:, t, k * P:(k + 1) * P],
                                           sel[:, half, t, :], start=(t == 0), stop=(t == NT - 1))
                            if 2 * k + t < len(frees):
                                mm.then_inc(frees[2 * k + t], 1)
                    mm.then_inc(filled, 1)

                def gate_up_e(i, half, j, frees=()):
                    for q in range(2):
                        b = claim3(i, j + q)
                        for g in range(2):
                            wait_pair(pe, half, i, 2 * q + g)
                            w = pair_part(half, 2 * q + g)
                            for c in range(2):
                                for k in range(KD):
                                    mm = pe.matmul(b[:, (2 * g + c) * CAP:(2 * g + c + 1) * CAP],
                                                   w[:, k, c * P:(c + 1) * P], ueT[:, half, k, :],
                                                   start=(k == 0), stop=(k == KD - 1))
                                    at_ = (g * 2 + c) * KD + k
                                    if at_ < len(frees):
                                        mm.then_inc(frees[at_], 1)
                        mm.then_inc(filled, 1)
                        frees = [pair_freed(half, g) for g in range(2)]

                def down_e(i, half, j, frees):
                    banks = [claim3(i, j + c) for c in range(2)]
                    for c in range(CPE):
                        wait_pair_d(pe, half, i, c)
                        for cc in range(2):
                            mm = pe.matmul(banks[cc], hid_e[:, c, :], pair_rows(half, c)[:, cc * 512:(cc + 1) * 512],
                                           start=(c == 0), stop=(c == CPE - 1))
                            if c == CPE - 1:
                                mm.then_inc(filled, 1)
                            elif cc == 1:
                                mm.then_inc(pair_freed_d(half, c), 1)
                            elif c < len(frees):
                                mm.then_inc(frees[c], 1)

                def scatter(start):
                    for t in range(NT):
                        for c in range(2):
                            mm = pe.matmul(acc[:, t, c * 512:(c + 1) * 512], selT[:, t * P:(t + 1) * P],
                                           out_e[:, c * 512:(c + 1) * 512], start=start, stop=True,
                                           skip_group_check=True)
                    return mm

                pe.wait_ge(acc_free, A1 + 1)
                pe.wait_ge(zero_ready, 1)
                scatter(True)
                pe.wait_ge(sel_ready, 1)
                gather(claim_bank(FILL["moe"]), 0)
                with pe.Fori(0, EXPERTS // 2) as i:
                    i2 = i * 2
                    drained3(i, -1)
                    gate_up_e(i, 0, 0)
                    pe.wait_ge(sel_ready, i2 + 2)
                    gather(claim3(i, 2), 1, [pair_freed(0, 2 + g) for g in range(2)])
                    pe.wait_ge(selw_ready, i + 1)
                    for t in range(NT):
                        pe.transpose(claim3(i, 3 + t)[:, 0:P], selw[:, t, :], ident).then_inc(filled, 1)
                    for q in range(2):
                        drained3(i, q)
                    down_e(i, 0, 5, [])
                    drained3(i, 2)
                    gate_up_e(i, 1, 7, [pair_freed_d(0, CPE - 1)])
                    for q in range(2):
                        drained3(i, 7 + q)
                    down_e(i, 1, 9, [pair_freed(1, 2 + g) for g in range(2)])
                    pe.wait_ge(sel_ready, i2 + 3)
                    gather(claim3(i, 11), 0, [pair_freed_d(1, CPE - 1)])
                    for j in (9, 10):
                        drained3(i, j)
                    scatter(False).then_inc(scattered, 1)

            def experts():
                m0 = FILL["moe"]

                def gate_up8(i, c):
                    b = claim8(i, c)
                    half, turn_ = c // CPE % 2, i + c // 8
                    for g in range(2):
                        x = c % CPE // 2 * 2 + g
                        if c % 2 == 0:
                            wait_pair(pe, half, turn_, x)
                        w = pair_part(half, x)
                        for k in range(KD):
                            mm = pe.matmul(b[:, g * SEQ:(g + 1) * SEQ], w[:, k, c % 2 * P:(c % 2 + 1) * P],
                                           xnT[:, k, :], start=(k == 0), stop=(k == KD - 1))
                    mm.then_inc(filled, 1)

                def claim8(i, c):
                    m = m0 + c
                    pe.wait_ge(drained[m % 4], i * 2 + m // 4)
                    return bank_of(m)

                def down8(i, c):
                    m = m0 + c
                    pe.wait_ge(drained[m % 4], i * 2 + (m // 4 + 1))
                    half, cc = divmod(c, CPE)
                    wait_pair_d(pe, half, i, cc)
                    w = pair_rows(half, cc)
                    h = hid[:, m % 2, :]
                    for t in range(NT):
                        for q in range(2):
                            mm = pe.matmul(acc[:, t, q * 512:(q + 1) * 512], h[:, t * P:(t + 1) * P],
                                           w[:, q * 512:(q + 1) * 512], start=(cc == 0), stop=(cc == CPE - 1),
                                           skip_group_check=True)
                            if cc % 2 == 0 and t == 0:
                                mm.then_inc(pair_freed(half, cc + q), 1)
                    mm.then_inc(pair_freed_d(half, cc), 1)

                def two_experts(i, last):
                    for c in range(2 * CPE):
                        if not (last and c == 2 * CPE - 1):
                            gate_up8(i, c + 1)
                        if c % CPE == 0:
                            pe.wait_ge(acc_free, i * 2 + (A1 + 1 + c // CPE))
                        down8(i, c)

                gate_up8(0, 0)
                with pe.Fori(0, EXPERTS // 2 - 1) as i:
                    two_experts(i, False)
                two_experts(EXPERTS // 2 - 1, True)

            pe.wait_ge(params_in, N_PARAMS * 16)
            for i, n in enumerate((N_COLA, N_COLA, P, N_COLC)):
                pe.transpose(bank_of(i)[:, 0:n], rows[0:n, i, :], ident[0:n, 0:n]).then_inc(filled, 1)
            pe.wait_ge(ones_set, 1)
            for l in range(DEPTH):
                norm(3 * l)
                ffn(2 * l, 5 * l)
                modulation(4 * l)
                norm(3 * l + 1)
                w_in(l)
                modulation(4 * l + 1)
                ssd(l, 5 * l + 1)
                attention(l, 5 * l + 2)
                w_out(l, 5 * l + 3)
                modulation(4 * l + 2)
                norm(3 * l + 2)
                ffn(2 * l + 1, 5 * l + 4)
                modulation(4 * l + 3)
            norm(U1)
            w_in2()
            gla()
            conv_branch()
            w_out2()
            norm(U1 + 1)
            router()
            for i in range(5):
                row_fill(FILL["rows"] + 2 * i, i + 2)
            count()
            pe.wait_ge(flag_ready, 1)
            few = pe.value_load(flag[0:1, 0:1], min_val=0, max_val=1)
            with pe.If(few > 0):
                gathered_experts()
            with pe.Else():
                experts()

        @block.gpsimd
        def _(pool):
            def load(p, k):
                w, col = (d["w_ada_2"][0], p * D) if p < 6 else (d["w_ada_f_2"], (p - 6) * D)
                pool.dma_start(w_ada[:, k % 2, :], w[k * P:(k + 1) * P, col:col + D]).then_inc(ada_in[k % 2], 16)

            pool.wait_ge(cact_ready, 1)
            load(0, 0)
            load(0, 1)
            for p in range(PIECES):
                for k in range(KD):
                    u = p * KD + k
                    pool.wait_ge(ada_in[k % 2], 16 * (u // 2 + 1))
                    row = w_ada[:, k % 2, :]
                    if k == 0:
                        if p:
                            pool.wait_ge(filled, fill_count(FILL["mod", p - 1]))
                        pool.tensor_scalar(ada, row, cact[:, 0:1], None, ALU.mult).then_inc(ada_used, 1)
                        pool.wait_ge(ada_used, u + 1)
                    else:
                        pool.tensor_scalar(row, row, cact[:, k:k + 1], None, ALU.mult).then_inc(pool_step, 1)
                        pool.wait_ge(pool_step, p * (KD - 1) + k)
                        pool.tensor_tensor(ada, ada, row, ALU.add).then_inc(ada_used, 1)
                        pool.wait_ge(ada_used, u + 1)
                    if u + 2 < PIECES * KD:
                        load((u + 2) // KD, (u + 2) % KD)
                pool.nop().then_inc(ada_ready, 1)

        @block.scalar
        def _(act):
            n = [0]

            def step(ins):
                n[0] += 1
                ins.then_inc(act_step, 1)
                return n[0]

            def line(src):
                return src.rearrange("(k p) -> k p", p=P)

            act.dma_start(x[:, :, :], d["x"][0].rearrange("(t p) e -> p t e", p=P)).then_inc(x_in, 16)
            act.dma_start(konst[:, :], d["consts"]).then_inc(params_in, 16)
            for i, name in enumerate(("dt_bias", "a_log", "d_skip")):
                act.dma_start(heads3[:, i, :, :], d[name].partition_broadcast(P)).then_inc(params_in, 16)
            act.dma_start(wdt[:, :, :, :].rearrange("p l k h -> p (l k) h"),
                          d["w_in"][:, :, D + XBC:D + XBC + HEADS].rearrange("l (k p) h -> p (l k) h", p=P)).then_inc(params_in, 16)
            for l in range(DEPTH):
                for col, src in ((C_FFN1, line(d["ffn1_norm"][l])), (C_MIX, line(d["mix_norm"][l])),
                                 (C_FFN2, line(d["ffn2_norm"][l])),
                                 (C_CW, d["conv_w"][l].rearrange("k (c p) -> (k c) p", p=P)),
                                 (C_CB, line(d["conv_b"][l])), (C_SSD, line(d["ssd_norm"][l]))):
                    k = src.shape[0]
                    act.dma_start(rows[col:col + k, l, :], src).then_inc(params_in, 16)
                for col, name in ((C_QN, "q_norm"), (C_KN, "k_norm")):
                    src = d[name][l:l + 1, :].unsqueeze(1).to_broadcast([1, 2, HD])
                    act.dma_start(rows[col:col + 1, l, :].rearrange("a (b c) -> a b c", b=2), src).then_inc(params_in, 16)
            for col, src in ((B_ADA, d["b_ada_2"][0]), (B_ADA + 48, d["b_ada_f_2"]), (B_C, d["c_2"][0]),
                             (B_N1, d["g_norm1_2"][0]), (B_N2, d["g_norm2_2"][0]), (B_NF, d["g_final_2"]),
                             (B_PW, d["b_conv_pw_2"][0]), (B_GLA, d["g_gla_norm_2"][0]), (B_DW, d["b_dw_2"][0]),
                             (B_LG, d["g_conv_ln_2"][0]), (B_LB, d["b_conv_ln_2"][0]), (B_A2, d["b_a2_2"][0])):
                src = line(src)
                act.dma_start(rows[col:col + src.shape[0], 2, :], src).then_inc(params_in, 16)
            act.dma_start(rows[0:N_COLC, 3, :], d["w_dw_2"][0, :, 0, :].rearrange("k (c p) -> (k c) p", p=P))\
                .then_inc(params_in, 16)
            act.dma_start(wa1[:, :, :], d["w_in_2"][0, :, A0:A0 + RANK].rearrange("(k p) r -> p k r", p=P))\
                .then_inc(params_in, 16)
            act.dma_start(wa2[:, :], d["w_a2_2"][0]).then_inc(params_in, 16)
            for a, b, name in ((0, N_GROUPS, "g"), (N_GROUPS, N_GROUPS + EXPERTS, "e")):
                act.dma_start(wr[:, :, a:b], d[f"w_router_{name}_2"][0].rearrange("(k p) r -> p k r", p=P))\
                    .then_inc(params_in, 16)
                act.dma_start(br[:, a:b], d[f"b_router_{name}_2"][0].partition_broadcast(P)).then_inc(params_in, 16)
            wait_drained(act, 2)
            act.activation(cact[:, :], colb[:, B_C:B_C + KD], ACT.Silu).then_inc(cact_ready, 1)

            def norm(u, gain, dst=xnT, shift=None):
                act.wait_ge(var_ready, u + 1)
                act.activation(std, ss, ACT.Sqrt).then_inc(std_ready, 1)
                if gain:
                    turned(FILL["norm", u], (0, 2), dst, 0, gain, shift)

            def norm_high(u, gain):
                act.wait_ge(var_ready, u + 1)
                act.activation(std, ss, ACT.Sqrt).then_inc(std_ready, 1)
                for q in range(4):
                    wait_filled(act, FILL["norm", u] + q)
                    b = bank_of(FILL["norm", u] + q)
                    for kk in range(2):
                        k = 2 * q + kk
                        ins = act.mul(xh[:, k, :], b[:, kk * SEQ:(kk + 1) * SEQ], gain(k))
                    ins.then_inc(xh_ready, 1)

            def high_block(n0, i, j):
                s = (n0 + j) % SLOTS
                act.wait_ge(loaded[s], i * LOAD + LOAD * ((n0 + j) // SLOTS + 1))
                act.activation(high_b[:, s, :], ring[:, s, :], ACT.Copy).then_inc(high_in[s], 1)

            def high_rows(d0, i, c):
                s = (d0 + c) % SLOTS
                act.wait_ge(loaded_d[s], i * LOAD + LOAD * ((d0 + c) // SLOTS + 1))
                act.activation(high_r[:, s, :], ring_d[:, s, :], ACT.Copy).then_inc(high_in_d[s], 1)

            def turned(m0, groups, dst, first, gain, shift=None):
                for q in groups:
                    wait_filled(act, m0 + q)
                    b = bank_of(m0 + q)
                    for kk in range(2):
                        k = 2 * q + kk
                        src = b[:, kk * SEQ:(kk + 1) * SEQ]
                        if shift:
                            ins = act.activation(dst[:, first + k, :], src, ACT.Identity, scale=gain(k), bias=shift(k))
                        else:
                            ins = act.mul(dst[:, first + k, :], src, gain(k))
                    ins.then_inc(drained[(m0 + q) % 4], 1)

            def gate(m0, i, j):
                act.wait_ge(filled, i * 4 + fill_count(m0 + j))
                act.activation(gate_s[:, (m0 + j) % 2, :], bank_of(m0 + j)[:, 0:SEQ], ACT.Silu).then_inc(gate_ready, 1)

            def ffn(f):
                m0, n0, d0 = FILL["ffn", f], RING["ffn", f], ROWD["ffn", f]

                def four(i, a, last):
                    for j in range(a, a + 4):
                        wait_drained(act, m0, i, j - 2)
                        gate(m0, i, j)
                        high_rows(d0, i, j)
                        if j % 2 == 0 and not (last and j == a + 2):
                            for g in range(2):
                                high_block(n0, i, j + 2 + g)

                for c in range(2):
                    if c or f:
                        act.wait_ge(drained[(m0 + c - 2) % 4], (m0 + c - 2) // 4 + 1)
                    gate(m0 + c, 0, 0)
                    high_rows(d0, 0, c)
                    if c == 0:
                        for g in range(2):
                            high_block(n0, 0, 2 + g)
                with act.Fori(0, (NF - 2) // 4 - 1) as i:
                    four(i, 2, False)
                four(0, NF - 4, True)

            def w_in(l):
                with act.Fori(0, 2) as i:
                    for j in range(4):
                        m = FILL["xbc", l] + j
                        wait_slot_read(act, RING["win", l], i, j)
                        act.activation(xraw[:, bass.ds(i * 8 + 2 * j, 2), CONV_K - 1:],
                                       bank_of(m).rearrange("p (a b) -> p a b", a=2), ACT.Copy)\
                            .then_inc(drained[m % 4], 1)
                act.wait_ge(dn_ready, l + 1)
                s = step(act.activation(de, dn, ACT.Exp))
                act.activation(ea[:, 0:HEADS], heads3[:, 1, l, :], ACT.Exp)
                act.wait_ge(act_step, s)
                act.activation(dl, de, ACT.Ln, bias=1.0).then_inc(dl_ready, 1)
                for j in range(4):
                    m = FILL["z", l] + j
                    wait_slot_read(act, RING["win", l] + 8 + j)
                    act.activation(z[:, :, j * BLK:(j + 1) * BLK], bank_of(m).rearrange("p (a b) -> p a b", a=2),
                                   ACT.Silu).then_inc(drained[m % 4], 1)
                for q in range(4):
                    act.wait_ge(conv_done, NX * l + 4 * (q + 1))
                    act.activation(xc[:, 4 * q:4 * q + 4, :], xc[:, 4 * q:4 * q + 4, :], ACT.Silu).then_inc(xc_ready, 1)
                with act.Fori(0, 2) as i:
                    for j in range(4):
                        m = FILL["qkv", l] + j
                        wait_slot_read(act, RING["win", l] + 12, i, j)
                        act.activation(qk[:, :, bass.ds(i * D + j * BLK, BLK)],
                                       bank_of(m).rearrange("p (a b) -> p a b", a=2), ACT.Copy)\
                            .then_inc(drained[m % 4], 1)
                for j in range(4):
                    m = FILL["qkv", l] + 8 + j
                    wait_slot_read(act, RING["win", l] + 20 + j)
                    act.activation(v[:, :, j * BLK:(j + 1) * BLK], bank_of(m).rearrange("p (a b) -> p a b", a=2),
                                   ACT.Copy).then_inc(drained[m % 4], 1)

            def ssd(l):
                act.wait_ge(sq_ready, 2 * l + 1)
                act.activation(rqs, rq, ACT.Sqrt).then_inc(std_ready2, 1)
                act.wait_ge(nac_ready, l + 1)
                act.activation(dec[:, 0:HEADS], dd[:, 0:HEADS], ACT.Exp)
                act.activation(ex, nac, ACT.Exp, scale=-1.0).then_inc(decay_ready, 1)
                for q in range(4):
                    t, half = divmod(q, 2)
                    m = FILL["xt", l] + q
                    wait_filled(act, m)
                    act.activation(xtok[:, t, half * 512:(half + 1) * 512], bank_of(m), ACT.Copy)\
                        .then_inc(drained[m % 4], 1)
                m = FILL["bt", l]
                wait_filled(act, m)
                act.activation(btok.rearrange("p a b -> p (a b)"), bank_of(m), ACT.Copy).then_inc(drained[m % 4], 1)
                for part_, dst, col in ((0, qT, C_QN), (1, kT, C_KN)):
                    for q in (0, 2):
                        m = FILL["qkt", l] + 4 * part_ + q
                        wait_filled(act, m)
                        act.mul(dst[:, 2 * q:2 * q + 2, :], bank_of(m).rearrange("p (a b) -> p a b", a=2),
                                cola[:, l, col:col + 1]).then_inc(drained[m % 4], 1)
                for s in range(8):
                    act.wait_ge(seg_ready, 8 * l + s + 1)
                    act.activation(seg[:, s % 2, :], seg[:, s % 2, :], ACT.Exp).then_inc(seg_exp, 1)
                for q in range(2):
                    m = FILL["state", l] + q
                    wait_filled(act, m)
                    act.activation(prev[:, 2 * q:2 * q + 2, :], bank_of(m).rearrange("p (a b) -> p a b", a=2),
                                   ACT.Copy).then_inc(drained[m % 4], 1)
                act.wait_ge(sq_ready, 2 * l + 2)
                act.activation(gss, gs, ACT.Sqrt).then_inc(std_ready2, 1)

            def attention(l):
                m0 = FILL["att", l]
                scale = HD ** -0.5
                for h in range(HEADS + 2):
                    if h < HEADS:
                        act.wait_ge(smax_ready, HEADS * l + h + 1)
                        act.activation(sp3[:, h % 3, 0:P], sp3[:, h % 3, 0:P], ACT.Exp,
                                       bias=nmx[:, 2 * h:2 * h + 1], scale=scale)
                        act.activation(sp3[:, h % 3, P:3 * P], sp3[:, h % 3, P:3 * P], ACT.Exp,
                                       bias=nmx[:, 2 * h + 1:2 * h + 2], scale=scale).then_inc(p_exp, 1)
                    if h >= 2:
                        hh = h - 2
                        m = m0 + AF["T", hh]
                        wait_filled(act, m)
                        if hh >= 2:
                            act.wait_ge(av_done, HEADS * l + hh - 1)
                        act.activation(pT[:, hh % 2, :], bank_of(m)[:, 0:3 * P], ACT.Copy).then_inc(drained[m % 4], 1)

            def evac(m, n, dst, src_n, func=ACT.Copy, scale=1.0):
                wait_slot_read(act, n)
                act.activation(dst, bank_of(m).rearrange("p (a b) -> p a b", a=2), func, scale=scale)\
                    .then_inc(drained[m % 4], 1)

            def w_in2():
                m, n0 = FILL["a1"], RING["win2"]
                wait_filled(act, m)
                act.activation(a1T[0:RANK, :], bank_of(m)[0:RANK, 0:SEQ], ACT.Copy).then_inc(drained[m % 4], 1)
                for j in range(4):
                    evac(FILL["qk2"] + j, n0 + j, q2k2[:, 2 * j:2 * j + 2, :], 2,
                         scale=DK ** -0.5 if j < 2 else 1.0)
                for j in range(4):
                    evac(FILL["v2"] + j, n0 + 4 + j, v2[:, :, j * BLK:(j + 1) * BLK], 2)
                    if j == 0:
                        act.wait_ge(gl_ready, 1)
                        s = step(act.activation(lev_e[:, 0, :], lev_e[:, 0, :], ACT.Exp))
                        act.wait_ge(act_step, s)
                        act.activation(lev_e[:, 0, :], lev_e[:, 0, :], ACT.Ln, bias=1.0).then_inc(gl_log, 1)
                for j in range(4):
                    evac(FILL["pc"] + j, n0 + 8 + j, pc[:, 2 * j:2 * j + 2, :], 2,
                         ACT.Copy if j < 2 else ACT.Sigmoid)
                for j in range(4):
                    evac(FILL["r"] + j, n0 + 12 + j, rT[:, 2 * j:2 * j + 2, :], 2, ACT.Silu)
                with act.Fori(0, 2) as i:
                    for j in range(4):
                        m = FILL["gates"] + j
                        wait_slot_read(act, n0 + 16, i, j)
                        act.activation(gT[:, bass.ds(i * 8 + 2 * j, 2), :],
                                       bank_of(m).rearrange("p (a b) -> p a b", a=2), ACT.Sigmoid)\
                            .then_inc(drained[m % 4], 1)

            def gla():
                for s in range(len(LEVELS) + 1):
                    act.wait_ge(lev_ready, s + 1)
                    act.activation(lev_e[:, s % 2, :], lev_e[:, s % 2, :], ACT.Exp, scale=1.0 / TAU)\
                        .then_inc(lev_exp, 1)
                for h in range(GH):
                    m = FILL["o"] + h
                    wait_filled(act, m)
                    act.activation(oT[:, 2 * h:2 * h + 2, :], bank_of(m).rearrange("p (a b) -> p a b", a=2),
                                   ACT.Copy).then_inc(drained[m % 4], 1)
                act.wait_ge(var2, 1)
                act.activation(rgs, rg, ACT.Sqrt).then_inc(std2, 1)

            def conv_branch():
                act.wait_ge(var2, 2)
                act.activation(mean, mean, ACT.Sqrt).then_inc(std2, 1)
                act.wait_ge(zn_ready, 1)
                for c in range(NC2):
                    ins = act.activation(zc[:, c, :], zc[:, c, :], ACT.Silu, scale=colb[:, B_LG + c:B_LG + c + 1],
                                         bias=colb[:, B_LB + c:B_LB + c + 1])
                ins.then_inc(zs_ready, 1)

            def gathered_experts():
                m0 = FILL["moe"] + 1

                def copy3(i, j, dst, src=lambda b: b):
                    m = m0 + j
                    act.wait_ge(filled, i * 12 + fill_count(m0 + j))
                    act.activation(dst, src(bank_of(m)), ACT.Copy).then_inc(drained[m % 4], 1)

                def gates3(i, half, j):
                    for q in range(2):
                        m = m0 + j + q
                        act.wait_ge(filled, i * 12 + fill_count(m))
                        act.activation(gate_e[:, 2 * half + q, :], bank_of(m)[:, 0:2 * CAP], ACT.Silu)\
                            .then_inc(gate_ready, 1)

                def outs3(i, half, j):
                    rows_ = slice(half * CAP, (half + 1) * CAP)
                    for c in range(2):
                        copy3(i, j + c, out_e[rows_, c * 512:(c + 1) * 512], lambda b: b[rows_, :])

                def tokens(half):
                    return ueT[:, half, :, :].rearrange("p a b -> p (a b)")

                copy3(0, -1, tokens(0))
                with act.Fori(0, EXPERTS // 2) as i:
                    gates3(i, 0, 0)
                    copy3(i, 2, tokens(1))
                    for t in range(NT):
                        copy3(i, 3 + t, selT[:, t * P:(t + 1) * P], lambda b: b[:, 0:P])
                    outs3(i, 0, 5)
                    gates3(i, 1, 7)
                    outs3(i, 1, 9)
                    copy3(i, 11, tokens(0))

            def experts():
                m0 = FILL["moe"]
                for c in range(CPE):
                    wait_drained(act, m0 + c - 2)
                    gate(m0 + c, 0, 0)
                with act.Fori(0, EXPERTS - 1) as e:
                    for j in range(CPE):
                        wait_drained(act, m0 + 2, e, j)
                        gate(m0 + 4, e, j)

            for l in range(DEPTH):
                for g in range(2):
                    high_block(RING["ffn", 2 * l], 0, g)
                norm_high(3 * l, lambda k: cola[:, l, C_FFN1 + k:C_FFN1 + k + 1])
                ffn(2 * l)
                norm(3 * l + 1, lambda k: cola[:, l, C_MIX + k:C_MIX + k + 1])
                w_in(l)
                ssd(l)
                attention(l)
                turned(FILL["yt", l], (0, 2), yT, 0, lambda k: cola[:, l, C_SSD + k:C_SSD + k + 1])
                turned(FILL["yt", l] + 4, (0, 2), yT, KD, lambda k: 1.0)
                for g in range(2):
                    high_block(RING["ffn", 2 * l + 1], 0, g)
                norm_high(3 * l + 2, lambda k: cola[:, l, C_FFN2 + k:C_FFN2 + k + 1])
                ffn(2 * l + 1)
            wait_summed(act, ROWD["ffn", 2 * DEPTH - 1], 0, NF - 1)
            act.dma_start(masks.rearrange("p a b -> p (a b)"), d["masks"]).then_inc(masks_in, 16)
            norm(U1, lambda k: gains[:, 0, k:k + 1], shift=lambda k: mod[:, SH1, k:k + 1])
            w_in2()
            gla()
            conv_branch()
            for q in range(2):
                m = FILL["garow"] + q
                wait_filled(act, m)
                act.activation(garow[:, q * 512:(q + 1) * 512], bank_of(m), ACT.Copy).then_inc(drained[m % 4], 1)
            norm(U1 + 1, lambda k: gains[:, 1, k:k + 1], shift=lambda k: mod[:, SH2, k:k + 1])
            act.wait_ge(rt_in, 1)
            act.activation(rt_ge, rt_gd, ACT.Exp)
            act.activation(rt_pe, rt_pd, ACT.Exp).then_inc(rt_exp, 1)
            act.wait_ge(flag_ready, 1)
            few = act.value_load(flag[0:1, 0:1], min_val=0, max_val=1)
            with act.If(few > 0):
                gathered_experts()
            with act.Else():
                experts()
            norm(U1 + 2, None)
            act.wait_ge(y_final, 1)
            act.dma_start(out[0].rearrange("(t p) e -> p t e", p=P), x[:, :, :]).then_inc(out_done, 16)
            act.wait_ge(out_done, 16)

        @block.vector
        def _(dve):
            n = [0]

            def step(ins):
                n[0] += 1
                ins.then_inc(dve_step, 1)
                return n[0]

            def after_step(s):
                dve.wait_ge(dve_step, s)

            def link(ins):
                after_step(step(ins))

            def turned(m0, groups, dst, first, gain, shift=None):
                for q in groups:
                    wait_filled(dve, m0 + q)
                    b = bank_of(m0 + q)
                    for kk in range(2):
                        k = 2 * q + kk
                        src = b[:, kk * SEQ:(kk + 1) * SEQ]
                        if shift:
                            ins = dve.tensor_scalar(dst[:, first + k, :], src, gain(k), shift(k), ALU.mult, ALU.add)
                        else:
                            ins = dve.tensor_scalar(dst[:, first + k, :], src, gain(k), None, ALU.mult)
                    ins.then_inc(drained[(m0 + q) % 4], 1)

            def norm(u, gain, shift=None):
                for t in range(NT):
                    s = step(dve.tensor_tensor_reduce(xsc[:, t, :], x[:, t, :], x[:, t, :], 1.0, 0.0,
                                                      ALU.mult, ALU.add, ss[:, t:t + 1]))
                after_step(s)
                dve.tensor_scalar(ss, ss, 1.0 / D, EPS, ALU.mult, ALU.add).then_inc(var_ready, 1)
                dve.wait_ge(std_ready, u + 1)
                link(dve.reciprocal(rstd, std))
                for t in range(NT):
                    ins = dve.tensor_scalar(xsc[:, t, :], x[:, t, :], rstd[:, t:t + 1], None, ALU.mult)
                ins.then_inc(xsc_ready, 1)
                if gain:
                    turned(FILL["norm", u], (1, 3), xnT, 0, gain, shift)

            def norm_low(u, gain):
                norm(u, None)
                m0 = FILL["norm", u]
                for q in range(4):
                    dve.wait_ge(xh_ready, 4 * (u - u // 3) + q + 1 if u % 3 == 0 else 4 * (u - u // 3 - 1) + q + 1)
                    b = bank_of(m0 + q)
                    for kk in range(2):
                        k = 2 * q + kk
                        ins = dve.scalar_tensor_tensor(out=xl[:, k, :], in0=b[:, kk * SEQ:(kk + 1) * SEQ],
                                                       scalar=gain(k), in1=xh[:, k, :].bitcast(F32), op0=ALU.mult,
                                                       op1=ALU.subtract)
                    ins.then_inc(drained[(m0 + q) % 4], 1)

            def low_block(n0, i, j):
                wait_split(dve, high_in, n0, i, j)
                s = (n0 + j) % SLOTS
                dve.tensor_tensor(ring_low[:, s, :], ring[:, s, :], high_b[:, s, :].bitcast(F32), ALU.subtract)\
                    .then_inc(low_in[s], 1)

            def low_rows(d0, i, c):
                wait_split_d(dve, high_in_d, d0, i, c)
                s = (d0 + c) % SLOTS
                dve.tensor_tensor(ring_d_low[:, s, :], ring_d[:, s, :], high_r[:, s, :].bitcast(F32), ALU.subtract)\
                    .then_inc(low_in_d[s], 1)

            def hidden(g0, m0, d0, i, c):
                dve.wait_ge(gate_ready, i * 4 + (g0 + c + 1))
                if c >= 2:
                    wait_summed(dve, d0, i, c - 2)
                m = m0 + c
                q = m % 2
                dve.tensor_tensor(hid[:, q, :], bank_of(m)[:, SEQ:2 * SEQ], gate_s[:, q, :], ALU.mult)\
                    .then_inc(drained[m % 4], 1)
                wait_drained(dve, m0, i, c)
                dve.tensor_copy(hidh[:, q, :], hid[:, q, :]).then_inc(hid_high, 1)
                dve.wait_ge(hid_high, i * 4 + (g0 + c + 1))
                dve.tensor_tensor(hidl[:, q, :], hid[:, q, :], hidh[:, q, :].bitcast(F32), ALU.subtract)\
                    .then_inc(hid_low, 1)

            def ffn(f, a):
                m0, n0, d0, g0 = FILL["ffn", f], RING["ffn", f], ROWD["ffn", f], NF * f

                def chunk(i, j, more_):
                    hidden(g0, m0, d0, i, j)
                    low_rows(d0, i, j)
                    if j % 2 == 0 and more_:
                        for g in range(2):
                            low_block(n0, i, j + 2 + g)

                for c in range(2):
                    chunk(0, c, True)
                with dve.Fori(0, (NF - 2) // 4 - 1) as i:
                    for j in range(2, 6):
                        chunk(i, j, True)
                for c in range(NF - 4, NF):
                    chunk(0, c, c < NF - 2)
                if f % 2 and f < 2 * DEPTH - 1:
                    for g in range(2):
                        low_block(RING["ffn", f + 1], 0, g)
                wait_summed(dve, d0, 0, NF - 1)
                add_x(0.5)

            def add_x(factor):
                for t in range(NT):
                    for c in range(2):
                        cs = slice(c * 512, (c + 1) * 512)
                        s = step(dve.scalar_tensor_tensor(out=x[:, t, cs], in0=acc[:, t, cs], scalar=factor,
                                                          in1=x[:, t, cs], op0=ALU.mult, op1=ALU.add))
                after_step(s)
                dve.nop().then_inc(acc_free, 1)

            def w_in(l):
                link(dve.memset(xraw[:, :, 0:CONV_K - 1], 0.0))

                def taps(ch):
                    return lambda k: cola[:, l, C_CW + k * NX + ch:C_CW + k * NX + ch + 1]

                for q in range(NX // 4):
                    chunks = range(4 * q, 4 * q + 4)
                    for m in range(2):
                        wait_drained(dve, FILL["xbc", l] + 2 * q + m)
                    last = {}
                    for ch in chunks:
                        last[ch] = step(dve.tensor_scalar(
                            xc[:, ch, :], xraw[:, ch, CONV_K - 1:], taps(ch)(CONV_K - 1),
                            cola[:, l, C_CB + ch:C_CB + ch + 1], ALU.mult, ALU.add))
                    for k in range(CONV_K - 1):
                        for ch in chunks:
                            after_step(last[ch])
                            ins = dve.scalar_tensor_tensor(out=xc[:, ch, :], in0=xraw[:, ch, k:k + SEQ],
                                                           scalar=taps(ch)(k), in1=xc[:, ch, :],
                                                           op0=ALU.mult, op1=ALU.add)
                            if k < CONV_K - 2:
                                last[ch] = step(ins)
                            else:
                                ins.then_inc(conv_done, 1)
                m = FILL["dt", l]
                wait_filled(dve, m)
                for t in range(NT):
                    ins = dve.tensor_tensor(dr[:, t * HEADS:(t + 1) * HEADS],
                                            bank_of(m)[:, t * HEADS:(t + 1) * HEADS], heads3[:, 0, l, :], ALU.add)
                ins.then_inc(drained[m % 4], 1)
                wait_drained(dve, m)
                dve.scalar_tensor_tensor(out=dn, in0=dr, scalar=-1.0, in1=dr, op0=ALU.mult, op1=ALU.min)\
                    .then_inc(dn_ready, 1)
                dve.wait_ge(dl_ready, l + 1)
                link(dve.scalar_tensor_tensor(out=dtv, in0=dr, scalar=0.0, in1=dl, op0=ALU.max, op1=ALU.add))
                for t in range(NT):
                    hs = slice(t * HEADS, (t + 1) * HEADS)
                    ins = dve.scalar_tensor_tensor(out=adt[:, hs], in0=dtv[:, hs], scalar=-1.0,
                                                   in1=ea[:, 0:HEADS], op0=ALU.mult, op1=ALU.mult)
                ins.then_inc(adt_ready, 1)

            def heads_of(ap, n):
                return ap.rearrange("p (h e) -> p h e", h=n)

            def ssd(l, a):
                for q in range(8):
                    wait_drained(dve, FILL["qkv", l] + q)
                sq = qT.rearrange("p a b -> p (a b)")
                for t in range(NT):
                    link(dve.tensor_tensor(sq, qk[:, t, :], qk[:, t, :], ALU.mult))
                    s = step(dve.tensor_reduce(rq[:, t * 32:(t + 1) * 32], heads_of(sq, 32), AX_X, ALU.add))
                    after_step(s)
                dve.tensor_scalar(rq, rq, 1.0 / HD, EPS, ALU.mult, ALU.add).then_inc(sq_ready, 1)
                dve.wait_ge(std_ready2, 2 * l + 1)
                link(dve.reciprocal(rqr, rqs))
                for t in range(NT):
                    ins = dve.tensor_tensor(heads_of(qk[:, t, :], 32), heads_of(qk[:, t, :], 32),
                                            rqr[:, t * 32:(t + 1) * 32].unsqueeze(2).to_broadcast([P, 32, HD]),
                                            ALU.mult)
                ins.then_inc(qk_ready, 1)
                m = FILL["acum", l]
                wait_filled(dve, m)
                link(dve.tensor_scalar(nac, bank_of(m)[:, 0:32], -1.0, None, ALU.mult))
                dve.tensor_tensor(dd[:, 0:HEADS], bank_of(m)[:, 32:48], nac[:, 0:HEADS], ALU.add)\
                    .then_inc(drained[m % 4], 1)
                wait_drained(dve, m)
                dve.nop().then_inc(nac_ready, 1)
                for q in range(4):
                    wait_drained(dve, FILL["xt", l] + q)
                flat = xtok.rearrange("p t e -> p (t e)")
                flat_dt = xdt.rearrange("p t e -> p (t e)")
                link(dve.tensor_tensor(heads_of(flat_dt, 32), heads_of(flat, 32),
                                       dtv.unsqueeze(2).to_broadcast([P, 32, HD]), ALU.mult))
                dve.wait_ge(decay_ready, l + 1)
                wait_drained(dve, FILL["bt", l])
                dve.tensor_tensor(heads_of(xdec, HEADS), heads_of(xdt[:, 0, :], HEADS),
                                  dec[:, 0:HEADS].unsqueeze(2).to_broadcast([P, HEADS, HD]), ALU.mult)\
                    .then_inc(xdt_ready, 1)
                for part_, dst, col in ((0, qT, C_QN), (1, kT, C_KN)):
                    for q in (1, 3):
                        m = FILL["qkt", l] + 4 * part_ + q
                        wait_filled(dve, m)
                        dve.tensor_scalar(dst[:, 2 * q:2 * q + 2, :], bank_of(m).rearrange("p (a b) -> p a b", a=2),
                                          cola[:, l, col:col + 1], None, ALU.mult).then_inc(drained[m % 4], 1)
                link(dve.tensor_tensor(
                    flat.rearrange("p (t h e) -> p t h e", t=NT, h=HEADS)[:, 0], heads_of(xtok[:, 0, :], HEADS),
                    heads3[:, 2, l, :].unsqueeze(2).to_broadcast([P, HEADS, HD]), ALU.mult))
                link(dve.tensor_tensor(
                    heads_of(xtok[:, 1, :], HEADS), heads_of(xtok[:, 1, :], HEADS),
                    heads3[:, 2, l, :].unsqueeze(2).to_broadcast([P, HEADS, HD]), ALU.mult))
                for c in range(NT):
                    m = FILL["cb", l] + c
                    wait_filled(dve, m)
                    dve.tensor_tensor(cbm[:, c], bank_of(m).rearrange("p (a b) -> p a b", a=GROUPS),
                                      tri.unsqueeze(1).to_broadcast([P, GROUPS, P]), ALU.mult)\
                        .then_inc(drained[m % 4], 1)

                def decays(s):
                    c, g = divmod(s, GROUPS)
                    m = FILL["bc", l] + s
                    wait_filled(dve, m)
                    if s >= 2:
                        dve.wait_ge(y_done, 8 * l + s - 1)
                    for r in range(HPG):
                        col = c * HEADS + g * HPG + r
                        ins = dve.tensor_scalar(seg[:, s % 2, r * P:(r + 1) * P], bank_of(m)[:, r * P:(r + 1) * P],
                                                nac[:, col:col + 1], 0.0, ALU.add, ALU.min)
                    ins.then_inc(drained[m % 4], 1)
                    wait_drained(dve, m)
                    dve.nop().then_inc(seg_ready, 1)

                def mixes(s):
                    c, g = divmod(s, GROUPS)
                    dve.wait_ge(seg_exp, 8 * l + s + 1)
                    sv = seg[:, s % 2, :].rearrange("p (a b) -> p a b", a=HPG)
                    dve.tensor_tensor(sv, sv, cbm[:, c, g, :].unsqueeze(1).to_broadcast([P, HPG, P]), ALU.mult)\
                        .then_inc(mix_ready, 1)

                for s in range(9):
                    if s < 8:
                        decays(s)
                    if s >= 1:
                        mixes(s - 1)
                dve.wait_ge(y_done, 8 * (l + 1))
                for t in range(NT):
                    for c in range(2):
                        cs = slice(c * 512, (c + 1) * 512)
                        s = step(dve.tensor_tensor(xtok[:, t, cs], xtok[:, t, cs], acc[:, t, cs], ALU.add))
                after_step(s)
                dve.nop().then_inc(acc_free, 1)
                for q in range(2):
                    m = FILL["off", l] + q
                    wait_filled(dve, m)
                    o = xdt[:, 0, 0:512]
                    dve.tensor_tensor(heads_of(o, 8), heads_of(bank_of(m), 8),
                                      ex[:, HEADS + 8 * q:HEADS + 8 * q + 8].unsqueeze(2).to_broadcast([P, 8, HD]),
                                      ALU.mult).then_inc(drained[m % 4], 1)
                    wait_drained(dve, m)
                    cs = slice(q * 512, (q + 1) * 512)
                    link(dve.tensor_tensor(xtok[:, 1, cs], xtok[:, 1, cs], o, ALU.add))
                link(dve.tensor_tensor(flat, flat, z.rearrange("p t e -> p (t e)"), ALU.mult))
                link(dve.tensor_tensor(flat_dt, flat, flat, ALU.mult))
                link(dve.tensor_reduce(gs, heads_of(flat_dt, 8), AX_X, ALU.add))
                dve.tensor_scalar(gs, gs, 1.0 / BLK, EPS, ALU.mult, ALU.add).then_inc(sq_ready, 1)
                dve.wait_ge(std_ready2, 2 * l + 2)
                link(dve.reciprocal(gsr, gss))
                dve.tensor_tensor(heads_of(flat, 8), heads_of(flat, 8), gsr.unsqueeze(2).to_broadcast([P, 8, BLK]),
                                  ALU.mult).then_inc(ysd_ready, 1)

            def attention(l, a):
                m0 = FILL["att", l]

                def maxima(h):
                    m = m0 + AF["S", h]
                    wait_filled(dve, m)
                    if h >= 3:
                        wait_filled(dve, m0 + AF["T", h - 3])
                    dve.tensor_tensor_reduce(sp3[:, h % 3, 0:P], bank_of(m)[:, 0:P], konst[:, K_NEG:K_NEG + P],
                                             1.0, NEG, ALU.add, ALU.max, mx[:, 2 * h:2 * h + 1])
                    dve.tensor_tensor_reduce(sp3[:, h % 3, P:3 * P], bank_of(m)[:, P:3 * P],
                                             konst[:, K_NEG + P:K_NEG + 3 * P],
                                             1.0, NEG, ALU.add, ALU.max, mx[:, 2 * h + 1:2 * h + 2])\
                        .then_inc(drained[m % 4], 1)
                    wait_drained(dve, m)
                    dve.tensor_scalar(nmx[:, 2 * h:2 * h + 2], mx[:, 2 * h:2 * h + 2], -(HD ** -0.5), None,
                                      ALU.mult).then_inc(smax_ready, 1)

                def weights(h):
                    dve.wait_ge(p_exp, HEADS * l + h + 1)
                    dve.tensor_tensor_reduce(sp3[:, h % 3, 0:P], sp3[:, h % 3, 0:P], konst[:, K_CNT:K_CNT + P],
                                             1.0, 0.0, ALU.mult, ALU.add, den[:, h:h + 1])
                    dve.tensor_tensor_reduce(sp3[:, h % 3, P:3 * P], sp3[:, h % 3, P:3 * P],
                                             konst[:, K_CNT + P:K_CNT + 3 * P],
                                             1.0, 0.0, ALU.mult, ALU.add, den[:, HEADS + h:HEADS + h + 1])\
                        .then_inc(p_ready, 1)

                for h in range(HEADS + 1):
                    if h < HEADS:
                        maxima(h)
                    if h >= 1:
                        weights(h - 1)
                dve.wait_ge(p_ready, HEADS * (l + 1))
                link(dve.reciprocal(rden, den))
                dve.wait_ge(av_done, HEADS * (l + 1))
                for t in range(NT):
                    for c in range(2):
                        cs = slice(c * 512, (c + 1) * 512)
                        rs = rden[:, t * HEADS + 8 * c:t * HEADS + 8 * c + 8]
                        s = step(dve.tensor_tensor(heads_of(yatt[:, t, cs], 8), heads_of(acc[:, t, cs], 8),
                                                   rs.unsqueeze(2).to_broadcast([P, 8, HD]), ALU.mult))
                after_step(s)
                dve.nop().then_inc(acc_free, 1)
                dve.nop().then_inc(yatt_ready, 1)

            def modulation(p):
                m = FILL["mod", p]
                wait_filled(dve, m)
                dve.tensor_tensor(mod[:, p, :], bank_of(m)[:, 0:KD], colb[:, B_ADA + KD * p:B_ADA + KD * (p + 1)],
                                  ALU.add).then_inc(drained[m % 4], 1)
                wait_drained(dve, m)

            def decays2():
                link(dve.memset(attn.rearrange("p a b -> p (a b)"), 0.0))
                link(dve.memset(lev_e[:, 1, 0:P], 1.0))
                link(dve.memset(zpad[:, :, 0:CONV_W - 1], 0.0))
                flat = graw.rearrange("p h s -> p (h s)")
                for q in range(2):
                    m = FILL["a2"] + q
                    wait_filled(dve, m)
                    for hh in range(2):
                        h = 2 * q + hh
                        ins = dve.tensor_scalar(graw[:, h, :], bank_of(m)[:, hh * SEQ:(hh + 1) * SEQ],
                                                colb[:, B_A2 + h:B_A2 + h + 1], None, ALU.add)
                    ins.then_inc(drained[m % 4], 1)
                for q in range(2):
                    wait_drained(dve, FILL["a2"] + q)
                dve.scalar_tensor_tensor(out=lev_e[:, 0, :], in0=flat, scalar=-1.0, in1=flat, op0=ALU.mult,
                                         op1=ALU.min).then_inc(gl_ready, 1)
                dve.wait_ge(gl_log, 1)
                link(dve.scalar_tensor_tensor(out=flat, in0=flat, scalar=0.0, in1=lev_e[:, 0, :],
                                              op0=ALU.min, op1=ALU.subtract))
                for h in range(GH):
                    for t in range(NT):
                        ts = slice(t * P, (t + 1) * P)
                        s = step(dve.tensor_tensor_scan(bcum[:, h, ts], lev_e[:, 1, 0:P], graw[:, h, ts], 0.0,
                                                        ALU.mult, ALU.add))
                after_step(s)
                for j in range(4):
                    wait_drained(dve, FILL["qk2"] + j)

            def level(s):
                e, o = lev_e[:, s % 2, :], lev_qk[:, s % 2, :]
                if s < len(LEVELS):
                    w = LEVELS[s]
                    ev, bv = (a.rearrange("p (n w) -> p n w", w=2 * w) for a in (e, bcum.rearrange("p h s -> p (h s)")))
                    mid = bv[:, :, w - 1:w].to_broadcast([P, GH * SEQ // (2 * w), w])
                    dve.tensor_tensor(ev[:, :, 0:w], mid, bv[:, :, 0:w], ALU.subtract)
                    dve.tensor_tensor(ev[:, :, w:2 * w], bv[:, :, w:2 * w], mid, ALU.subtract).then_inc(lev_ready, 1)
                    first, second = slice(0, w), slice(w, 2 * w)
                    n, width = GH * SEQ // (2 * w), 2 * w
                else:
                    ev = e.rearrange("p (h s) -> p h s", h=GH)
                    dve.tensor_tensor(ev[:, :, 0:P], bcum[:, :, P - 1:P].to_broadcast([P, GH, P]), bcum[:, :, 0:P],
                                      ALU.subtract)
                    dve.tensor_copy(ev[:, :, P:SEQ], bcum[:, :, P:SEQ]).then_inc(lev_ready, 1)
                    first, second = slice(0, P), slice(P, SEQ)
                    width = SEQ
                dve.wait_ge(lev_exp, s + 1)
                if s >= 2:
                    wait_filled(dve, FILL["pairs"] + 2 * (s - 2) + 1)
                ev, ov, qv, kv = (a.rearrange("p (n w) -> p n w", w=width) for a in
                                  (e, o, q2k2[:, 0:GH, :].rearrange("p h s -> p (h s)"),
                                   q2k2[:, GH:2 * GH, :].rearrange("p h s -> p (h s)")))
                dve.tensor_tensor(ov[:, :, first], ev[:, :, first], kv[:, :, first], ALU.mult)
                dve.tensor_tensor(ov[:, :, second], ev[:, :, second], qv[:, :, second], ALU.mult)\
                    .then_inc(lev_qk_ready, 1)

            def gated():
                for j in range(4):
                    wait_drained(dve, FILL["pc"] + j)
                link(dve.tensor_tensor(zpad[:, :, CONV_W - 1:], pc[:, 0:NC2, :], pc[:, NC2:2 * NC2, :], ALU.mult))
                last = [0] * NC2
                for c in range(NC2):
                    last[c] = step(dve.tensor_scalar(zc[:, c, :], zpad[:, c, 0:SEQ], colc[:, c:c + 1],
                                                     colb[:, B_DW + c:B_DW + c + 1], ALU.mult, ALU.add))
                for k in range(1, CONV_W):
                    for c in range(NC2):
                        after_step(last[c])
                        last[c] = step(dve.scalar_tensor_tensor(
                            out=zc[:, c, :], in0=zpad[:, c, k:k + SEQ], scalar=colc[:, k * NC2 + c:k * NC2 + c + 1],
                            in1=zc[:, c, :], op0=ALU.mult, op1=ALU.add))
                after_step(last[NC2 - 1])
                dve.nop().then_inc(z_out, 1)

            def gla():
                dve.wait_ge(masks_in, 16)
                for s in range(len(LEVELS) + 1):
                    for t in range(NT):
                        m = FILL["pairs"] + 2 * s + t
                        wait_filled(dve, m)
                        dve.copy_predicated(attn[:, t * GH:(t + 1) * GH, :],
                                            masks[:, s:s + 1, :].bitcast(U32).to_broadcast([P, GH, P]),
                                            bank_of(m).rearrange("p (a b) -> p a b", a=GH))\
                            .then_inc(drained[m % 4], 1)
                        wait_drained(dve, m)
                    if s + 2 <= len(LEVELS):
                        level(s + 2)
                m = FILL["cross"]
                wait_filled(dve, m)
                dve.tensor_copy(across.rearrange("p a b -> p (a b)"), bank_of(m)).then_inc(drained[m % 4], 1)
                for h in range(GH):
                    wait_drained(dve, FILL["o"] + h)
                dve.tensor_tensor(osq, oT, oT, ALU.mult).then_inc(o_sq, 1)
                for q in range(2):
                    m = FILL["osum"] + q
                    wait_filled(dve, m)
                    ins = dve.tensor_scalar(rg[:, 2 * q:2 * q + 2, :], bank_of(m).rearrange("p (a b) -> p a b", a=2),
                                            1.0 / DV, EPS, ALU.mult, ALU.add).then_inc(drained[m % 4], 1)
                for q in range(2):
                    wait_drained(dve, FILL["osum"] + q)
                dve.nop().then_inc(var2, 1)
                dve.wait_ge(std2, 1)
                link(dve.reciprocal(rg, rgs))
                for j in range(4):
                    wait_drained(dve, FILL["r"] + j)
                o4 = oT.rearrange("p (h c) s -> p h c s", h=GH)
                for c in range(2):
                    s = step(dve.tensor_tensor(o4[:, :, c, :], o4[:, :, c, :], rg, ALU.mult))
                after_step(s)
                for k in range(KD):
                    ins = dve.scalar_tensor_tensor(out=oT[:, k, :], in0=oT[:, k, :],
                                                   scalar=colb[:, B_GLA + k:B_GLA + k + 1], in1=rT[:, k, :],
                                                   op0=ALU.mult, op1=ALU.mult)
                ins.then_inc(og_ready, 1)

            def conv_branch():
                m = FILL["mean"]
                wait_filled(dve, m)
                dve.tensor_scalar(mean, bank_of(m)[:, 0:SEQ], 1.0 / CW2, None, ALU.mult).then_inc(drained[m % 4], 1)
                wait_drained(dve, m)
                link(dve.tensor_tensor(zc, zc, mean.unsqueeze(1).to_broadcast([P, NC2, SEQ]), ALU.subtract))
                dve.tensor_tensor(zsq, zc, zc, ALU.mult).then_inc(z_out, 1)
                m = FILL["var"]
                wait_filled(dve, m)
                dve.tensor_scalar(mean, bank_of(m)[:, 0:SEQ], 1.0 / CW2, EPS, ALU.mult, ALU.add)\
                    .then_inc(drained[m % 4], 1)
                wait_drained(dve, m)
                dve.nop().then_inc(var2, 1)
                dve.wait_ge(std2, 2)
                link(dve.reciprocal(mean, mean))
                dve.tensor_tensor(zc, zc, mean.unsqueeze(1).to_broadcast([P, NC2, SEQ]), ALU.mult)\
                    .then_inc(zn_ready, 1)

            def merge():
                for j in range(8):
                    wait_drained(dve, FILL["gates"] + j)
                for q in range(4):
                    m = FILL["pwa", 0] + q
                    if q % 2:
                        wait_slot_read(dve, RING["pw"] + q // 2)
                    else:
                        wait_filled(dve, m)
                    for c in range(2):
                        k = 2 * q + c
                        ins = dve.scalar_tensor_tensor(out=merged[:, k, :], in0=bank_of(m)[:, c * SEQ:(c + 1) * SEQ],
                                                       scalar=colb[:, B_PW + k:B_PW + k + 1], in1=gT[:, k, :],
                                                       op0=ALU.add, op1=ALU.mult)
                    ins.then_inc(drained[m % 4], 1)
                for q in range(4):
                    m = FILL["ygla"] + q
                    ks = slice(2 * q, 2 * q + 2)
                    wait_slot_read(dve, RING["glao"] + q)
                    wait_drained(dve, FILL["pwa", 0] + q)
                    dve.tensor_tensor(osq[:, ks, :], bank_of(m).rearrange("p (a b) -> p a b", a=2),
                                      gT[:, KD + 2 * q:KD + 2 * q + 2, :], ALU.mult).then_inc(drained[m % 4], 1)
                    wait_drained(dve, m)
                    s = step(dve.tensor_tensor(merged[:, ks, :], merged[:, ks, :], osq[:, ks, :], ALU.add))
                after_step(s)
                dve.nop().then_inc(merged_ready, 1)
                diagonal(mod[:, GA1, :])
                n = RING["wout2"] + 3
                wait_slot_read(dve, n)
                for q in range(2):
                    wait_drained(dve, FILL["garow"] + q)
                for t in range(NT):
                    for c in range(2):
                        cs = slice(c * 512, (c + 1) * 512)
                        s = step(dve.tensor_tensor(xsc[:, t, cs], acc[:, t, cs], garow[:, cs], ALU.mult))
                after_step(s)
                dve.nop().then_inc(acc_free, 1)
                link(dve.tensor_tensor(x[:, :, :], x[:, :, :], xsc, ALU.add))

            def diagonal(col):
                dve.tensor_tensor(diag.rearrange("p (k m) -> p k m", k=KD),
                                  ident.unsqueeze(1).to_broadcast([P, KD, P]),
                                  col.unsqueeze(2).to_broadcast([P, KD, P]), ALU.mult).then_inc(diag_ready, 1)

            def routing():
                m = FILL["router"]
                wait_filled(dve, m)
                n36 = N_GROUPS + EXPERTS
                dve.tensor_tensor(logit, bank_of(m)[:, 0:NT * n36].rearrange("p (t e) -> p t e", t=NT),
                                  br[:, :].unsqueeze(1).to_broadcast([P, NT, n36]), ALU.add)\
                    .then_inc(drained[m % 4], 1)
                wait_drained(dve, m)
                lg, le = logit[:, :, 0:N_GROUPS], logit[:, :, N_GROUPS:]

                def first_max(score, width, top, mark):
                    link(dve.tensor_reduce(top, score, AX_X, ALU.max))
                    link(dve.tensor_tensor(mark, score, top.to_broadcast([P, NT, width]), ALU.is_equal))
                    link(dve.tensor_tensor(mark, mark, rank[:, 0:width].unsqueeze(1).to_broadcast([P, NT, width]),
                                           ALU.mult))
                    link(dve.tensor_reduce(rt_r, mark, AX_X, ALU.max))
                    link(dve.tensor_tensor(mark, mark, rt_r.to_broadcast([P, NT, width]), ALU.is_equal))

                for e in range(EXPERTS):
                    s = step(dve.memset(rank[:, e:e + 1], float(EXPERTS - e)))
                after_step(s)
                first_max(lg, N_GROUPS, rt_mg, rt_og)
                link(dve.tensor_tensor(rt_gd, lg, rt_mg.to_broadcast([P, NT, N_GROUPS]), ALU.subtract))
                link(dve.tensor_scalar(rt_pen, rt_og, -NEG, NEG, ALU.mult, ALU.add))
                for t in range(NT):
                    s = step(dve.tensor_tensor(
                        cand[:, t, :].rearrange("p (g e) -> p g e", g=N_GROUPS),
                        le[:, t, :].rearrange("p (g e) -> p g e", g=N_GROUPS),
                        rt_pen[:, t, :].unsqueeze(2).to_broadcast([P, N_GROUPS, PER_GROUP]), ALU.add))
                after_step(s)
                first_max(cand, EXPERTS, rt_m1, mark1)
                link(dve.scalar_tensor_tensor(out=cand, in0=mark1, scalar=2 * NEG, in1=cand,
                                              op0=ALU.mult, op1=ALU.add))
                first_max(cand, EXPERTS, rt_m2, mark2)
                dve.tensor_tensor(rt_pd, rt_m2, rt_m1, ALU.subtract).then_inc(rt_in, 1)
                dve.wait_ge(rt_exp, 1)
                link(dve.tensor_reduce(rt_m, rt_ge, AX_X, ALU.add))
                link(dve.scalar_tensor_tensor(out=rt_m, in0=rt_pe, scalar=1.0, in1=rt_m, op0=ALU.add, op1=ALU.mult))
                link(dve.reciprocal(rt_m, rt_m))
                link(dve.memset(comb.rearrange("p a b -> p (a b)"), 0.0))
                cv = comb[:, :, 0:EXPERTS]
                for t in range(NT):
                    link(dve.scalar_tensor_tensor(out=cv[:, t, :], in0=mark2[:, t, :], scalar=rt_pe[:, t, :],
                                                  in1=mark1[:, t, :], op0=ALU.mult, op1=ALU.add))
                    link(dve.tensor_scalar(cv[:, t, :], cv[:, t, :], rt_m[:, t, :], None, ALU.mult))
                dve.tensor_tensor(mark1, mark1, mark2, ALU.add).then_inc(mask_ready, 1)

            def rows_and_tokens():
                for i, (col, dst) in enumerate(((gains[:, 1, :], row2[:, 0, :]), (mod[:, SH2, :], row2[:, 1, :]),
                                                (mod[:, GA2, :], rowf[:, 0, :]), (gains[:, 2, :], rowf[:, 1, :]),
                                                (mod[:, SHF, :], rowf[:, 2, :]))):
                    diagonal(col)
                    for q in range(2):
                        m = FILL["rows"] + 2 * i + q
                        wait_filled(dve, m)
                        dve.tensor_copy(dst[:, q * 512:(q + 1) * 512], bank_of(m)).then_inc(drained[m % 4], 1)
                for q in range(10):
                    wait_drained(dve, FILL["rows"] + q)
                for t in range(NT):
                    link(dve.tensor_tensor(u2[:, t, :], xsc[:, t, :], row2[:, 0, :], ALU.mult))
                    link(dve.tensor_tensor(u2[:, t, :], u2[:, t, :], row2[:, 1, :], ALU.add))
                dve.nop().then_inc(more_free, 1)

            def placing():
                m = FILL["count"]
                wait_filled(dve, m)
                b = bank_of(m)
                link(dve.memset(place.rearrange("p a b -> p (a b)"), -1.0))
                link(dve.tensor_tensor(place[:, :, 0:EXPERTS], b[:, 0:2 * EXPERTS].rearrange("p (t e) -> p t e", t=NT),
                                       mark1, ALU.mult))
                link(dve.tensor_scalar(place[:, :, 0:EXPERTS], place[:, :, 0:EXPERTS], -1.0, None, ALU.add))
                dve.tensor_reduce(number[:, 0, :], b[:, 2 * EXPERTS:3 * EXPERTS], AX_X, ALU.max)\
                    .then_inc(drained[m % 4], 1)
                wait_drained(dve, m)
                dve.tensor_scalar(flag[:, :], number[:, 0, :], CAP + 0.5, None, ALU.is_lt).then_inc(flag_ready, 1)

            def gathered_experts():
                m0, g0 = FILL["moe"] + 1, 2 * DEPTH * NF
                iota = konst[:, K_IOTA:K_IOTA + CAP]

                def at_(a, t, e):
                    return a[:, t, e:e + 1] if isinstance(e, int) else a[:, t, bass.ds(e, 1)]

                def choose(e, half):
                    for t in range(NT):
                        ins = dve.tensor_scalar(sel[:, half, t, :], iota, at_(place, t, e), None, ALU.is_equal)
                    ins.then_inc(sel_ready, 1)

                def weigh(e):
                    for half in range(2):
                        for t in range(NT):
                            ins = dve.tensor_scalar(selw[:, t, half * CAP:(half + 1) * CAP], iota,
                                                    at_(place, t, e + half), at_(comb, t, e + half),
                                                    ALU.is_equal, ALU.mult)
                    ins.then_inc(selw_ready, 1)

                def products(i, half, j):
                    for q in range(2):
                        m = m0 + j + q
                        dve.wait_ge(gate_ready, i * 4 + (g0 + 2 * half + q + 1))
                        dve.tensor_tensor(hid_e[:, 2 * q:2 * q + 2, half * CAP:(half + 1) * CAP],
                                          bank_of(m)[:, 2 * CAP:4 * CAP].rearrange("p (a b) -> p a b", a=2),
                                          gate_e[:, 2 * half + q, :].rearrange("p (a b) -> p a b", a=2), ALU.mult)\
                            .then_inc(drained[m % 4], 1)

                def filled3(i, j):
                    dve.wait_ge(filled, i * 12 + fill_count(m0 + j))

                dve.memset(hid_e.rearrange("p a b -> p (a b)"), 0.0)
                dve.memset(selT, 0.0)
                dve.memset(out_e, 0.0).then_inc(zero_ready, 1)
                choose(0, 0)
                choose(1, 1)
                weigh(0)
                with dve.Fori(0, EXPERTS // 2) as i:
                    i2 = i * 2
                    products(i, 0, 0)
                    choose(i2 + 2, 0)
                    filled3(i, 4)
                    choose(i2 + 3, 1)
                    weigh(i2 + 2)
                    products(i, 1, 7)
                dve.wait_ge(scattered, EXPERTS // 2)
                for t in range(NT):
                    for c in range(2):
                        cs = slice(c * 512, (c + 1) * 512)
                        ins = dve.tensor_copy(y2[:, t, cs], acc[:, t, cs])
                ins.then_inc(y_ready, 1)

            def experts():
                m0, g0 = FILL["moe"], 2 * DEPTH * NF

                def hidden8(i, c):
                    dve.wait_ge(gate_ready, i * 8 + (g0 + c + 1))
                    if c >= 2:
                        half, cc = divmod((c - 2) % 8, CPE)
                        wait_pair_summed(dve, half, i + (c - 2) // 8, cc)
                    m = m0 + c
                    dve.tensor_tensor(hid[:, m % 2, :], bank_of(m)[:, SEQ:2 * SEQ], gate_s[:, m % 2, :], ALU.mult)\
                        .then_inc(drained[m % 4], 1)

                def add_expert(i, half):
                    dve.wait_ge(acc_free, i * 2 + (A1 + 1 + half))
                    wait_pair_summed(dve, half, i, CPE - 1)
                    for t in range(NT):
                        for c in range(2):
                            cs = slice(c * 512, (c + 1) * 512)
                            e = i * 2 + half
                            w = comb[:, t, e:e + 1] if isinstance(e, int) else comb[:, t, bass.ds(e, 1)]
                            ins = dve.scalar_tensor_tensor(out=y2[:, t, cs], in0=acc[:, t, cs], scalar=w,
                                                           in1=y2[:, t, cs], op0=ALU.mult, op1=ALU.add)
                    return ins

                dve.memset(y2.rearrange("p a b -> p (a b)"), 0.0).then_inc(zero_ready, 1)
                dve.wait_ge(zero_ready, 1)
                for c in range(CPE):
                    hidden8(0, c)
                with dve.Fori(0, EXPERTS // 2 - 1) as i:
                    for half in range(2):
                        hidden8(i, CPE * (half + 1))
                        add_expert(i, half).then_inc(acc_free, 1)
                        for j in range(1, CPE):
                            hidden8(i, CPE * (half + 1) + j)
                i = EXPERTS // 2 - 1
                hidden8(i, CPE)
                add_expert(i, 0).then_inc(acc_free, 1)
                for j in range(1, CPE):
                    hidden8(i, CPE + j)
                add_expert(i, 1).then_inc(y_ready, 1)

            def final():
                dve.wait_ge(y_ready, 1)
                for t in range(NT):
                    link(dve.tensor_tensor(y2[:, t, :], y2[:, t, :], rowf[:, 0, :], ALU.mult))
                    link(dve.tensor_tensor(x[:, t, :], x[:, t, :], y2[:, t, :], ALU.add))
                norm(U1 + 2, None)
                dve.wait_ge(xsc_ready, U1 + 3)
                for t in range(NT):
                    link(dve.tensor_tensor(xsc[:, t, :], xsc[:, t, :], rowf[:, 1, :], ALU.mult))
                    s = step(dve.tensor_tensor(x[:, t, :], xsc[:, t, :], rowf[:, 2, :], ALU.add))
                after_step(s)
                dve.nop().then_inc(y_final, 1)

            dve.memset(ones[:, :], 1.0).then_inc(ones_set, 1)
            for i, dst in enumerate((cola[:, 0, :], cola[:, 1, :], colb[:, :], colc[:, :])):
                wait_filled(dve, i)
                dve.tensor_copy(dst, bank_of(i)[:, 0:dst.shape[1]]).then_inc(drained[i], 1)
            for i in range(4):
                wait_drained(dve, i)
            dve.wait_ge(x_in, 16)
            for l in range(DEPTH):
                if not l:
                    for g in range(2):
                        low_block(RING["ffn", 0], 0, g)
                norm_low(3 * l, lambda k: cola[:, l, C_FFN1 + k:C_FFN1 + k + 1])
                ffn(2 * l, 5 * l)
                modulation(4 * l)
                norm(3 * l + 1, lambda k: cola[:, l, C_MIX + k:C_MIX + k + 1])
                w_in(l)
                modulation(4 * l + 1)
                ssd(l, 5 * l + 1)
                attention(l, 5 * l + 2)
                turned(FILL["yt", l], (1, 3), yT, 0, lambda k: cola[:, l, C_SSD + k:C_SSD + k + 1])
                turned(FILL["yt", l] + 4, (1, 3), yT, KD, lambda k: 1.0)
                for g in range(2):
                    low_block(RING["ffn", 2 * l + 1], 0, g)
                wait_slot_read(dve, RING["wout", l] + 7)
                add_x(1.0)
                modulation(4 * l + 2)
                norm_low(3 * l + 2, lambda k: cola[:, l, C_FFN2 + k:C_FFN2 + k + 1])
                ffn(2 * l + 1, 5 * l + 4)
                modulation(4 * l + 3)
            for i, (col, sc) in enumerate(((B_N1, SC1), (B_N2, SC2), (B_NF, SCF))):
                s = step(dve.scalar_tensor_tensor(out=gains[:, i, :], in0=mod[:, sc, :], scalar=1.0,
                                                  in1=colb[:, col:col + KD], op0=ALU.add, op1=ALU.mult))
            after_step(s)
            norm(U1, lambda k: gains[:, 0, k:k + 1], shift=lambda k: mod[:, SH1, k:k + 1])
            decays2()
            level(0)
            level(1)
            gated()
            gla()
            conv_branch()
            merge()
            norm(U1 + 1, lambda k: gains[:, 1, k:k + 1], shift=lambda k: mod[:, SH2, k:k + 1])
            routing()
            rows_and_tokens()
            placing()
            dve.wait_ge(flag_ready, 1)
            few = dve.value_load(flag[0:1, 0:1], min_val=0, max_val=1)
            with dve.If(few > 0):
                gathered_experts()
            with dve.Else():
                experts()
            final()




_INS = ["x", "ffn1_norm", "ffn1_w_gate", "ffn1_w_up", "ffn1_w_down", "mix_norm", "w_in", "conv_w", "conv_b",
        "dt_bias", "a_log", "d_skip", "ssd_norm", "q_norm", "k_norm", "w_out", "ffn2_norm", "ffn2_w_gate",
        "ffn2_w_up", "ffn2_w_down", "c_2", "w_ada_2", "b_ada_2", "g_norm1_2", "w_in_2", "w_dw_2", "b_dw_2",
        "g_conv_ln_2", "b_conv_ln_2", "w_conv_pw_2", "b_conv_pw_2", "w_a2_2", "b_a2_2", "g_gla_norm_2",
        "w_gla_o_2", "w_out_2", "g_norm2_2", "w_router_g_2", "b_router_g_2", "w_router_e_2", "b_router_e_2",
        "w1_2", "w3_2", "w2_2", "w_ada_f_2", "b_ada_f_2", "g_final_2"]
_OUTS = [((1, 256, 1024), "float32")]


def kernel(**inputs):
    import numpy as _np
    import concourse.bacc as _bacc
    from concourse import mybir as _mybir
    from concourse.bass_utils import run_bass_kernel_spmd as _run

    nc = _bacc.Bacc("TRN2", target_bir_lowering=False, num_devices=1)
    arrays, args = {}, {}
    for name in _INS:
        a = _np.ascontiguousarray(inputs[name])
        arrays[f"in_{name}_dram"] = a
        args[name] = nc.dram_tensor(f"in_{name}_dram", a.shape, _mybir.dt.from_np(a.dtype), kind="ExternalInput").ap()
    for name, table in (("consts", constants()), ("masks", pair_masks())):
        arrays[f"in_{name}_dram"] = table
        args[name] = nc.dram_tensor(f"in_{name}_dram", table.shape, F32, kind="ExternalInput").ap()
    (shape, dtype), = _OUTS
    out = nc.dram_tensor("out_0_dram", shape, _mybir.dt.from_np(_np.dtype(dtype)), kind="ExternalOutput").ap()
    two_blocks(nc, args, out)
    r = _run(nc, [arrays], core_ids=[0])
    return r.results[0]["out_0_dram"]
```

```python
from contextlib import ExitStack

import concourse.bass as bass
from concourse import mybir
import numpy as np

F32 = mybir.dt.float32
F32R = mybir.dt.float32r
U32 = mybir.dt.uint32
ALU = mybir.AluOpType
ACT = mybir.ActivationFunctionType
AX_X = mybir.AxisListType.X

P = 128
SEQ = 256
NT = SEQ // P
D = 1024
KD = D // P
DEPTH = 2
D_FF = 2816
NF = D_FF // P
EPS = 1e-6
HEADS = 16
HD = 64
GROUPS = 4
HPG = HEADS // GROUPS
CONV_K = 4
XBC = 2048
NX = XBC // P
BLK = 256
BACK = 128
DILATIONS = (1, 4, 16)
NEG = -1e30

ARENA = 32512
SLOTS = 4
SLOT = KD * BLK
SLOT_D = D
LOAD = 16

C_FFN1, C_MIX, C_FFN2, C_CW, C_CB, C_SSD, C_QN, C_KN = 0, 8, 16, 24, 88, 104, 112, 113
N_COLA = 114


CW2 = 512
NC2 = CW2 // P
CONV_W = 31
GH = 4
DK = 128
DV = 256
RANK = 16
TAU = 16.0
QK0, V0, R0, A0, G0 = 1024, 2048, 3072, 4096, 4112
N_PROJ2 = 24
N_GROUPS = 4
PER_GROUP = 8
EXPERTS = N_GROUPS * PER_GROUP
D_EXPERT = 512
CPE = D_EXPERT // P
CAP = 64
LEVELS = (64, 32, 16, 8, 4, 2, 1)
PIECES = 8
SH1, SC1, GA1, SH2, SC2, GA2, SHF, SCF = range(PIECES)

B_ADA, B_C, B_N1, B_N2, B_NF, B_PW, B_GLA, B_DW, B_LG, B_LB, B_A2 = 0, 64, 72, 80, 88, 96, 104, 112, 116, 120, 124
N_COLC = CONV_W * NC2

K_ID, K_TRI, K_NEG, K_CNT, K_IOTA = 0, 128, 256, 640, 1024
N_CONST = 1088


def constants():
    t = np.arange(P)[:, None]
    out = [np.eye(P), (np.arange(P)[:, None] <= np.arange(P)[None, :])]
    cnts = []
    for tile, keys in ((0, P), (1, 2 * P)):
        d = t + tile * P - np.arange(keys)[None, :]
        cnts.append(sum(((d >= 0) & (d % r == 0) & (d // r <= BACK)).astype(np.float32) for r in DILATIONS))
    cnt = np.concatenate(cnts, 1)
    iota = np.broadcast_to(np.arange(CAP), (P, CAP))
    return np.ascontiguousarray(np.concatenate(out + [np.where(cnt > 0, 0.0, NEG), cnt, iota], 1).astype(np.float32))


def pair_masks():
    j, i = np.arange(P)[:, None], np.arange(P)[None, :]
    out = [(j // (2 * s) == i // (2 * s)) & (j % (2 * s) < s) & (i % (2 * s) >= s) for s in LEVELS] + [j == i]
    return np.ascontiguousarray(np.concatenate(out, 1).astype(np.float32))


class Order:

    def __init__(self, phases):
        self.first, n = {}, 0
        for name, uses in phases:
            self.first[name] = n
            n += uses
        self.total = n

    def __getitem__(self, name):
        return self.first[name]


def attention_fills():
    order = []
    for h in range(HEADS + 2):
        if h < HEADS:
            order.append(("S", h))
        if h >= 2:
            order.append(("T", h - 2))
    return {step: i for i, step in enumerate(order)}


def two_blocks(nc, d, out):
    fills = [("params", 4)]
    slots, rows_d = [], []
    for l in range(DEPTH):
        fills += [(("norm", 3 * l), 4), (("ffn", 2 * l), NF), (("mod", 4 * l), 1), (("norm", 3 * l + 1), 4),
                  (("xbc", l), 8), (("dt", l), 1), (("z", l), 4), (("qkv", l), 12), (("mod", 4 * l + 1), 1),
                  (("acum", l), 1), (("xt", l), 4), (("bt", l), 1), (("qkt", l), 8), (("cb", l), 2),
                  (("bc", l), 8), (("state", l), 2), (("off", l), 2), (("att", l), 2 * HEADS),
                  (("yt", l), 8), (("mod", 4 * l + 2), 1), (("norm", 3 * l + 2), 4), (("ffn", 2 * l + 1), NF),
                  (("mod", 4 * l + 3), 1)]
        slots += [(("ffn", 2 * l), NF), (("win", l), 24), (("wout", l), 8), (("ffn", 2 * l + 1), NF)]
        rows_d += [(("ffn", 2 * l), NF), (("ffn", 2 * l + 1), NF)]
    U1 = 3 * DEPTH
    A1 = 5 * DEPTH
    fills += [(("norm", U1), 4), ("a1", 1), ("a2", 2), ("qk2", 4), ("v2", 4), ("pc", 4), ("r", 4), ("gates", 8),
              ("pairs", 2 * len(LEVELS) + 2), ("cross", 1), ("o", GH), ("osum", 2),
              ("mean", 1), ("var", 1), (("pwa", 0), 1), (("pwb", 0), 1), (("pwa", 1), 1), (("pwb", 1), 1), ("ygla", 4), ("garow", 2), (("norm", U1 + 1), 4), ("router", 1),
              ("rows", 10), ("count", 1), ("moe", 7 + EXPERTS // 2 * 16)]
    slots += [("win2", N_PROJ2), ("pw", 2), ("glao", 4), ("wout2", 4), ("moe", EXPERTS * CPE)]
    rows_d += [("moe", EXPERTS * CPE)]
    BLOCKS = ("xbc", "z", "qkv", "qk2", "v2", "pc", "r", "gates", "ygla", "pwb")
    FILL, RING, ROWD = Order(fills), Order(slots), Order(rows_d)
    AF = attention_fills()

    ctx = ExitStack()
    with ctx:
        def sb(name, shape, dt=F32):
            return ctx.enter_context(nc.sbuf_tensor(name, shape, dt))

        def sem(name):
            return ctx.enter_context(nc.semaphore(name))

        with nc.sbuf_tensor("ring", [P, SLOTS, SLOT], F32) as ring, \
                nc.sbuf_tensor("ring_d", [P, SLOTS, SLOT_D], F32) as ring_d, \
                nc.sbuf_tensor("arena", [P, ARENA], F32) as arena:
            pass
        ring_low = sb("ring_low", [P, SLOTS, SLOT], F32R)
        ring_d_low = sb("ring_d_low", [P, SLOTS, SLOT_D], F32R)
        low_at = [0]

        def beside(to):
            if to > low_at[0]:
                sb(f"pad{to}", [P, to - low_at[0]])
            low_at[0] = to

        def over(name, shape):
            low_at[0] += int(np.prod(shape))
            return sb(name, [P] + shape, F32R)

        A_HIGH = 2 * 2 * SEQ + NT * D
        A_HID = A_HIGH + NX * (SEQ + CONV_K - 1) + NX * SEQ + 3 * NT * D
        A_X = A_HIGH + NX * (SEQ + CONV_K - 1) + NX * SEQ + 4 * NT * D
        beside(2 * 2 * SEQ)
        ue = over("ue", [KD, 2, 2 * CAP])
        assert low_at[0] == A_HIGH
        high_b = over("high_b", [SLOTS, SLOT])
        high_r = over("high_r", [SLOTS, SLOT_D])
        A_OUT = low_at[0]
        beside(A_HID)
        hidh, hidl = over("hidh", [2, SEQ]), over("hidl", [2, SEQ])
        beside(A_X)
        xh, xl = over("xh", [KD, SEQ]), over("xl", [KD, SEQ])
        high_w = over("high_w", [2, SLOT])
        beside(ARENA)
        x = sb("x", [P, NT, D])
        xnT = sb("xnT", [P, KD, SEQ])
        konst = sb("konst", [P, N_CONST])
        ones = sb("ones", [P, P])
        cola = sb("cola", [P, 2, N_COLA])
        heads3 = sb("heads3", [P, 3, DEPTH, HEADS])
        wdt = sb("wdt", [P, DEPTH, KD, HEADS])
        colb = sb("colb", [P, P])
        colc = sb("colc", [P, N_COLC])
        wa1 = sb("wa1", [P, KD, RANK])
        wa2 = sb("wa2", [RANK, GH * DK])
        wr = sb("wr", [P, KD, N_GROUPS + EXPERTS])
        br = sb("br", [P, N_GROUPS + EXPERTS])
        mod = sb("mod", [P, PIECES, KD])
        gains = sb("gains", [P, 3, KD])
        cact = sb("cact", [P, KD])
        N_PARAMS = 1 + 3 + 1 + DEPTH * 8 + 12 + 1 + 1 + 1 + 2 + 2
        at = [0]

        def part(shape):
            n = int(np.prod(shape))
            v = arena[:, at[0]:at[0] + n]
            at[0] += n
            if len(shape) == 2:
                v = v.rearrange("p (a b) -> p a b", a=shape[0])
            elif len(shape) == 3:
                v = v.rearrange("p (a b c) -> p a b c", a=shape[0], b=shape[1])
            return v

        stat = sb("stat", [P, 64])
        ss, std, rstd = stat[:, 0:2], stat[:, 2:4], stat[:, 4:6]
        gate_s = part([2, SEQ])
        hid = part([2, SEQ])
        xsc = part([NT, D])
        yatt = xsc
        here = at[0]
        xraw = part([NX, SEQ + CONV_K - 1])
        after = at[0]
        at[0] = here
        xtok = part([NT, D])
        xdt = part([NT, D])
        at[0] = max(after, at[0])
        here = at[0]
        xc = part([NX, SEQ])
        after = at[0]
        at[0] = here
        xdec = part([D])
        prev = part([GROUPS, BLK])
        at[0] = after
        z = part([NT, D])
        here = at[0]
        qk = part([NT, 2 * D])
        v = part([NT, D])
        at[0] = here
        yT = part([2 * KD, SEQ])
        at[0] = here + 3 * NT * D
        assert at[0] == A_X
        qT = part([KD, SEQ])
        kT = part([KD, SEQ])
        btok = part([GROUPS, P])
        seg = part([2, HPG * P])
        cbm = part([2, GROUPS, P])
        sp3 = part([3, 3 * P])
        pT = part([2, 3 * P])
        small = part([768])
        sm = [0]

        def tiny(n):
            sm[0] += n
            return small[:, sm[0] - n:sm[0]]

        dr, dn, de, dl, dtv, ea, adt, nac, ex, dd, dec = (tiny(32) for _ in range(11))
        rq, rqs, rqr = tiny(64), tiny(64), tiny(64)
        gs, gss, gsr = tiny(8), tiny(8), tiny(8)
        mx, nmx, den, rden = tiny(32), tiny(32), tiny(32), tiny(32)
        w_ada = part([2, D])
        ada = part([D])
        assert at[0] <= ARENA, at[0]

        at[0] = 2 * 2 * SEQ + NT * D
        masks = part([len(LEVELS) + 1, P])
        q2k2 = part([2 * GH, SEQ])
        v2 = part([NT, D])
        pc = part([2 * NC2, SEQ])
        rT = part([KD, SEQ])
        gT = part([2 * KD, SEQ])
        a1T = part([SEQ])
        graw = part([GH, SEQ])
        bcum = part([GH, SEQ])
        here = at[0]
        lev_e = part([2, GH * SEQ])
        lev_qk = part([2, GH * SEQ])
        at[0] = here
        merged = part([KD, SEQ])
        at[0] = here + 4 * GH * SEQ
        attn = part([2 * GH, P])
        across = part([GH, P])
        oT = part([KD, SEQ])
        osq = part([KD, SEQ])
        zpad = part([NC2, SEQ + CONV_W - 1])
        zc = part([NC2, SEQ])
        zsq = part([NC2, SEQ])
        mean = part([SEQ])
        assert at[0] <= ARENA, at[0]
        rg = graw
        rgs = bcum
        onesr = lev_e
        diag = osq.rearrange("p a b -> p (a b)")[:, 0:D]
        garow = pc.rearrange("p a b -> p (a b)")[:, 0:D]
        at[0] = here + 4 * GH * SEQ + 2 * GH * P + GH * P + KD * SEQ
        y2 = part([NT, D])
        rowf = part([3, D])
        assert at[0] <= ARENA, at[0]
        at[0] = A_X + 2 * KD * SEQ
        routed = part([NT * D])
        rt = [0]

        def route(n, t=NT):
            rt[0] += t * n
            return routed[:, rt[0] - t * n:rt[0]].rearrange("p (t e) -> p t e", t=t)

        row2 = q2k2.rearrange("p a b -> p (a b)").rearrange("p (a b) -> p a b", a=2)
        EP = EXPERTS + 2
        comb, place = route(EP), route(EP)
        logit = route(N_GROUPS + EXPERTS)
        number = route(1)
        at[0] = A_X
        u2 = part([NT, D])
        sel = part([NT, 2 * CAP])
        both = part([2, 2, BLK])
        join = part([CAP])
        assert at[0] <= A_X + 2 * KD * SEQ
        at[0] = A_OUT
        out_e = part([D])
        selw = part([NT, 2 * CAP])
        selT = part([SEQ])
        assert at[0] <= A_HID
        gate_e = arena[:, 0:2 * SEQ]
        hid_e = arena[:, 2 * SEQ:4 * SEQ].rearrange("p (a b) -> p a b", a=CPE)
        heh, hel = (a[:, :, :].rearrange("p a b -> p (a b)").rearrange("p (a b) -> p a b", a=CPE)
                    for a in (hidh, hidl))
        flag = sb("flag", [P, 1], mybir.dt.int32)
        cand, mark1, mark2 = route(EXPERTS), route(EXPERTS), route(EXPERTS)
        rt_og, rt_gd, rt_ge, rt_pen = (route(N_GROUPS) for _ in range(4))
        rt_mg, rt_m1, rt_m2, rt_m, rt_r, rt_pd, rt_pe = (route(1) for _ in range(7))
        rank = route(EXPERTS, 1)[:, 0, :]
        rows = gT.rearrange("p a b -> p (a b)")[:, 0:4 * P].rearrange("p (a b) -> p a b", a=4)

        acc = ctx.enter_context(nc.psum_tensor("acc", [P, NT, D], F32))
        misc = ctx.enter_context(nc.psum_tensor("misc", [P, 4, 512], F32))
        ident = konst[:, K_ID:K_ID + P]
        tri = konst[:, K_TRI:K_TRI + P]

        params_in = sem("params_in")
        x_in = sem("x_in")
        loaded = [sem(f"loaded{s}") for s in range(SLOTS)]
        loaded_d = [sem(f"loaded_d{s}") for s in range(SLOTS)]
        freed_d = [sem(f"freed_d{s}") for s in range(SLOTS)]
        freed = [sem(f"freed{s}") for s in range(SLOTS)]
        filled = sem("filled")
        drained = [sem(f"drained{b}") for b in range(4)]
        acc_free = sem("acc_free")
        ones_set = sem("ones_set")
        var_ready = sem("var_ready")
        std_ready = sem("std_ready")
        xsc_ready = sem("xsc_ready")
        std_ready2 = sem("std_ready2")
        gate_ready = sem("gate_ready")
        conv_done = sem("conv_done")
        xc_ready = sem("xc_ready")
        z_ready = sem("z_ready")
        dn_ready = sem("dn_ready")
        dl_ready = sem("dl_ready")
        adt_ready = sem("adt_ready")
        nac_ready = sem("nac_ready")
        decay_ready = sem("decay_ready")
        sq_ready = sem("sq_ready")
        qk_ready = sem("qk_ready")
        seg_ready = sem("seg_ready")
        seg_exp = sem("seg_exp")
        mix_ready = sem("mix_ready")
        y_done = sem("y_done")
        xdt_ready = sem("xdt_ready")
        ysd_ready = sem("ysd_ready")
        smax_ready = sem("smax_ready")
        p_exp = sem("p_exp")
        p_ready = sem("p_ready")
        av_done = sem("av_done")
        yatt_ready = sem("yatt_ready")
        out_done = sem("out_done")
        masks_in = sem("masks_in")
        cact_ready = sem("cact_ready")
        ada_in = [sem("ada_in0"), sem("ada_in1")]
        ada_used = sem("ada_used")
        pool_step = sem("pool_step")
        ada_ready = sem("ada_ready")
        gl_ready = sem("gl_ready")
        gl_log = sem("gl_log")
        lev_ready = sem("lev_ready")
        lev_exp = sem("lev_exp")
        lev_qk_ready = sem("lev_qk_ready")
        o_sq = sem("o_sq")
        z_out = sem("z_out")
        pc_in = sem("pc_in")
        var2 = sem("var2")
        std2 = sem("std2")
        zn_ready = sem("zn_ready")
        zs_ready = sem("zs_ready")
        og_ready = sem("og_ready")
        merged_ready = sem("merged_ready")
        diag_ready = sem("diag_ready")
        rt_in = sem("rt_in")
        rt_exp = sem("rt_exp")
        y_final = sem("y_final")
        mask_ready = sem("mask_ready")
        flag_ready = sem("flag_ready")
        sel_ready = sem("sel_ready")
        selw_ready = sem("selw_ready")
        zero_ready = sem("zero_ready")
        high_in = [sem(f"high_in{s}") for s in range(SLOTS)]
        low_in = [sem(f"low_in{s}") for s in range(SLOTS)]
        high_in_d = [sem(f"high_in_d{s}") for s in range(SLOTS)]
        low_in_d = [sem(f"low_in_d{s}") for s in range(SLOTS)]
        hid_high = sem("hid_high")
        hid_low = sem("hid_low")
        xs_high = sem("xs_high")
        xs_low = sem("xs_low")
        xh_ready = sem("xh_ready")
        ue_high = sem("ue_high")
        y_ready = sem("y_ready")
        scattered = sem("scattered")
        dve_step = sem("dve_step")
        act_step = sem("act_step")

        def fill_count(m):
            return m + 1 - sum(min(max(m + 1 - FILL[k], 0), uses) for k, uses in fills
                               if (k[0] if isinstance(k, tuple) else k) in BLOCKS)

        def wait_filled(eng, m):
            eng.wait_ge(filled, fill_count(m))

        def wait_slot_read(eng, n0, i=0, j=0):
            n = n0 + j
            eng.wait_ge(freed[n % SLOTS], i + (n // SLOTS + 1))

        def wait_drained(eng, m0, i=0, j=0):
            m = m0 + j
            eng.wait_ge(drained[m % 4], i + (m // 4 + 1))

        def bank_of(m):
            return misc[:, m % 4, :]

        def wait_summed(eng, n0, i, j):
            n = n0 + j
            eng.wait_ge(freed_d[n % SLOTS], i + (n // SLOTS + 1))

        def block_part(n):
            return ring[:, n % SLOTS, :].rearrange("p (k f) -> p k f", k=KD)

        SPLIT = [(RING[k], uses) for k, uses in slots if k[0] == "ffn" or k == "moe"]
        SPLIT += [(RING["win", l] + 8, 16) for l in range(DEPTH)]

        def split_count(n):
            return sum(1 for n0, uses in SPLIT for u in range(n0, n0 + uses) if u <= n and u % SLOTS == n % SLOTS)

        def wait_split(eng, sems, n0, i=0, j=0):
            eng.wait_ge(sems[(n0 + j) % SLOTS], i + split_count(n0 + j))

        def wait_split_d(eng, sems, n0, i=0, j=0):
            eng.wait_ge(sems[(n0 + j) % SLOTS], i + ((n0 + j) // SLOTS + 1))

        def low_part(n):
            return ring_low[:, n % SLOTS, :].rearrange("p (k f) -> p k f", k=KD)

        def high_part(n):
            return high_b[:, n % SLOTS, :].rearrange("p (k f) -> p k f", k=KD)

        def pw_part(n):
            return ring[:, n % SLOTS, :].rearrange("p (k f) -> p k f", k=NC2)

        def pair_part(half, x):
            return block_part(RING["moe"] + 4 * half + x)

        def pair_rows(half, c):
            return ring_d[:, (ROWD["moe"] + c) % SLOTS, :]

        def pair_freed(half, x):
            return freed[(RING["moe"] + x) % SLOTS]

        def pair_freed_d(half, c):
            return freed_d[(ROWD["moe"] + c) % SLOTS]

        def wait_pair(eng, half, i, x):
            n = RING["moe"] + 4 * half + x
            eng.wait_ge(loaded[n % SLOTS], i * (2 * LOAD) + LOAD * (n // SLOTS + 1))

        def wait_pair_d(eng, half, i, c):
            n = ROWD["moe"] + 4 * half + c
            eng.wait_ge(loaded_d[n % SLOTS], i * (2 * LOAD) + LOAD * (n // SLOTS + 1))

        def wait_pair_read(eng, half, i, x):
            n = RING["moe"] + 4 * half + x
            eng.wait_ge(freed[n % SLOTS], i * 2 + (n // SLOTS + 1))

        def wait_pair_summed(eng, half, i, c):
            n = ROWD["moe"] + 4 * half + c
            eng.wait_ge(freed_d[n % SLOTS], i * 2 + (n // SLOTS + 1))

        def wait_pair_split(eng, sems, half, i, x):
            n = RING["moe"] + 4 * half + x
            eng.wait_ge(sems[n % SLOTS], i * 2 + split_count(n))

        def wait_pair_split_d(eng, sems, half, i, c):
            n = ROWD["moe"] + 4 * half + c
            eng.wait_ge(sems[n % SLOTS], i * 2 + (n // SLOTS + 1))

        M0 = FILL["moe"] + 7
        JOINED, OUT, TOKENS = (2, 11), (5, 14), (9, 10, 12, 13)
        FILLED0 = fill_count(FILL["moe"] - 1) + 4
        FILLS = 10
        F_JOINED, F_CHOICE, F_OUT, F_TOKENS = (1, 7), (2, 3), (4, 10), (5, 6, 8, 9)

        def wait_pair_drained(eng, i, j):
            eng.wait_ge(drained[(M0 + j) % 4], i * 4 + ((M0 + j) // 4 + 1))

        def wait_pair_filled(eng, i, k):
            eng.wait_ge(filled, i * FILLS + (FILLED0 + k))

        def high_w_part(n):
            return high_w[:, n % 2, :].rearrange("p (k f) -> p k f", k=KD)

        def rows_part(n):
            return ring[:, n % SLOTS, :].rearrange("p (a f) -> p a f", a=2)

        block = ctx.enter_context(nc.Block())

        @block.sync
        def _(sp):
            def claim(n0, i, j):
                n = n0 + j
                if n >= SLOTS or not isinstance(i, int):
                    sp.wait_ge(freed[n % SLOTS], i + n // SLOTS)

            def claim_d(n0, i, j):
                n = n0 + j
                if n >= SLOTS or not isinstance(i, int):
                    sp.wait_ge(freed_d[n % SLOTS], i + n // SLOTS)

            def load_pair(n0, i, q, gate, up, col):
                for g, w in enumerate((gate, up)):
                    load_block(n0, i, 2 * q + g, w, col)

            def load_down(n0, i, j, down, row):
                claim_d(n0, i, j)
                s = (n0 + j) % SLOTS
                sp.dma_start(ring_d[:, s, :], down[bass.ds(row, P), :]).then_inc(loaded_d[s], LOAD)

            def load_block(n0, i, j, w, col):
                claim(n0, i, j)
                n = n0 + j
                sp.dma_start(block_part(n), w[:, bass.ds(col, BLK)].rearrange("(k p) f -> p k f", p=P))\
                    .then_inc(loaded[n % SLOTS], LOAD)

            def load_rows(n0, i, j, w, r):
                claim(n0, i, j)
                n = n0 + j
                sp.dma_start(rows_part(n), w[bass.ds(r * 2 * P, 2 * P), :].rearrange("(a p) f -> p a f", p=P))\
                    .then_inc(loaded[n % SLOTS], LOAD)

            def ffn(f):
                l, which = divmod(f, 2)
                w = [d[f"ffn{which + 1}_w_{s}"][l] for s in ("gate", "up", "down")]
                n0, d0 = RING["ffn", f], ROWD["ffn", f]

                def four(n, dn, i, c):
                    for q in range(2):
                        load_pair(n, i, q, w[0], w[1], c * P + q * BLK)
                        for j in range(2 * q, 2 * q + 2):
                            load_down(dn, i, j, w[2], c * P + j * P)

                if not f:
                    four(n0, d0, 0, 0)
                with sp.Fori(0 if f else 1, NF // 4) as i:
                    four(n0, d0, i, i * 4)
                c = NF // 4 * 4
                load_pair(n0 + c, 0, 0, w[0], w[1], c * P)
                for j in range(2):
                    load_down(d0 + c, 0, j, w[2], (c + j) * P)

            for l in range(DEPTH):
                ffn(2 * l)
                n0 = RING["win", l]
                w_in = d["w_in"][l]
                with sp.Fori(0, 2) as i:
                    for j in range(4):
                        load_block(n0, i, j, w_in, (i * 4 + j) * BLK + D)
                for j in range(4):
                    load_block(n0 + 8 + j, 0, 0, w_in, j * BLK)
                with sp.Fori(0, 3) as i:
                    for j in range(4):
                        load_block(n0 + 12, i, j, w_in, (i * 4 + j) * BLK + (D + XBC + HEADS))
                n0 = RING["wout", l]
                with sp.Fori(0, 2) as i:
                    for j in range(4):
                        load_rows(n0, i, j, d["w_out"][l], i * 4 + j)
                ffn(2 * l + 1)
            w_in = d["w_in_2"][0]
            n0 = RING["win2"]
            for j in range(4):
                load_block(n0 + j, 0, 0, w_in, QK0 + j * BLK)
            for j in range(4):
                load_block(n0 + 4 + j, 0, 0, w_in, V0 + j * BLK)
            for j in range(4):
                load_block(n0 + 8 + j, 0, 0, w_in, j * BLK)
            for j in range(4):
                load_block(n0 + 12 + j, 0, 0, w_in, R0 + j * BLK)
            with sp.Fori(0, 2) as i:
                for j in range(4):
                    load_block(n0 + 16, i, j, w_in, (i * 4 + j) * BLK + G0)
            n0 = RING["pw"]
            for j in range(2):
                claim(n0 + j, 0, 0)
                sp.dma_start(pw_part(n0 + j), d["w_conv_pw_2"][0][:, j * 512:(j + 1) * 512]
                             .rearrange("(k p) f -> p k f", p=P)).then_inc(loaded[(n0 + j) % SLOTS], LOAD)
            for j in range(4):
                load_block(RING["glao"] + j, 0, 0, d["w_gla_o_2"][0], j * BLK)
            for j in range(4):
                load_rows(RING["wout2"] + j, 0, 0, d["w_out_2"][0], j)
            w1, w3 = (d[k][0].rearrange("e m f -> (e m) f") for k in ("w1_2", "w3_2"))
            w2 = d["w2_2"][0].rearrange("e f m -> (e f) m")

            with sp.Fori(0, EXPERTS) as e:
                for x in range(4):
                    w = w1 if x % 2 == 0 else w3
                    load_block(RING["moe"], e, x, w[bass.ds(e * D, D), :], x // 2 * BLK)
                for c in range(CPE):
                    load_down(ROWD["moe"], e, c, w2, e * D_EXPERT + c * P)
            sp.wait_ge(out_done, 16)

        @block.tensor
        def _(pe):
            def three(dst, wh, wl, mh, ml, start, stop, **kw):
                pe.matmul(dst, wh, ml, start=start, stop=False, **kw)
                pe.matmul(dst, wl, mh, start=False, stop=False, **kw)
                return pe.matmul(dst, wh, mh, start=False, stop=stop, **kw)

            def claim_bank(m0, i=0, j=0):
                m = m0 + j
                if m >= 4 or not isinstance(i, int):
                    pe.wait_ge(drained[m % 4], i + m // 4)
                return bank_of(m)

            def wait_slot(n0, i=0, j=0):
                n = n0 + j
                pe.wait_ge(loaded[n % SLOTS], i * LOAD + LOAD * (n // SLOTS + 1))

            def turn(m0, src, groups):
                for q in groups:
                    b = claim_bank(m0 + q)
                    for kk in range(2):
                        for t in range(NT):
                            k = 2 * q + kk
                            mm = pe.transpose(b[:, kk * SEQ + t * P:kk * SEQ + (t + 1) * P],
                                              src[:, t, k * P:(k + 1) * P], ident)
                    mm.then_inc(filled, 1)

            def norm(u):
                pe.wait_ge(xsc_ready, u + 1)
                turn(FILL["norm", u], xsc, range(4))
                for q in range(4):
                    wait_drained(pe, FILL["norm", u] + q)

            def gate_up(m0, n0, i, c):
                b = claim_bank(m0, i, c)
                for g in range(2):
                    n = n0 + c // 2 * 2 + g
                    if c % 2 == 0:
                        wait_split(pe, low_in, n, i)
                    cs = slice(c % 2 * P, (c % 2 + 1) * P)
                    for k in range(KD):
                        mm = three(b[:, g * SEQ:(g + 1) * SEQ], high_part(n)[:, k, cs], low_part(n)[:, k, cs],
                                   xh[:, k, :], xl[:, k, :], k == 0, k == KD - 1)
                mm.then_inc(filled, 1)

            def down(m0, n0, d0, g0, i, c, start, stop):
                pe.wait_ge(hid_low, i * 4 + (g0 + c + 1))
                dn = d0 + c
                wait_split_d(pe, low_in_d, d0, i, c)
                q = (m0 + c) % 2
                for t in range(NT):
                    ts = slice(t * P, (t + 1) * P)
                    for cc in range(2):
                        cs = slice(cc * 512, (cc + 1) * 512)
                        mm = three(acc[:, t, cs], hidh[:, q, ts], hidl[:, q, ts], high_r[:, dn % SLOTS, cs],
                                   ring_d_low[:, dn % SLOTS, cs], start, stop, skip_group_check=True)
                        if c % 2 == 0 and t == 0:
                            mm.then_inc(freed[(n0 + c + cc) % SLOTS], 1)
                mm.then_inc(freed_d[dn % SLOTS], 1)

            def ffn(f, a):
                m0, n0, d0 = FILL["ffn", f], RING["ffn", f], ROWD["ffn", f]
                gate_up(m0, n0, 0, 0)
                if a:
                    pe.wait_ge(acc_free, a)
                gate_up(m0, n0, 0, 1)
                down(m0, n0, d0, NF * f, 0, 0, True, False)
                with pe.Fori(0, (NF - 2) // 4) as i:
                    for j in range(4):
                        gate_up(m0, n0, i, j + 2)
                        down(m0, n0, d0, NF * f, i, j + 1, False, False)
                down(m0, n0, d0, NF * f, 0, NF - 1, False, True)

            def cols_out(m0, n0, i, j, src=xnT):
                wait_slot(n0, i, j)
                b = claim_bank(m0, i, j)
                w = block_part(n0 + j)
                for c in range(2):
                    for k in range(KD):
                        mm = pe.matmul(b[:, c * SEQ:(c + 1) * SEQ], w[:, k, c * P:(c + 1) * P], src[:, k, :],
                                       start=(k == 0), stop=(k == KD - 1))
                mm.then_inc(freed[(n0 + j) % SLOTS], 1)

            def toks_out(m0, n0, i, j):
                wait_slot(n0, i, j)
                b = claim_bank(m0, i, j)
                w = block_part(n0 + j)
                for t in range(NT):
                    for k in range(KD):
                        mm = pe.matmul(b[:, t * BLK:(t + 1) * BLK], xnT[:, k, t * P:(t + 1) * P], w[:, k, :],
                                       start=(k == 0), stop=(k == KD - 1))
                mm.then_inc(freed[(n0 + j) % SLOTS], 1)

            def toks_out3(m0, n0, i, j):
                wait_split(pe, low_in, n0, i, j)
                b = claim_bank(m0, i, j)
                for t in range(NT):
                    ts = slice(t * P, (t + 1) * P)
                    for k in range(KD):
                        mm = three(b[:, t * BLK:(t + 1) * BLK], xh[:, k, ts], xl[:, k, ts],
                                   high_w_part(n0 + j)[:, k, :], low_part(n0 + j)[:, k, :], k == 0, k == KD - 1)
                mm.then_inc(freed[(n0 + j) % SLOTS], 1)

            def w_in(l):
                n0 = RING["win", l]
                with pe.Fori(0, 2) as i:
                    for j in range(4):
                        cols_out(FILL["xbc", l], n0, i, j)
                b = claim_bank(FILL["dt", l])
                for t in range(NT):
                    for k in range(KD):
                        mm = pe.matmul(b[:, t * HEADS:(t + 1) * HEADS], xnT[:, k, t * P:(t + 1) * P],
                                       wdt[:, l, k, :], start=(k == 0), stop=(k == KD - 1))
                mm.then_inc(filled, 1)
                pe.wait_ge(xs_low, l + 1)
                for j in range(4):
                    toks_out3(FILL["z", l] + j, n0 + 8 + j, 0, 0)
                with pe.Fori(0, 3) as i:
                    for j in range(4):
                        toks_out3(FILL["qkv", l], n0 + 12, i, j)

            def ssd(l, a):
                pe.wait_ge(adt_ready, l + 1)
                b = claim_bank(FILL["acum", l])
                pe.matmul(b[:, 0:32], tri, adt, start=True, stop=True)
                pe.matmul(b[:, 32:48], ones[:, :], adt[:, 0:HEADS], start=True, stop=True).then_inc(filled, 1)
                pe.wait_ge(xc_ready, 4 * (l + 1))
                for q in range(4):
                    t, half = divmod(q, 2)
                    b = claim_bank(FILL["xt", l] + q)
                    for c in range(4):
                        mm = pe.transpose(b[:, c * P:(c + 1) * P], xc[:, half * 4 + c, t * P:(t + 1) * P], ident)
                    mm.then_inc(filled, 1)
                b = claim_bank(FILL["bt", l])
                for g in range(GROUPS):
                    mm = pe.transpose(b[:, g * P:(g + 1) * P], xc[:, 8 + g, 0:P], ident)
                mm.then_inc(filled, 1)
                pe.wait_ge(qk_ready, l + 1)
                turn(FILL["qkt", l], qk[:, :, 0:D], range(4))
                turn(FILL["qkt", l] + 4, qk[:, :, D:2 * D], range(4))
                for c in range(NT):
                    b = claim_bank(FILL["cb", l] + c)
                    for g in range(GROUPS):
                        mm = pe.matmul(b[:, g * P:(g + 1) * P], xc[:, 8 + g, c * P:(c + 1) * P],
                                       xc[:, 12 + g, c * P:(c + 1) * P], start=True, stop=True)
                    mm.then_inc(filled, 1)
                pe.wait_ge(xdt_ready, l + 1)
                pe.wait_ge(acc_free, a)

                def y_diag(s):
                    pe.wait_ge(mix_ready, 8 * l + s + 1)
                    c, g = divmod(s, GROUPS)
                    for r in range(HPG):
                        h = g * HPG + r
                        mm = pe.matmul(acc[:, c, h * HD:(h + 1) * HD], seg[:, s % 2, r * P:(r + 1) * P],
                                       xdt[:, c, h * HD:(h + 1) * HD], start=True, stop=True,
                                       skip_group_check=True)
                    mm.then_inc(y_done, 1)

                for s in range(8):
                    c, g = divmod(s, GROUPS)
                    b = claim_bank(FILL["bc", l] + s)
                    for r in range(HPG):
                        col = c * HEADS + g * HPG + r
                        mm = pe.matmul(b[:, r * P:(r + 1) * P], adt[:, col:col + 1].to_broadcast([P, P]), tri,
                                       start=True, stop=True)
                    mm.then_inc(filled, 1)
                    if s >= 1:
                        y_diag(s - 1)
                y_diag(7)
                for q in range(2):
                    b = claim_bank(FILL["state", l] + q)
                    for gg in range(2):
                        g = 2 * q + gg
                        mm = pe.matmul(b[:, gg * BLK:(gg + 1) * BLK], btok[:, g, :], xdec[:, g * BLK:(g + 1) * BLK],
                                       start=True, stop=True)
                    mm.then_inc(filled, 1)
                for q in range(2):
                    wait_drained(pe, FILL["state", l] + q)
                for q in range(2):
                    b = claim_bank(FILL["off", l] + q)
                    for gg in range(2):
                        g = 2 * q + gg
                        mm = pe.matmul(b[:, gg * BLK:(gg + 1) * BLK], xc[:, 12 + g, P:SEQ], prev[:, g, :],
                                       start=True, stop=True)
                    mm.then_inc(filled, 1)

            def attention(l, a):
                m0 = FILL["att", l]

                def scores(h):
                    rows64 = slice(h % 2 * HD, h % 2 * HD + HD)
                    b = claim_bank(m0 + AF["S", h])
                    pe.matmul(b[:, 0:P], qT[rows64, h // 2, 0:P], kT[rows64, h // 2, 0:P], start=True, stop=True)
                    pe.matmul(b[:, P:3 * P], qT[rows64, h // 2, P:SEQ], kT[rows64, h // 2, :],
                              start=True, stop=True).then_inc(filled, 1)

                def turn_weights(h):
                    pe.wait_ge(p_ready, HEADS * l + h + 1)
                    b = claim_bank(m0 + AF["T", h])
                    for c in range(3):
                        mm = pe.transpose(b[:, c * P:(c + 1) * P], sp3[:, h % 3, c * P:(c + 1) * P], ident)
                    mm.then_inc(filled, 1)

                def values(h):
                    wait_drained(pe, m0 + AF["T", h])
                    if h == 0:
                        pe.wait_ge(acc_free, a)
                    for t, c, key in ((0, 0, 0), (1, 1, 0), (1, 2, 1)):
                        mm = pe.matmul(acc[:, t, h * HD:(h + 1) * HD], pT[:, h % 2, c * P:(c + 1) * P],
                                       v[:, key, h * HD:(h + 1) * HD], start=(key == 0), stop=(key == t),
                                       skip_group_check=True)
                    mm.then_inc(av_done, 1)

                for q in range(8):
                    wait_drained(pe, FILL["qkt", l] + q)
                for h in range(HEADS + 3):
                    if h < HEADS:
                        scores(h)
                    if 2 <= h < HEADS + 2:
                        turn_weights(h - 2)
                    if h >= 3:
                        values(h - 3)

            def w_out(l, a):
                pe.wait_ge(ysd_ready, l + 1)
                turn(FILL["yt", l], xtok, range(4))
                pe.wait_ge(yatt_ready, l + 1)
                turn(FILL["yt", l] + 4, yatt, range(4))
                for q in range(8):
                    wait_drained(pe, FILL["yt", l] + q)
                pe.wait_ge(acc_free, a)
                n0 = RING["wout", l]
                for r in range(8):
                    wait_slot(n0 + r)
                    w = rows_part(n0 + r)
                    for kk in range(2):
                        k = 2 * r + kk
                        for t in range(NT):
                            for c in range(2):
                                mm = pe.matmul(acc[:, t, c * 512:(c + 1) * 512], yT[:, k, t * P:(t + 1) * P],
                                               w[:, kk, c * 512:(c + 1) * 512], start=(k == 0), stop=(k == 15),
                                               skip_group_check=True)
                    mm.then_inc(freed[(n0 + r) % SLOTS], 1)

            def modulation(p):
                pe.wait_ge(ada_ready, p + 1)
                b = claim_bank(FILL["mod", p])
                for k in range(KD):
                    mm = pe.matmul(b[:, k:k + 1], ada[:, k * P:(k + 1) * P], ones[:, 0:1], start=True, stop=True)
                mm.then_inc(filled, 1)

            def w_in2():
                n0 = RING["win2"]
                b = claim_bank(FILL["a1"])
                for k in range(KD):
                    mm = pe.matmul(b[0:RANK, 0:SEQ], wa1[:, k, :], xnT[:, k, :], start=(k == 0), stop=(k == KD - 1))
                mm.then_inc(filled, 1)
                for j in range(4):
                    cols_out(FILL["qk2"] + j, n0 + j, 0, 0)
                    if j == 0:
                        wait_drained(pe, FILL["a1"])
                        for q in range(2):
                            b = claim_bank(FILL["a2"] + q)
                            for hh in range(2):
                                h = 2 * q + hh
                                mm = pe.matmul(b[:, hh * SEQ:(hh + 1) * SEQ], wa2[:, h * DK:(h + 1) * DK],
                                               a1T[0:RANK, :], start=True, stop=True)
                            mm.then_inc(filled, 1)
                for j in range(4):
                    toks_out(FILL["v2"] + j, n0 + 4 + j, 0, 0)
                for j in range(4):
                    cols_out(FILL["pc"] + j, n0 + 8 + j, 0, 0)
                for j in range(4):
                    cols_out(FILL["r"] + j, n0 + 12 + j, 0, 0)
                with pe.Fori(0, 2) as i:
                    for j in range(4):
                        cols_out(FILL["gates"], n0 + 16, i, j)

            def gla():
                for s in range(len(LEVELS) + 1):
                    if s < len(LEVELS):
                        pe.wait_ge(lev_qk_ready, s + 1)
                    for t in range(NT):
                        b = claim_bank(FILL["pairs"] + 2 * s + t)
                        for h in range(GH):
                            if s < len(LEVELS):
                                keys = lev_qk[:, s % 2, h * SEQ + t * P:h * SEQ + (t + 1) * P]
                                queries = keys
                            else:
                                keys = q2k2[:, GH + h, t * P:(t + 1) * P]
                                queries = q2k2[:, h, t * P:(t + 1) * P]
                            mm = pe.matmul(b[:, h * P:(h + 1) * P], keys, queries, start=True, stop=True)
                        mm.then_inc(filled, 1)
                pe.wait_ge(lev_qk_ready, len(LEVELS) + 1)
                b = claim_bank(FILL["cross"])
                lq = lev_qk[:, len(LEVELS) % 2, :]
                for h in range(GH):
                    mm = pe.matmul(b[:, h * P:(h + 1) * P], lq[:, h * SEQ:h * SEQ + P],
                                   lq[:, h * SEQ + P:(h + 1) * SEQ], start=True, stop=True)
                mm.then_inc(filled, 1)
                for i in range(2 * len(LEVELS) + 2):
                    if i >= 2 * len(LEVELS) - 2:
                        wait_drained(pe, FILL["pairs"] + i)
                wait_drained(pe, FILL["cross"])
                for h in range(GH):
                    b = claim_bank(FILL["o"] + h)
                    for c in range(2):
                        ch = slice(h * DV + c * P, h * DV + (c + 1) * P)
                        pe.matmul(b[:, c * SEQ:c * SEQ + P], v2[:, 0, ch], attn[:, h, :], start=True, stop=True)
                        pe.matmul(b[:, c * SEQ + P:(c + 1) * SEQ], v2[:, 1, ch], attn[:, GH + h, :],
                                  start=True, stop=False)
                        mm = pe.matmul(b[:, c * SEQ + P:(c + 1) * SEQ], v2[:, 0, ch], across[:, h, :],
                                       start=False, stop=True)
                    mm.then_inc(filled, 1)
                pe.wait_ge(o_sq, 1)
                for q in range(2):
                    b = claim_bank(FILL["osum"] + q)
                    for hh in range(2):
                        for c in range(2):
                            mm = pe.matmul(b[:, hh * SEQ:(hh + 1) * SEQ], ones[:, :], osq[:, 2 * (2 * q + hh) + c, :],
                                           start=(c == 0), stop=(c == 1))
                    mm.then_inc(filled, 1)

            def conv_branch():
                for k, (name, src) in enumerate((("mean", zc), ("var", zsq))):
                    pe.wait_ge(z_out, k + 1)
                    b = claim_bank(FILL[name])
                    for c in range(NC2):
                        mm = pe.matmul(b[:, 0:SEQ], ones[:, :], src[:, c, :], start=(c == 0), stop=(c == NC2 - 1))
                    mm.then_inc(filled, 1)
                pe.wait_ge(zs_ready, 1)
                for j in range(2):
                    n = RING["pw"] + j
                    wait_slot(n)
                    w = pw_part(n)
                    for q in range(2):
                        b = claim_bank(FILL["pwa", 0] + 2 * j + q)
                        for c in range(2):
                            cc = (2 * q + c) * P
                            for k in range(NC2):
                                mm = pe.matmul(b[:, c * SEQ:(c + 1) * SEQ], w[:, k, cc:cc + P], zc[:, k, :],
                                               start=(k == 0), stop=(k == NC2 - 1))
                        mm.then_inc(freed[n % SLOTS] if q else filled, 1)
                pe.wait_ge(og_ready, 1)
                for j in range(4):
                    cols_out(FILL["ygla"] + j, RING["glao"] + j, 0, 0, src=oT)

            def row_fill(m0, which):
                pe.wait_ge(diag_ready, which)
                for q in range(2):
                    b = claim_bank(m0 + q)
                    mm = pe.matmul(b, ones[:, :], diag[:, q * 512:(q + 1) * 512], start=True, stop=True)
                    mm.then_inc(filled, 1)

            def w_out2():
                pe.wait_ge(merged_ready, 1)
                pe.wait_ge(acc_free, A1)
                for r in range(4):
                    n = RING["wout2"] + r
                    wait_slot(n)
                    w = rows_part(n)
                    for kk in range(2):
                        k = 2 * r + kk
                        for t in range(NT):
                            for c in range(2):
                                mm = pe.matmul(acc[:, t, c * 512:(c + 1) * 512], merged[:, k, t * P:(t + 1) * P],
                                               w[:, kk, c * 512:(c + 1) * 512], start=(k == 0), stop=(k == KD - 1),
                                               skip_group_check=True)
                    mm.then_inc(freed[n % SLOTS], 1)
                row_fill(FILL["garow"], 1)

            def router():
                b = claim_bank(FILL["router"])
                for t in range(NT):
                    for k in range(KD):
                        mm = pe.matmul(b[:, t * 36:(t + 1) * 36], xnT[:, k, t * P:(t + 1) * P], wr[:, k, :],
                                       start=(k == 0), stop=(k == KD - 1))
                mm.then_inc(filled, 1)

            def count():
                pe.wait_ge(mask_ready, 1)
                b = claim_bank(FILL["count"])
                pe.matmul(b[:, 0:EXPERTS], tri, mark1[:, 0, :], start=True, stop=True)
                pe.matmul(b[:, EXPERTS:2 * EXPERTS], tri, mark1[:, 1, :], start=True, stop=False)
                pe.matmul(b[:, EXPERTS:2 * EXPERTS], ones[:, :], mark1[:, 0, :], start=False, stop=True)
                pe.matmul(b[:, 2 * EXPERTS:3 * EXPERTS], ones[:, :], mark1[:, 0, :], start=True, stop=False)
                pe.matmul(b[:, 2 * EXPERTS:3 * EXPERTS], ones[:, :], mark1[:, 1, :], start=False, stop=True)\
                    .then_inc(filled, 1)

            def gathered_experts():
                def claim3(i, j):
                    wait_pair_drained(pe, i, j - 4)
                    return bank_of(M0 + j)

                def gather(i, groups, before=0):
                    for q in groups:
                        b = claim3(i, TOKENS[q] - before)
                        for kk in range(2):
                            k = 2 * q + kk
                            for t in range(NT):
                                mm = pe.matmul(b[:, kk * P:(kk + 1) * P], u2[:, t, k * P:(k + 1) * P], sel[:, t, :],
                                               start=(t == 0), stop=(t == NT - 1))
                        mm.then_inc(filled, 1)

                def gate_up_e(i, half, j):
                    for q in range(2):
                        b = claim3(i, j + q)
                        for g in range(2):
                            x = 2 * q + g
                            wait_pair_split(pe, low_in, half, i, x)
                            n = RING["moe"] + 4 * half + x
                            dst = b[:, g * BLK:(g + 1) * BLK]
                            for k in range(KD):
                                pe.matmul(dst, ue[:, k, half, :], high_part(n)[:, k, :], start=(k == 0), stop=False)
                                mm = pe.matmul(dst, ue[:, k, half, :], low_part(n)[:, k, :], start=False,
                                               stop=(k == KD - 1))
                            mm.then_inc(pair_freed(half, x), 1)

                def joined(i, half, j):
                    for q in range(2):
                        wait_pair_drained(pe, i, j + q)
                    b = claim3(i, JOINED[half])
                    for g in range(2):
                        for c in range(CPE):
                            at_ = (g * CPE + c) * CAP
                            mm = pe.matmul(b[:, at_:at_ + CAP], both[:, c // 2, g, c % 2 * P:(c % 2 + 1) * P], join,
                                           start=True, stop=True)
                    mm.then_inc(filled, 1)

                def down_e(i, half, j):
                    banks = [claim3(i, j + c) for c in range(2)]
                    for c in range(CPE):
                        wait_pair_split_d(pe, low_in_d, half, i, c)
                        s = (ROWD["moe"] + c) % SLOTS
                        for cc in range(2):
                            cs = slice(cc * 512, (cc + 1) * 512)
                            mm = three(banks[cc], heh[:, c, :], hel[:, c, :], high_r[:, s, cs], ring_d_low[:, s, cs],
                                       c == 0, c == CPE - 1)
                            if cc == 1:
                                mm.then_inc(pair_freed_d(half, c), 1)
                            elif c == CPE - 1:
                                mm.then_inc(filled, 1)

                def scatter(i, start, tokens=range(NT)):
                    for j in (-2, -1):
                        wait_pair_drained(pe, i, j)
                    for t in tokens:
                        for c in range(2):
                            mm = pe.matmul(acc[:, t, c * 512:(c + 1) * 512], selT[:, t * P:(t + 1) * P],
                                           out_e[:, c * 512:(c + 1) * 512], start=start, stop=True,
                                           skip_group_check=True)
                    return mm

                g0 = 2 * DEPTH * NF
                pe.wait_ge(sel_ready, 1)
                gather(0, range(4), 16)
                pe.wait_ge(acc_free, A1 + 1)
                pe.wait_ge(zero_ready, 4)
                scatter(0, True)
                with pe.Fori(0, EXPERTS // 2) as i:
                    for j in TOKENS:
                        wait_pair_drained(pe, i, j - 16)
                    gate_up_e(i, 0, 0)
                    scatter(i, False, [0])
                    joined(i, 0, 0)
                    scatter(i, False, [1])
                    pe.wait_ge(selw_ready, i + 1)
                    for t in range(NT):
                        pe.transpose(claim3(i, 3 + t)[:, 0:P], selw[:, t, :], ident).then_inc(filled, 1)
                    pe.wait_ge(hid_low, i * 2 + (g0 + 1))
                    down_e(i, 0, OUT[0])
                    gate_up_e(i, 1, 7)
                    pe.wait_ge(sel_ready, i + 2)
                    gather(i, range(0, 2))
                    joined(i, 1, 7)
                    gather(i, range(2, 4))
                    pe.wait_ge(hid_low, i * 2 + (g0 + 2))
                    down_e(i, 1, OUT[1])
                scatter(EXPERTS // 2, False).then_inc(scattered, 1)

            def experts():
                m0 = FILL["moe"]

                def gate_up8(i, c):
                    b = claim8(i, c)
                    half, turn_ = c // CPE % 2, i + c // 8
                    for g in range(2):
                        x = c % CPE // 2 * 2 + g
                        if c % 2 == 0:
                            wait_pair(pe, half, turn_, x)
                        w = pair_part(half, x)
                        for k in range(KD):
                            mm = pe.matmul(b[:, g * SEQ:(g + 1) * SEQ], w[:, k, c % 2 * P:(c % 2 + 1) * P],
                                           xnT[:, k, :], start=(k == 0), stop=(k == KD - 1))
                    mm.then_inc(filled, 1)

                def claim8(i, c):
                    m = m0 + c
                    pe.wait_ge(drained[m % 4], i * 2 + m // 4)
                    return bank_of(m)

                def down8(i, c):
                    m = m0 + c
                    pe.wait_ge(drained[m % 4], i * 2 + (m // 4 + 1))
                    half, cc = divmod(c, CPE)
                    wait_pair_d(pe, half, i, cc)
                    w = pair_rows(half, cc)
                    h = hid[:, m % 2, :]
                    for t in range(NT):
                        for q in range(2):
                            mm = pe.matmul(acc[:, t, q * 512:(q + 1) * 512], h[:, t * P:(t + 1) * P],
                                           w[:, q * 512:(q + 1) * 512], start=(cc == 0), stop=(cc == CPE - 1),
                                           skip_group_check=True)
                            if cc % 2 == 0 and t == 0:
                                mm.then_inc(pair_freed(half, cc + q), 1)
                    mm.then_inc(pair_freed_d(half, cc), 1)

                def two_experts(i, last):
                    for c in range(2 * CPE):
                        if not (last and c == 2 * CPE - 1):
                            gate_up8(i, c + 1)
                        if c % CPE == 0:
                            pe.wait_ge(acc_free, i * 2 + (A1 + 1 + c // CPE))
                        down8(i, c)

                gate_up8(0, 0)
                with pe.Fori(0, EXPERTS // 2 - 1) as i:
                    two_experts(i, False)
                two_experts(EXPERTS // 2 - 1, True)

            pe.wait_ge(params_in, N_PARAMS * 16)
            for i, n in enumerate((N_COLA, N_COLA, P, N_COLC)):
                pe.transpose(bank_of(i)[:, 0:n], rows[0:n, i, :], ident[0:n, 0:n]).then_inc(filled, 1)
            pe.wait_ge(ones_set, 1)
            for l in range(DEPTH):
                norm(3 * l)
                ffn(2 * l, 5 * l)
                modulation(4 * l)
                norm(3 * l + 1)
                w_in(l)
                modulation(4 * l + 1)
                ssd(l, 5 * l + 1)
                attention(l, 5 * l + 2)
                w_out(l, 5 * l + 3)
                modulation(4 * l + 2)
                norm(3 * l + 2)
                ffn(2 * l + 1, 5 * l + 4)
                modulation(4 * l + 3)
            norm(U1)
            w_in2()
            gla()
            conv_branch()
            w_out2()
            norm(U1 + 1)
            router()
            for i in range(5):
                row_fill(FILL["rows"] + 2 * i, i + 2)
            count()
            pe.wait_ge(flag_ready, 1)
            few = pe.value_load(flag[0:1, 0:1], min_val=0, max_val=1)
            with pe.If(few > 0):
                gathered_experts()
            with pe.Else():
                experts()

        @block.gpsimd
        def _(pool):
            def load(p, k):
                w, col = (d["w_ada_2"][0], p * D) if p < 6 else (d["w_ada_f_2"], (p - 6) * D)
                pool.dma_start(w_ada[:, k % 2, :], w[k * P:(k + 1) * P, col:col + D]).then_inc(ada_in[k % 2], 16)

            pool.wait_ge(cact_ready, 1)
            load(0, 0)
            load(0, 1)
            for p in range(PIECES):
                for k in range(KD):
                    u = p * KD + k
                    pool.wait_ge(ada_in[k % 2], 16 * (u // 2 + 1))
                    row = w_ada[:, k % 2, :]
                    if k == 0:
                        if p:
                            pool.wait_ge(filled, fill_count(FILL["mod", p - 1]))
                        pool.tensor_scalar(ada, row, cact[:, 0:1], None, ALU.mult).then_inc(ada_used, 1)
                        pool.wait_ge(ada_used, u + 1)
                    else:
                        pool.tensor_scalar(row, row, cact[:, k:k + 1], None, ALU.mult).then_inc(pool_step, 1)
                        pool.wait_ge(pool_step, p * (KD - 1) + k)
                        pool.tensor_tensor(ada, ada, row, ALU.add).then_inc(ada_used, 1)
                        pool.wait_ge(ada_used, u + 1)
                    if u + 2 < PIECES * KD:
                        load((u + 2) // KD, (u + 2) % KD)
                pool.nop().then_inc(ada_ready, 1)

        @block.scalar
        def _(act):
            n = [0]

            def step(ins):
                n[0] += 1
                ins.then_inc(act_step, 1)
                return n[0]

            def line(src):
                return src.rearrange("(k p) -> k p", p=P)

            act.dma_start(x[:, :, :], d["x"][0].rearrange("(t p) e -> p t e", p=P)).then_inc(x_in, 16)
            act.dma_start(konst[:, :], d["consts"]).then_inc(params_in, 16)
            for i, name in enumerate(("dt_bias", "a_log", "d_skip")):
                act.dma_start(heads3[:, i, :, :], d[name].partition_broadcast(P)).then_inc(params_in, 16)
            act.dma_start(wdt[:, :, :, :].rearrange("p l k h -> p (l k) h"),
                          d["w_in"][:, :, D + XBC:D + XBC + HEADS].rearrange("l (k p) h -> p (l k) h", p=P)).then_inc(params_in, 16)
            for l in range(DEPTH):
                for col, src in ((C_FFN1, line(d["ffn1_norm"][l])), (C_MIX, line(d["mix_norm"][l])),
                                 (C_FFN2, line(d["ffn2_norm"][l])),
                                 (C_CW, d["conv_w"][l].rearrange("k (c p) -> (k c) p", p=P)),
                                 (C_CB, line(d["conv_b"][l])), (C_SSD, line(d["ssd_norm"][l]))):
                    k = src.shape[0]
                    act.dma_start(rows[col:col + k, l, :], src).then_inc(params_in, 16)
                for col, name in ((C_QN, "q_norm"), (C_KN, "k_norm")):
                    src = d[name][l:l + 1, :].unsqueeze(1).to_broadcast([1, 2, HD])
                    act.dma_start(rows[col:col + 1, l, :].rearrange("a (b c) -> a b c", b=2), src).then_inc(params_in, 16)
            for col, src in ((B_ADA, d["b_ada_2"][0]), (B_ADA + 48, d["b_ada_f_2"]), (B_C, d["c_2"][0]),
                             (B_N1, d["g_norm1_2"][0]), (B_N2, d["g_norm2_2"][0]), (B_NF, d["g_final_2"]),
                             (B_PW, d["b_conv_pw_2"][0]), (B_GLA, d["g_gla_norm_2"][0]), (B_DW, d["b_dw_2"][0]),
                             (B_LG, d["g_conv_ln_2"][0]), (B_LB, d["b_conv_ln_2"][0]), (B_A2, d["b_a2_2"][0])):
                src = line(src)
                act.dma_start(rows[col:col + src.shape[0], 2, :], src).then_inc(params_in, 16)
            act.dma_start(rows[0:N_COLC, 3, :], d["w_dw_2"][0, :, 0, :].rearrange("k (c p) -> (k c) p", p=P))\
                .then_inc(params_in, 16)
            act.dma_start(wa1[:, :, :], d["w_in_2"][0, :, A0:A0 + RANK].rearrange("(k p) r -> p k r", p=P))\
                .then_inc(params_in, 16)
            act.dma_start(wa2[:, :], d["w_a2_2"][0]).then_inc(params_in, 16)
            for a, b, name in ((0, N_GROUPS, "g"), (N_GROUPS, N_GROUPS + EXPERTS, "e")):
                act.dma_start(wr[:, :, a:b], d[f"w_router_{name}_2"][0].rearrange("(k p) r -> p k r", p=P))\
                    .then_inc(params_in, 16)
                act.dma_start(br[:, a:b], d[f"b_router_{name}_2"][0].partition_broadcast(P)).then_inc(params_in, 16)
            wait_drained(act, 2)
            act.activation(cact[:, :], colb[:, B_C:B_C + KD], ACT.Silu).then_inc(cact_ready, 1)

            def norm(u, gain, dst=xnT, shift=None):
                act.wait_ge(var_ready, u + 1)
                act.activation(std, ss, ACT.Sqrt).then_inc(std_ready, 1)
                if gain:
                    turned(FILL["norm", u], (0, 2), dst, 0, gain, shift)

            def norm_high(u, gain):
                act.wait_ge(var_ready, u + 1)
                act.activation(std, ss, ACT.Sqrt).then_inc(std_ready, 1)
                for q in range(4):
                    wait_filled(act, FILL["norm", u] + q)
                    b = bank_of(FILL["norm", u] + q)
                    for kk in range(2):
                        k = 2 * q + kk
                        ins = act.mul(xh[:, k, :], b[:, kk * SEQ:(kk + 1) * SEQ], gain(k))
                    ins.then_inc(xh_ready, 1)

            def high_block(n0, i, j):
                s = (n0 + j) % SLOTS
                act.wait_ge(loaded[s], i * LOAD + LOAD * ((n0 + j) // SLOTS + 1))
                act.activation(high_b[:, s, :], ring[:, s, :], ACT.Copy).then_inc(high_in[s], 1)

            def high_rows(d0, i, c):
                s = (d0 + c) % SLOTS
                act.wait_ge(loaded_d[s], i * LOAD + LOAD * ((d0 + c) // SLOTS + 1))
                act.activation(high_r[:, s, :], ring_d[:, s, :], ACT.Copy).then_inc(high_in_d[s], 1)

            def turned(m0, groups, dst, first, gain, shift=None):
                for q in groups:
                    wait_filled(act, m0 + q)
                    b = bank_of(m0 + q)
                    for kk in range(2):
                        k = 2 * q + kk
                        src = b[:, kk * SEQ:(kk + 1) * SEQ]
                        if shift:
                            ins = act.activation(dst[:, first + k, :], src, ACT.Identity, scale=gain(k), bias=shift(k))
                        else:
                            ins = act.mul(dst[:, first + k, :], src, gain(k))
                    ins.then_inc(drained[(m0 + q) % 4], 1)

            def gate(m0, i, j):
                act.wait_ge(filled, i * 4 + fill_count(m0 + j))
                act.activation(gate_s[:, (m0 + j) % 2, :], bank_of(m0 + j)[:, 0:SEQ], ACT.Silu).then_inc(gate_ready, 1)

            def ffn(f):
                m0, n0, d0 = FILL["ffn", f], RING["ffn", f], ROWD["ffn", f]

                def four(i, a, last):
                    for j in range(a, a + 4):
                        wait_drained(act, m0, i, j - 2)
                        gate(m0, i, j)
                        high_rows(d0, i, j)
                        if j % 2 == 0 and not (last and j == a + 2):
                            for g in range(2):
                                high_block(n0, i, j + 2 + g)

                for c in range(2):
                    if c or f:
                        act.wait_ge(drained[(m0 + c - 2) % 4], (m0 + c - 2) // 4 + 1)
                    gate(m0 + c, 0, 0)
                    high_rows(d0, 0, c)
                    if c == 0:
                        for g in range(2):
                            high_block(n0, 0, 2 + g)
                with act.Fori(0, (NF - 2) // 4 - 1) as i:
                    four(i, 2, False)
                four(0, NF - 4, True)

            def w_in(l):
                n0 = RING["win", l]
                for q in range(4):
                    wait_drained(act, FILL["norm", 3 * l + 1] + q)
                act.activation(xh[:, :, :], xnT[:, :, :], ACT.Copy).then_inc(xs_high, 1)

                def xbc_out(j):
                    m = FILL["xbc", l] + j
                    wait_slot_read(act, n0 + j)
                    act.activation(xraw[:, 2 * j:2 * j + 2, CONV_K - 1:], bank_of(m).rearrange("p (a b) -> p a b", a=2), ACT.Copy)\
                        .then_inc(drained[m % 4], 1)

                def high_w_block(i, j, first=False):
                    n = n0 + 8 + j
                    if not first:
                        wait_slot_read(act, n - 2, i)
                    act.wait_ge(loaded[n % SLOTS], i * LOAD + LOAD * (n // SLOTS + 1))
                    act.activation(high_w[:, n % 2, :], ring[:, n % SLOTS, :], ACT.Copy).then_inc(high_in[n % SLOTS], 1)

                for j in range(8):
                    xbc_out(j)
                    if j in (5, 6):
                        high_w_block(0, j - 5, first=True)
                act.wait_ge(dn_ready, l + 1)
                s = step(act.activation(de, dn, ACT.Exp))
                act.activation(ea[:, 0:HEADS], heads3[:, 1, l, :], ACT.Exp)
                act.wait_ge(act_step, s)
                act.activation(dl, de, ACT.Ln, bias=1.0).then_inc(dl_ready, 1)
                for j in range(4):
                    m = FILL["z", l] + j
                    high_w_block(0, j + 2)
                    wait_slot_read(act, n0 + 8 + j)
                    act.activation(z[:, :, j * BLK:(j + 1) * BLK], bank_of(m).rearrange("p (a b) -> p a b", a=2),
                                   ACT.Silu).then_inc(drained[m % 4], 1)
                for q in range(4):
                    act.wait_ge(conv_done, NX * l + 4 * (q + 1))
                    act.activation(xc[:, 4 * q:4 * q + 4, :], xc[:, 4 * q:4 * q + 4, :], ACT.Silu).then_inc(xc_ready, 1)
                with act.Fori(0, 2) as i:
                    for j in range(4):
                        m = FILL["qkv", l] + j
                        high_w_block(i, j + 6)
                        wait_slot_read(act, n0 + 12, i, j)
                        act.activation(qk[:, :, bass.ds(i * D + j * BLK, BLK)],
                                       bank_of(m).rearrange("p (a b) -> p a b", a=2), ACT.Copy)\
                            .then_inc(drained[m % 4], 1)
                for j in range(4):
                    m = FILL["qkv", l] + 8 + j
                    if j < 2:
                        high_w_block(0, j + 14)
                    wait_slot_read(act, n0 + 20 + j)
                    act.activation(v[:, :, j * BLK:(j + 1) * BLK], bank_of(m).rearrange("p (a b) -> p a b", a=2),
                                   ACT.Copy).then_inc(drained[m % 4], 1)

            def ssd(l):
                act.wait_ge(sq_ready, 2 * l + 1)
                act.activation(rqs, rq, ACT.Sqrt).then_inc(std_ready2, 1)
                act.wait_ge(nac_ready, l + 1)
                act.activation(dec[:, 0:HEADS], dd[:, 0:HEADS], ACT.Exp)
                act.activation(ex, nac, ACT.Exp, scale=-1.0).then_inc(decay_ready, 1)
                for q in range(4):
                    t, half = divmod(q, 2)
                    m = FILL["xt", l] + q
                    wait_filled(act, m)
                    act.activation(xtok[:, t, half * 512:(half + 1) * 512], bank_of(m), ACT.Copy)\
                        .then_inc(drained[m % 4], 1)
                m = FILL["bt", l]
                wait_filled(act, m)
                act.activation(btok.rearrange("p a b -> p (a b)"), bank_of(m), ACT.Copy).then_inc(drained[m % 4], 1)
                for part_, dst, col in ((0, qT, C_QN), (1, kT, C_KN)):
                    for q in (0, 2):
                        m = FILL["qkt", l] + 4 * part_ + q
                        wait_filled(act, m)
                        act.mul(dst[:, 2 * q:2 * q + 2, :], bank_of(m).rearrange("p (a b) -> p a b", a=2),
                                cola[:, l, col:col + 1]).then_inc(drained[m % 4], 1)
                for s in range(8):
                    act.wait_ge(seg_ready, 8 * l + s + 1)
                    act.activation(seg[:, s % 2, :], seg[:, s % 2, :], ACT.Exp).then_inc(seg_exp, 1)
                for q in range(2):
                    m = FILL["state", l] + q
                    wait_filled(act, m)
                    act.activation(prev[:, 2 * q:2 * q + 2, :], bank_of(m).rearrange("p (a b) -> p a b", a=2),
                                   ACT.Copy).then_inc(drained[m % 4], 1)
                act.wait_ge(sq_ready, 2 * l + 2)
                act.activation(gss, gs, ACT.Sqrt).then_inc(std_ready2, 1)

            def attention(l):
                m0 = FILL["att", l]
                scale = HD ** -0.5
                for h in range(HEADS + 2):
                    if h < HEADS:
                        act.wait_ge(smax_ready, HEADS * l + h + 1)
                        act.activation(sp3[:, h % 3, 0:P], sp3[:, h % 3, 0:P], ACT.Exp,
                                       bias=nmx[:, 2 * h:2 * h + 1], scale=scale)
                        act.activation(sp3[:, h % 3, P:3 * P], sp3[:, h % 3, P:3 * P], ACT.Exp,
                                       bias=nmx[:, 2 * h + 1:2 * h + 2], scale=scale).then_inc(p_exp, 1)
                    if h >= 2:
                        hh = h - 2
                        m = m0 + AF["T", hh]
                        wait_filled(act, m)
                        if hh >= 2:
                            act.wait_ge(av_done, HEADS * l + hh - 1)
                        act.activation(pT[:, hh % 2, :], bank_of(m)[:, 0:3 * P], ACT.Copy).then_inc(drained[m % 4], 1)

            def evac(m, n, dst, src_n, func=ACT.Copy, scale=1.0):
                wait_slot_read(act, n)
                act.activation(dst, bank_of(m).rearrange("p (a b) -> p a b", a=2), func, scale=scale)\
                    .then_inc(drained[m % 4], 1)

            def decay_exp(s):
                act.wait_ge(lev_ready, s + 1)
                act.activation(lev_e[:, s % 2, :], lev_e[:, s % 2, :], ACT.Exp, scale=1.0 / TAU).then_inc(lev_exp, 1)

            def w_in2():
                m, n0 = FILL["a1"], RING["win2"]
                wait_filled(act, m)
                act.activation(a1T[0:RANK, :], bank_of(m)[0:RANK, 0:SEQ], ACT.Copy).then_inc(drained[m % 4], 1)
                for j in range(4):
                    evac(FILL["qk2"] + j, n0 + j, q2k2[:, 2 * j:2 * j + 2, :], 2,
                         scale=DK ** -0.5 if j < 2 else 1.0)
                for j in range(4):
                    evac(FILL["v2"] + j, n0 + 4 + j, v2[:, :, j * BLK:(j + 1) * BLK], 2)
                    if j == 0:
                        act.wait_ge(gl_ready, 1)
                        s = step(act.activation(lev_e[:, 0, :], lev_e[:, 0, :], ACT.Exp))
                        act.wait_ge(act_step, s)
                        act.activation(lev_e[:, 0, :], lev_e[:, 0, :], ACT.Ln, bias=1.0).then_inc(gl_log, 1)
                for s in range(2):
                    decay_exp(s)
                for j in range(4):
                    evac(FILL["pc"] + j, n0 + 8 + j, pc[:, 2 * j:2 * j + 2, :], 2,
                         ACT.Copy if j < 2 else ACT.Sigmoid)
                for j in range(4):
                    evac(FILL["r"] + j, n0 + 12 + j, rT[:, 2 * j:2 * j + 2, :], 2, ACT.Silu)
                with act.Fori(0, 2) as i:
                    for j in range(4):
                        m = FILL["gates"] + j
                        wait_slot_read(act, n0 + 16, i, j)
                        act.activation(gT[:, bass.ds(i * 8 + 2 * j, 2), :],
                                       bank_of(m).rearrange("p (a b) -> p a b", a=2), ACT.Sigmoid)\
                            .then_inc(drained[m % 4], 1)

            def gla():
                for s in range(2, len(LEVELS) + 1):
                    decay_exp(s)
                for h in range(GH):
                    m = FILL["o"] + h
                    wait_filled(act, m)
                    act.activation(oT[:, 2 * h:2 * h + 2, :], bank_of(m).rearrange("p (a b) -> p a b", a=2),
                                   ACT.Copy).then_inc(drained[m % 4], 1)
                act.wait_ge(var2, 1)
                act.activation(rgs, rg, ACT.Sqrt).then_inc(std2, 1)

            def conv_branch():
                act.wait_ge(var2, 2)
                act.activation(mean, mean, ACT.Sqrt).then_inc(std2, 1)
                act.wait_ge(zn_ready, 1)
                for c in range(NC2):
                    ins = act.activation(zc[:, c, :], zc[:, c, :], ACT.Silu, scale=colb[:, B_LG + c:B_LG + c + 1],
                                         bias=colb[:, B_LB + c:B_LB + c + 1])
                ins.then_inc(zs_ready, 1)

            def gathered_experts():
                def high(i, half, x):
                    n = RING["moe"] + 4 * half + x
                    s = n % SLOTS
                    wait_pair(act, half, i, x)
                    act.activation(high_b[:, s, :], ring[:, s, :], ACT.Copy).then_inc(high_in[s], 1)

                def high_d(i, half, c):
                    s = (ROWD["moe"] + c) % SLOTS
                    wait_pair_d(act, half, i, c)
                    act.activation(high_r[:, s, :], ring_d[:, s, :], ACT.Copy).then_inc(high_in_d[s], 1)

                def copy3(i, j, dst, src):
                    act.activation(dst, src, ACT.Copy).then_inc(drained[(M0 + j) % 4], 1)

                def gate3(i, half):
                    wait_pair_filled(act, i, F_JOINED[half])
                    act.activation(gate_e[:, half * BLK:(half + 1) * BLK], bank_of(M0 + JOINED[half])[:, 0:BLK],
                                   ACT.Silu).then_inc(gate_ready, 1)

                def products(i, half, j):
                    wait_pair_read(act, half, i, 3)
                    copy3(i, j + 1, both[:, 1, :, :].rearrange("p a b -> p (a b)"), bank_of(M0 + j + 1))

                def outs3(i, half):
                    rows_ = slice(half * CAP, (half + 1) * CAP)
                    for c in range(2):
                        if c == 0:
                            wait_pair_filled(act, i, F_OUT[half])
                        else:
                            wait_pair_summed(act, half, i, CPE - 1)
                        j = OUT[half] + c
                        copy3(i, j, out_e[rows_, c * 512:(c + 1) * 512], bank_of(M0 + j)[rows_, :])

                def tokens(i, groups, turn_=0):
                    for q in groups:
                        wait_pair_filled(act, i, F_TOKENS[q] if turn_ == 0 else q - 3)
                        act.activation(ue[:, 2 * q:2 * q + 2, :, 0:CAP],
                                       bank_of(M0 + TOKENS[q])[:, 0:2 * P].rearrange("p (a b c) -> p a b c", a=2, b=2),
                                       ACT.Copy).then_inc(ue_high, 1)

                def first_weights(i, part_):
                    for x in range(2 * part_, 2 * part_ + 2):
                        high(i, 0, x)
                    if part_:
                        for c in range(CPE):
                            high_d(i, 0, c)
                        products(i, 0, 0)

                def pair(i, last):
                    gate3(i, 0)
                    for x in range(2):
                        high(i, 1, x)
                    for t in range(NT):
                        wait_pair_filled(act, i, F_CHOICE[t])
                        copy3(i, 3 + t, selT[:, t * P:(t + 1) * P], bank_of(M0 + 3 + t)[:, 0:P])
                    for x in range(2, 4):
                        high(i, 1, x)
                    outs3(i, 0)
                    for c in range(CPE):
                        high_d(i, 1, c)
                    products(i, 1, 7)
                    tokens(i, range(2))
                    gate3(i, 1)
                    tokens(i, range(2, 4))
                    if not last:
                        first_weights(i + 1, 0)
                    outs3(i, 1)
                    if not last:
                        first_weights(i + 1, 1)

                tokens(0, range(4), -1)
                first_weights(0, 0)
                first_weights(0, 1)
                with act.Fori(0, EXPERTS // 2 - 1) as i:
                    pair(i, False)
                pair(EXPERTS // 2 - 1, True)

            def experts():
                m0 = FILL["moe"]
                for c in range(CPE):
                    wait_drained(act, m0 + c - 2)
                    gate(m0 + c, 0, 0)
                with act.Fori(0, EXPERTS - 1) as e:
                    for j in range(CPE):
                        wait_drained(act, m0 + 2, e, j)
                        gate(m0 + 4, e, j)

            for l in range(DEPTH):
                for g in range(2):
                    high_block(RING["ffn", 2 * l], 0, g)
                norm_high(3 * l, lambda k: cola[:, l, C_FFN1 + k:C_FFN1 + k + 1])
                ffn(2 * l)
                norm(3 * l + 1, lambda k: cola[:, l, C_MIX + k:C_MIX + k + 1])
                w_in(l)
                ssd(l)
                attention(l)
                turned(FILL["yt", l], (0, 2), yT, 0, lambda k: cola[:, l, C_SSD + k:C_SSD + k + 1])
                turned(FILL["yt", l] + 4, (0, 2), yT, KD, lambda k: 1.0)
                for g in range(2):
                    high_block(RING["ffn", 2 * l + 1], 0, g)
                norm_high(3 * l + 2, lambda k: cola[:, l, C_FFN2 + k:C_FFN2 + k + 1])
                ffn(2 * l + 1)
            wait_summed(act, ROWD["ffn", 2 * DEPTH - 1], 0, NF - 1)
            act.dma_start(masks.rearrange("p a b -> p (a b)"), d["masks"]).then_inc(masks_in, 16)
            norm(U1, lambda k: gains[:, 0, k:k + 1], shift=lambda k: mod[:, SH1, k:k + 1])
            w_in2()
            gla()
            conv_branch()
            for q in range(2):
                m = FILL["garow"] + q
                wait_filled(act, m)
                act.activation(garow[:, q * 512:(q + 1) * 512], bank_of(m), ACT.Copy).then_inc(drained[m % 4], 1)
            norm(U1 + 1, lambda k: gains[:, 1, k:k + 1], shift=lambda k: mod[:, SH2, k:k + 1])
            act.wait_ge(rt_in, 1)
            act.activation(rt_ge, rt_gd, ACT.Exp)
            act.activation(rt_pe, rt_pd, ACT.Exp).then_inc(rt_exp, 1)
            act.wait_ge(flag_ready, 1)
            few = act.value_load(flag[0:1, 0:1], min_val=0, max_val=1)
            with act.If(few > 0):
                gathered_experts()
            with act.Else():
                experts()
            norm(U1 + 2, None)
            act.wait_ge(y_final, 1)
            act.dma_start(out[0].rearrange("(t p) e -> p t e", p=P), x[:, :, :]).then_inc(out_done, 16)
            act.wait_ge(out_done, 16)

        @block.vector
        def _(dve):
            n = [0]

            def step(ins):
                n[0] += 1
                ins.then_inc(dve_step, 1)
                return n[0]

            def after_step(s):
                dve.wait_ge(dve_step, s)

            def link(ins):
                after_step(step(ins))

            def turned(m0, groups, dst, first, gain, shift=None):
                for q in groups:
                    wait_filled(dve, m0 + q)
                    b = bank_of(m0 + q)
                    for kk in range(2):
                        k = 2 * q + kk
                        src = b[:, kk * SEQ:(kk + 1) * SEQ]
                        if shift:
                            ins = dve.tensor_scalar(dst[:, first + k, :], src, gain(k), shift(k), ALU.mult, ALU.add)
                        else:
                            ins = dve.tensor_scalar(dst[:, first + k, :], src, gain(k), None, ALU.mult)
                    ins.then_inc(drained[(m0 + q) % 4], 1)

            def norm(u, gain, shift=None):
                for t in range(NT):
                    s = step(dve.tensor_tensor_reduce(xsc[:, t, :], x[:, t, :], x[:, t, :], 1.0, 0.0,
                                                      ALU.mult, ALU.add, ss[:, t:t + 1]))
                after_step(s)
                dve.tensor_scalar(ss, ss, 1.0 / D, EPS, ALU.mult, ALU.add).then_inc(var_ready, 1)
                dve.wait_ge(std_ready, u + 1)
                link(dve.reciprocal(rstd, std))
                for t in range(NT):
                    ins = dve.tensor_scalar(xsc[:, t, :], x[:, t, :], rstd[:, t:t + 1], None, ALU.mult)
                ins.then_inc(xsc_ready, 1)
                if gain:
                    turned(FILL["norm", u], (1, 3), xnT, 0, gain, shift)

            def norm_low(u, gain):
                norm(u, None)
                m0 = FILL["norm", u]
                for q in range(4):
                    dve.wait_ge(xh_ready, 4 * (u - u // 3) + q + 1 if u % 3 == 0 else 4 * (u - u // 3 - 1) + q + 1)
                    b = bank_of(m0 + q)
                    for kk in range(2):
                        k = 2 * q + kk
                        ins = dve.scalar_tensor_tensor(out=xl[:, k, :], in0=b[:, kk * SEQ:(kk + 1) * SEQ],
                                                       scalar=gain(k), in1=xh[:, k, :].bitcast(F32), op0=ALU.mult,
                                                       op1=ALU.subtract)
                    ins.then_inc(drained[(m0 + q) % 4], 1)

            def low_block(n0, i, j):
                wait_split(dve, high_in, n0, i, j)
                s = (n0 + j) % SLOTS
                dve.tensor_tensor(ring_low[:, s, :], ring[:, s, :], high_b[:, s, :].bitcast(F32), ALU.subtract)\
                    .then_inc(low_in[s], 1)

            def low_rows(d0, i, c):
                wait_split_d(dve, high_in_d, d0, i, c)
                s = (d0 + c) % SLOTS
                dve.tensor_tensor(ring_d_low[:, s, :], ring_d[:, s, :], high_r[:, s, :].bitcast(F32), ALU.subtract)\
                    .then_inc(low_in_d[s], 1)

            def hidden(g0, m0, d0, i, c):
                dve.wait_ge(gate_ready, i * 4 + (g0 + c + 1))
                if c >= 2:
                    wait_summed(dve, d0, i, c - 2)
                m = m0 + c
                q = m % 2
                dve.tensor_tensor(hid[:, q, :], bank_of(m)[:, SEQ:2 * SEQ], gate_s[:, q, :], ALU.mult)\
                    .then_inc(drained[m % 4], 1)
                wait_drained(dve, m0, i, c)
                dve.tensor_copy(hidh[:, q, :], hid[:, q, :]).then_inc(hid_high, 1)
                dve.wait_ge(hid_high, i * 4 + (g0 + c + 1))
                dve.tensor_tensor(hidl[:, q, :], hid[:, q, :], hidh[:, q, :].bitcast(F32), ALU.subtract)\
                    .then_inc(hid_low, 1)

            def ffn(f, a):
                m0, n0, d0, g0 = FILL["ffn", f], RING["ffn", f], ROWD["ffn", f], NF * f

                def chunk(i, j, more_):
                    hidden(g0, m0, d0, i, j)
                    low_rows(d0, i, j)
                    if j % 2 == 0 and more_:
                        for g in range(2):
                            low_block(n0, i, j + 2 + g)

                for c in range(2):
                    chunk(0, c, True)
                with dve.Fori(0, (NF - 2) // 4 - 1) as i:
                    for j in range(2, 6):
                        chunk(i, j, True)
                for c in range(NF - 4, NF):
                    chunk(0, c, c < NF - 2)
                if f % 2 and f < 2 * DEPTH - 1:
                    for g in range(2):
                        low_block(RING["ffn", f + 1], 0, g)
                wait_summed(dve, d0, 0, NF - 1)
                add_x(0.5)

            def add_x(factor):
                for t in range(NT):
                    for c in range(2):
                        cs = slice(c * 512, (c + 1) * 512)
                        s = step(dve.scalar_tensor_tensor(out=x[:, t, cs], in0=acc[:, t, cs], scalar=factor,
                                                          in1=x[:, t, cs], op0=ALU.mult, op1=ALU.add))
                after_step(s)
                dve.nop().then_inc(acc_free, 1)

            def w_in(l):
                n0 = RING["win", l]
                dve.wait_ge(xs_high, l + 1)
                dve.tensor_tensor(xl[:, :, :], xnT[:, :, :], xh[:, :, :].bitcast(F32), ALU.subtract)\
                    .then_inc(xs_low, 1)

                def low_w_block(i, j):
                    n = n0 + 8 + j
                    wait_split(dve, high_in, n, i)
                    dve.tensor_tensor(ring_low[:, n % SLOTS, :], ring[:, n % SLOTS, :],
                                      high_w[:, n % 2, :].bitcast(F32), ALU.subtract).then_inc(low_in[n % SLOTS], 1)

                link(dve.memset(xraw[:, :, 0:CONV_K - 1], 0.0))

                def taps(ch):
                    return lambda k: cola[:, l, C_CW + k * NX + ch:C_CW + k * NX + ch + 1]

                for q in range(NX // 4):
                    if q == 3:
                        for j in range(2):
                            low_w_block(0, j)
                    chunks = range(4 * q, 4 * q + 4)
                    for m in range(2):
                        wait_drained(dve, FILL["xbc", l] + 2 * q + m)
                    last = {}
                    for ch in chunks:
                        last[ch] = step(dve.tensor_scalar(
                            xc[:, ch, :], xraw[:, ch, CONV_K - 1:], taps(ch)(CONV_K - 1),
                            cola[:, l, C_CB + ch:C_CB + ch + 1], ALU.mult, ALU.add))
                    for k in range(CONV_K - 1):
                        for ch in chunks:
                            after_step(last[ch])
                            ins = dve.scalar_tensor_tensor(out=xc[:, ch, :], in0=xraw[:, ch, k:k + SEQ],
                                                           scalar=taps(ch)(k), in1=xc[:, ch, :],
                                                           op0=ALU.mult, op1=ALU.add)
                            if k < CONV_K - 2:
                                last[ch] = step(ins)
                            else:
                                ins.then_inc(conv_done, 1)
                m = FILL["dt", l]
                wait_filled(dve, m)
                for t in range(NT):
                    ins = dve.tensor_tensor(dr[:, t * HEADS:(t + 1) * HEADS],
                                            bank_of(m)[:, t * HEADS:(t + 1) * HEADS], heads3[:, 0, l, :], ALU.add)
                ins.then_inc(drained[m % 4], 1)
                wait_drained(dve, m)
                dve.scalar_tensor_tensor(out=dn, in0=dr, scalar=-1.0, in1=dr, op0=ALU.mult, op1=ALU.min)\
                    .then_inc(dn_ready, 1)
                low_w_block(0, 2)
                dve.wait_ge(dl_ready, l + 1)
                link(dve.scalar_tensor_tensor(out=dtv, in0=dr, scalar=0.0, in1=dl, op0=ALU.max, op1=ALU.add))
                for t in range(NT):
                    hs = slice(t * HEADS, (t + 1) * HEADS)
                    ins = dve.scalar_tensor_tensor(out=adt[:, hs], in0=dtv[:, hs], scalar=-1.0,
                                                   in1=ea[:, 0:HEADS], op0=ALU.mult, op1=ALU.mult)
                ins.then_inc(adt_ready, 1)
                low_w_block(0, 3)
                with dve.Fori(0, 3) as i:
                    for j in range(4, 8):
                        low_w_block(i, j)

            def heads_of(ap, n):
                return ap.rearrange("p (h e) -> p h e", h=n)

            def ssd(l, a):
                for q in range(8):
                    wait_drained(dve, FILL["qkv", l] + q)
                sq = xdt.rearrange("p a b -> p (a b)")
                for t in range(NT):
                    link(dve.tensor_tensor(sq, qk[:, t, :], qk[:, t, :], ALU.mult))
                    s = step(dve.tensor_reduce(rq[:, t * 32:(t + 1) * 32], heads_of(sq, 32), AX_X, ALU.add))
                    after_step(s)
                dve.tensor_scalar(rq, rq, 1.0 / HD, EPS, ALU.mult, ALU.add).then_inc(sq_ready, 1)
                dve.wait_ge(std_ready2, 2 * l + 1)
                link(dve.reciprocal(rqr, rqs))
                for t in range(NT):
                    ins = dve.tensor_tensor(heads_of(qk[:, t, :], 32), heads_of(qk[:, t, :], 32),
                                            rqr[:, t * 32:(t + 1) * 32].unsqueeze(2).to_broadcast([P, 32, HD]),
                                            ALU.mult)
                ins.then_inc(qk_ready, 1)
                m = FILL["acum", l]
                wait_filled(dve, m)
                link(dve.tensor_scalar(nac, bank_of(m)[:, 0:32], -1.0, None, ALU.mult))
                dve.tensor_tensor(dd[:, 0:HEADS], bank_of(m)[:, 32:48], nac[:, 0:HEADS], ALU.add)\
                    .then_inc(drained[m % 4], 1)
                wait_drained(dve, m)
                dve.nop().then_inc(nac_ready, 1)
                for q in range(4):
                    wait_drained(dve, FILL["xt", l] + q)
                flat = xtok.rearrange("p t e -> p (t e)")
                flat_dt = xdt.rearrange("p t e -> p (t e)")
                link(dve.tensor_tensor(heads_of(flat_dt, 32), heads_of(flat, 32),
                                       dtv.unsqueeze(2).to_broadcast([P, 32, HD]), ALU.mult))
                dve.wait_ge(decay_ready, l + 1)
                wait_drained(dve, FILL["bt", l])
                dve.tensor_tensor(heads_of(xdec, HEADS), heads_of(xdt[:, 0, :], HEADS),
                                  dec[:, 0:HEADS].unsqueeze(2).to_broadcast([P, HEADS, HD]), ALU.mult)\
                    .then_inc(xdt_ready, 1)
                for part_, dst, col in ((0, qT, C_QN), (1, kT, C_KN)):
                    for q in (1, 3):
                        m = FILL["qkt", l] + 4 * part_ + q
                        wait_filled(dve, m)
                        dve.tensor_scalar(dst[:, 2 * q:2 * q + 2, :], bank_of(m).rearrange("p (a b) -> p a b", a=2),
                                          cola[:, l, col:col + 1], None, ALU.mult).then_inc(drained[m % 4], 1)
                link(dve.tensor_tensor(
                    flat.rearrange("p (t h e) -> p t h e", t=NT, h=HEADS)[:, 0], heads_of(xtok[:, 0, :], HEADS),
                    heads3[:, 2, l, :].unsqueeze(2).to_broadcast([P, HEADS, HD]), ALU.mult))
                link(dve.tensor_tensor(
                    heads_of(xtok[:, 1, :], HEADS), heads_of(xtok[:, 1, :], HEADS),
                    heads3[:, 2, l, :].unsqueeze(2).to_broadcast([P, HEADS, HD]), ALU.mult))
                for c in range(NT):
                    m = FILL["cb", l] + c
                    wait_filled(dve, m)
                    dve.tensor_tensor(cbm[:, c], bank_of(m).rearrange("p (a b) -> p a b", a=GROUPS),
                                      tri.unsqueeze(1).to_broadcast([P, GROUPS, P]), ALU.mult)\
                        .then_inc(drained[m % 4], 1)

                def decays(s):
                    c, g = divmod(s, GROUPS)
                    m = FILL["bc", l] + s
                    wait_filled(dve, m)
                    if s >= 2:
                        dve.wait_ge(y_done, 8 * l + s - 1)
                    for r in range(HPG):
                        col = c * HEADS + g * HPG + r
                        ins = dve.tensor_scalar(seg[:, s % 2, r * P:(r + 1) * P], bank_of(m)[:, r * P:(r + 1) * P],
                                                nac[:, col:col + 1], 0.0, ALU.add, ALU.min)
                    ins.then_inc(drained[m % 4], 1)
                    wait_drained(dve, m)
                    dve.nop().then_inc(seg_ready, 1)

                def mixes(s):
                    c, g = divmod(s, GROUPS)
                    dve.wait_ge(seg_exp, 8 * l + s + 1)
                    sv = seg[:, s % 2, :].rearrange("p (a b) -> p a b", a=HPG)
                    dve.tensor_tensor(sv, sv, cbm[:, c, g, :].unsqueeze(1).to_broadcast([P, HPG, P]), ALU.mult)\
                        .then_inc(mix_ready, 1)

                for s in range(9):
                    if s < 8:
                        decays(s)
                    if s >= 1:
                        mixes(s - 1)
                dve.wait_ge(y_done, 8 * (l + 1))
                for t in range(NT):
                    for c in range(2):
                        cs = slice(c * 512, (c + 1) * 512)
                        s = step(dve.tensor_tensor(xtok[:, t, cs], xtok[:, t, cs], acc[:, t, cs], ALU.add))
                after_step(s)
                dve.nop().then_inc(acc_free, 1)
                for q in range(2):
                    m = FILL["off", l] + q
                    wait_filled(dve, m)
                    o = xdt[:, 0, 0:512]
                    dve.tensor_tensor(heads_of(o, 8), heads_of(bank_of(m), 8),
                                      ex[:, HEADS + 8 * q:HEADS + 8 * q + 8].unsqueeze(2).to_broadcast([P, 8, HD]),
                                      ALU.mult).then_inc(drained[m % 4], 1)
                    wait_drained(dve, m)
                    cs = slice(q * 512, (q + 1) * 512)
                    link(dve.tensor_tensor(xtok[:, 1, cs], xtok[:, 1, cs], o, ALU.add))
                link(dve.tensor_tensor(flat, flat, z.rearrange("p t e -> p (t e)"), ALU.mult))
                link(dve.tensor_tensor(flat_dt, flat, flat, ALU.mult))
                link(dve.tensor_reduce(gs, heads_of(flat_dt, 8), AX_X, ALU.add))
                dve.tensor_scalar(gs, gs, 1.0 / BLK, EPS, ALU.mult, ALU.add).then_inc(sq_ready, 1)
                dve.wait_ge(std_ready2, 2 * l + 2)
                link(dve.reciprocal(gsr, gss))
                dve.tensor_tensor(heads_of(flat, 8), heads_of(flat, 8), gsr.unsqueeze(2).to_broadcast([P, 8, BLK]),
                                  ALU.mult).then_inc(ysd_ready, 1)

            def attention(l, a):
                m0 = FILL["att", l]

                def maxima(h):
                    m = m0 + AF["S", h]
                    wait_filled(dve, m)
                    if h >= 3:
                        wait_filled(dve, m0 + AF["T", h - 3])
                    dve.tensor_tensor_reduce(sp3[:, h % 3, 0:P], bank_of(m)[:, 0:P], konst[:, K_NEG:K_NEG + P],
                                             1.0, NEG, ALU.add, ALU.max, mx[:, 2 * h:2 * h + 1])
                    dve.tensor_tensor_reduce(sp3[:, h % 3, P:3 * P], bank_of(m)[:, P:3 * P],
                                             konst[:, K_NEG + P:K_NEG + 3 * P],
                                             1.0, NEG, ALU.add, ALU.max, mx[:, 2 * h + 1:2 * h + 2])\
                        .then_inc(drained[m % 4], 1)
                    wait_drained(dve, m)
                    dve.tensor_scalar(nmx[:, 2 * h:2 * h + 2], mx[:, 2 * h:2 * h + 2], -(HD ** -0.5), None,
                                      ALU.mult).then_inc(smax_ready, 1)

                def weights(h):
                    dve.wait_ge(p_exp, HEADS * l + h + 1)
                    dve.tensor_tensor_reduce(sp3[:, h % 3, 0:P], sp3[:, h % 3, 0:P], konst[:, K_CNT:K_CNT + P],
                                             1.0, 0.0, ALU.mult, ALU.add, den[:, h:h + 1])
                    dve.tensor_tensor_reduce(sp3[:, h % 3, P:3 * P], sp3[:, h % 3, P:3 * P],
                                             konst[:, K_CNT + P:K_CNT + 3 * P],
                                             1.0, 0.0, ALU.mult, ALU.add, den[:, HEADS + h:HEADS + h + 1])\
                        .then_inc(p_ready, 1)

                for h in range(HEADS + 1):
                    if h < HEADS:
                        maxima(h)
                    if h >= 1:
                        weights(h - 1)
                dve.wait_ge(p_ready, HEADS * (l + 1))
                link(dve.reciprocal(rden, den))
                dve.wait_ge(av_done, HEADS * (l + 1))
                for t in range(NT):
                    for c in range(2):
                        cs = slice(c * 512, (c + 1) * 512)
                        rs = rden[:, t * HEADS + 8 * c:t * HEADS + 8 * c + 8]
                        s = step(dve.tensor_tensor(heads_of(yatt[:, t, cs], 8), heads_of(acc[:, t, cs], 8),
                                                   rs.unsqueeze(2).to_broadcast([P, 8, HD]), ALU.mult))
                after_step(s)
                dve.nop().then_inc(acc_free, 1)
                dve.nop().then_inc(yatt_ready, 1)

            def modulation(p):
                m = FILL["mod", p]
                wait_filled(dve, m)
                dve.tensor_tensor(mod[:, p, :], bank_of(m)[:, 0:KD], colb[:, B_ADA + KD * p:B_ADA + KD * (p + 1)],
                                  ALU.add).then_inc(drained[m % 4], 1)
                wait_drained(dve, m)

            def decays2():
                link(dve.memset(attn.rearrange("p a b -> p (a b)"), 0.0))
                link(dve.memset(lev_e[:, 1, 0:P], 1.0))
                link(dve.memset(zpad[:, :, 0:CONV_W - 1], 0.0))
                flat = graw.rearrange("p h s -> p (h s)")
                for q in range(2):
                    m = FILL["a2"] + q
                    wait_filled(dve, m)
                    for hh in range(2):
                        h = 2 * q + hh
                        ins = dve.tensor_scalar(graw[:, h, :], bank_of(m)[:, hh * SEQ:(hh + 1) * SEQ],
                                                colb[:, B_A2 + h:B_A2 + h + 1], None, ALU.add)
                    ins.then_inc(drained[m % 4], 1)
                for q in range(2):
                    wait_drained(dve, FILL["a2"] + q)
                dve.scalar_tensor_tensor(out=lev_e[:, 0, :], in0=flat, scalar=-1.0, in1=flat, op0=ALU.mult,
                                         op1=ALU.min).then_inc(gl_ready, 1)
                dve.wait_ge(gl_log, 1)
                link(dve.scalar_tensor_tensor(out=flat, in0=flat, scalar=0.0, in1=lev_e[:, 0, :],
                                              op0=ALU.min, op1=ALU.subtract))
                for h in range(GH):
                    for t in range(NT):
                        ts = slice(t * P, (t + 1) * P)
                        s = step(dve.tensor_tensor_scan(bcum[:, h, ts], lev_e[:, 1, 0:P], graw[:, h, ts], 0.0,
                                                        ALU.mult, ALU.add))
                after_step(s)
                for j in range(4):
                    wait_drained(dve, FILL["qk2"] + j)

            def level(s):
                e, o = lev_e[:, s % 2, :], lev_qk[:, s % 2, :]
                if s < len(LEVELS):
                    w = LEVELS[s]
                    ev, bv = (a.rearrange("p (n w) -> p n w", w=2 * w) for a in (e, bcum.rearrange("p h s -> p (h s)")))
                    mid = bv[:, :, w - 1:w].to_broadcast([P, GH * SEQ // (2 * w), w])
                    dve.tensor_tensor(ev[:, :, 0:w], mid, bv[:, :, 0:w], ALU.subtract)
                    dve.tensor_tensor(ev[:, :, w:2 * w], bv[:, :, w:2 * w], mid, ALU.subtract).then_inc(lev_ready, 1)
                    first, second = slice(0, w), slice(w, 2 * w)
                    n, width = GH * SEQ // (2 * w), 2 * w
                else:
                    ev = e.rearrange("p (h s) -> p h s", h=GH)
                    dve.tensor_tensor(ev[:, :, 0:P], bcum[:, :, P - 1:P].to_broadcast([P, GH, P]), bcum[:, :, 0:P],
                                      ALU.subtract)
                    dve.tensor_copy(ev[:, :, P:SEQ], bcum[:, :, P:SEQ]).then_inc(lev_ready, 1)
                    first, second = slice(0, P), slice(P, SEQ)
                    width = SEQ
                dve.wait_ge(lev_exp, s + 1)
                if s >= 2:
                    wait_filled(dve, FILL["pairs"] + 2 * (s - 2) + 1)
                ev, ov, qv, kv = (a.rearrange("p (n w) -> p n w", w=width) for a in
                                  (e, o, q2k2[:, 0:GH, :].rearrange("p h s -> p (h s)"),
                                   q2k2[:, GH:2 * GH, :].rearrange("p h s -> p (h s)")))
                dve.tensor_tensor(ov[:, :, first], ev[:, :, first], kv[:, :, first], ALU.mult)
                dve.tensor_tensor(ov[:, :, second], ev[:, :, second], qv[:, :, second], ALU.mult)\
                    .then_inc(lev_qk_ready, 1)

            def gated():
                for j in range(4):
                    wait_drained(dve, FILL["pc"] + j)
                link(dve.tensor_tensor(zpad[:, :, CONV_W - 1:], pc[:, 0:NC2, :], pc[:, NC2:2 * NC2, :], ALU.mult))
                last = [0] * NC2
                for c in range(NC2):
                    last[c] = step(dve.tensor_scalar(zc[:, c, :], zpad[:, c, 0:SEQ], colc[:, c:c + 1],
                                                     colb[:, B_DW + c:B_DW + c + 1], ALU.mult, ALU.add))
                for k in range(1, CONV_W):
                    for c in range(NC2):
                        after_step(last[c])
                        last[c] = step(dve.scalar_tensor_tensor(
                            out=zc[:, c, :], in0=zpad[:, c, k:k + SEQ], scalar=colc[:, k * NC2 + c:k * NC2 + c + 1],
                            in1=zc[:, c, :], op0=ALU.mult, op1=ALU.add))
                after_step(last[NC2 - 1])
                dve.nop().then_inc(z_out, 1)

            def gla():
                dve.wait_ge(masks_in, 16)
                for s in range(len(LEVELS) + 1):
                    for t in range(NT):
                        m = FILL["pairs"] + 2 * s + t
                        wait_filled(dve, m)
                        dve.copy_predicated(attn[:, t * GH:(t + 1) * GH, :],
                                            masks[:, s:s + 1, :].bitcast(U32).to_broadcast([P, GH, P]),
                                            bank_of(m).rearrange("p (a b) -> p a b", a=GH))\
                            .then_inc(drained[m % 4], 1)
                        wait_drained(dve, m)
                    if s + 2 <= len(LEVELS):
                        level(s + 2)
                m = FILL["cross"]
                wait_filled(dve, m)
                dve.tensor_copy(across.rearrange("p a b -> p (a b)"), bank_of(m)).then_inc(drained[m % 4], 1)
                for h in range(GH):
                    wait_drained(dve, FILL["o"] + h)
                dve.tensor_tensor(osq, oT, oT, ALU.mult).then_inc(o_sq, 1)
                for q in range(2):
                    m = FILL["osum"] + q
                    wait_filled(dve, m)
                    ins = dve.tensor_scalar(rg[:, 2 * q:2 * q + 2, :], bank_of(m).rearrange("p (a b) -> p a b", a=2),
                                            1.0 / DV, EPS, ALU.mult, ALU.add).then_inc(drained[m % 4], 1)
                for q in range(2):
                    wait_drained(dve, FILL["osum"] + q)
                dve.nop().then_inc(var2, 1)
                dve.wait_ge(std2, 1)
                link(dve.reciprocal(rg, rgs))
                for j in range(4):
                    wait_drained(dve, FILL["r"] + j)
                o4 = oT.rearrange("p (h c) s -> p h c s", h=GH)
                for c in range(2):
                    s = step(dve.tensor_tensor(o4[:, :, c, :], o4[:, :, c, :], rg, ALU.mult))
                after_step(s)
                for k in range(KD):
                    ins = dve.scalar_tensor_tensor(out=oT[:, k, :], in0=oT[:, k, :],
                                                   scalar=colb[:, B_GLA + k:B_GLA + k + 1], in1=rT[:, k, :],
                                                   op0=ALU.mult, op1=ALU.mult)
                ins.then_inc(og_ready, 1)

            def conv_branch():
                m = FILL["mean"]
                wait_filled(dve, m)
                dve.tensor_scalar(mean, bank_of(m)[:, 0:SEQ], 1.0 / CW2, None, ALU.mult).then_inc(drained[m % 4], 1)
                wait_drained(dve, m)
                link(dve.tensor_tensor(zc, zc, mean.unsqueeze(1).to_broadcast([P, NC2, SEQ]), ALU.subtract))
                dve.tensor_tensor(zsq, zc, zc, ALU.mult).then_inc(z_out, 1)
                m = FILL["var"]
                wait_filled(dve, m)
                dve.tensor_scalar(mean, bank_of(m)[:, 0:SEQ], 1.0 / CW2, EPS, ALU.mult, ALU.add)\
                    .then_inc(drained[m % 4], 1)
                wait_drained(dve, m)
                dve.nop().then_inc(var2, 1)
                dve.wait_ge(std2, 2)
                link(dve.reciprocal(mean, mean))
                dve.tensor_tensor(zc, zc, mean.unsqueeze(1).to_broadcast([P, NC2, SEQ]), ALU.mult)\
                    .then_inc(zn_ready, 1)

            def merge():
                for j in range(8):
                    wait_drained(dve, FILL["gates"] + j)
                for q in range(4):
                    m = FILL["pwa", 0] + q
                    if q % 2:
                        wait_slot_read(dve, RING["pw"] + q // 2)
                    else:
                        wait_filled(dve, m)
                    for c in range(2):
                        k = 2 * q + c
                        ins = dve.scalar_tensor_tensor(out=merged[:, k, :], in0=bank_of(m)[:, c * SEQ:(c + 1) * SEQ],
                                                       scalar=colb[:, B_PW + k:B_PW + k + 1], in1=gT[:, k, :],
                                                       op0=ALU.add, op1=ALU.mult)
                    ins.then_inc(drained[m % 4], 1)
                for q in range(4):
                    m = FILL["ygla"] + q
                    ks = slice(2 * q, 2 * q + 2)
                    wait_slot_read(dve, RING["glao"] + q)
                    wait_drained(dve, FILL["pwa", 0] + q)
                    dve.tensor_tensor(osq[:, ks, :], bank_of(m).rearrange("p (a b) -> p a b", a=2),
                                      gT[:, KD + 2 * q:KD + 2 * q + 2, :], ALU.mult).then_inc(drained[m % 4], 1)
                    wait_drained(dve, m)
                    s = step(dve.tensor_tensor(merged[:, ks, :], merged[:, ks, :], osq[:, ks, :], ALU.add))
                after_step(s)
                dve.nop().then_inc(merged_ready, 1)
                diagonal(mod[:, GA1, :])
                n = RING["wout2"] + 3
                wait_slot_read(dve, n)
                for q in range(2):
                    wait_drained(dve, FILL["garow"] + q)
                for t in range(NT):
                    for c in range(2):
                        cs = slice(c * 512, (c + 1) * 512)
                        s = step(dve.tensor_tensor(xsc[:, t, cs], acc[:, t, cs], garow[:, cs], ALU.mult))
                after_step(s)
                dve.nop().then_inc(acc_free, 1)
                link(dve.tensor_tensor(x[:, :, :], x[:, :, :], xsc, ALU.add))

            def diagonal(col):
                dve.tensor_tensor(diag.rearrange("p (k m) -> p k m", k=KD),
                                  ident.unsqueeze(1).to_broadcast([P, KD, P]),
                                  col.unsqueeze(2).to_broadcast([P, KD, P]), ALU.mult).then_inc(diag_ready, 1)

            def routing():
                m = FILL["router"]
                wait_filled(dve, m)
                n36 = N_GROUPS + EXPERTS
                dve.tensor_tensor(logit, bank_of(m)[:, 0:NT * n36].rearrange("p (t e) -> p t e", t=NT),
                                  br[:, :].unsqueeze(1).to_broadcast([P, NT, n36]), ALU.add)\
                    .then_inc(drained[m % 4], 1)
                wait_drained(dve, m)
                lg, le = logit[:, :, 0:N_GROUPS], logit[:, :, N_GROUPS:]

                def first_max(score, width, top, mark):
                    link(dve.tensor_reduce(top, score, AX_X, ALU.max))
                    link(dve.tensor_tensor(mark, score, top.to_broadcast([P, NT, width]), ALU.is_equal))
                    link(dve.tensor_tensor(mark, mark, rank[:, 0:width].unsqueeze(1).to_broadcast([P, NT, width]),
                                           ALU.mult))
                    link(dve.tensor_reduce(rt_r, mark, AX_X, ALU.max))
                    link(dve.tensor_tensor(mark, mark, rt_r.to_broadcast([P, NT, width]), ALU.is_equal))

                for e in range(EXPERTS):
                    s = step(dve.memset(rank[:, e:e + 1], float(EXPERTS - e)))
                after_step(s)
                first_max(lg, N_GROUPS, rt_mg, rt_og)
                link(dve.tensor_tensor(rt_gd, lg, rt_mg.to_broadcast([P, NT, N_GROUPS]), ALU.subtract))
                link(dve.tensor_scalar(rt_pen, rt_og, -NEG, NEG, ALU.mult, ALU.add))
                for t in range(NT):
                    s = step(dve.tensor_tensor(
                        cand[:, t, :].rearrange("p (g e) -> p g e", g=N_GROUPS),
                        le[:, t, :].rearrange("p (g e) -> p g e", g=N_GROUPS),
                        rt_pen[:, t, :].unsqueeze(2).to_broadcast([P, N_GROUPS, PER_GROUP]), ALU.add))
                after_step(s)
                first_max(cand, EXPERTS, rt_m1, mark1)
                link(dve.scalar_tensor_tensor(out=cand, in0=mark1, scalar=2 * NEG, in1=cand,
                                              op0=ALU.mult, op1=ALU.add))
                first_max(cand, EXPERTS, rt_m2, mark2)
                dve.tensor_tensor(rt_pd, rt_m2, rt_m1, ALU.subtract).then_inc(rt_in, 1)
                dve.wait_ge(rt_exp, 1)
                link(dve.tensor_reduce(rt_m, rt_ge, AX_X, ALU.add))
                link(dve.scalar_tensor_tensor(out=rt_m, in0=rt_pe, scalar=1.0, in1=rt_m, op0=ALU.add, op1=ALU.mult))
                link(dve.reciprocal(rt_m, rt_m))
                link(dve.memset(comb.rearrange("p a b -> p (a b)"), 0.0))
                cv = comb[:, :, 0:EXPERTS]
                for t in range(NT):
                    link(dve.scalar_tensor_tensor(out=cv[:, t, :], in0=mark2[:, t, :], scalar=rt_pe[:, t, :],
                                                  in1=mark1[:, t, :], op0=ALU.mult, op1=ALU.add))
                    link(dve.tensor_scalar(cv[:, t, :], cv[:, t, :], rt_m[:, t, :], None, ALU.mult))
                dve.tensor_tensor(mark1, mark1, mark2, ALU.add).then_inc(mask_ready, 1)

            def rows_and_tokens():
                for i, (col, dst) in enumerate(((gains[:, 1, :], row2[:, 0, :]), (mod[:, SH2, :], row2[:, 1, :]),
                                                (mod[:, GA2, :], rowf[:, 0, :]), (gains[:, 2, :], rowf[:, 1, :]),
                                                (mod[:, SHF, :], rowf[:, 2, :]))):
                    diagonal(col)
                    for q in range(2):
                        m = FILL["rows"] + 2 * i + q
                        wait_filled(dve, m)
                        dve.tensor_copy(dst[:, q * 512:(q + 1) * 512], bank_of(m)).then_inc(drained[m % 4], 1)
                for q in range(10):
                    wait_drained(dve, FILL["rows"] + q)
                for t in range(NT):
                    link(dve.tensor_tensor(u2[:, t, :], xsc[:, t, :], row2[:, 0, :], ALU.mult))
                    link(dve.tensor_tensor(u2[:, t, :], u2[:, t, :], row2[:, 1, :], ALU.add))
                dve.tensor_tensor(join, ident[:, 0:CAP], ident[:, CAP:P], ALU.add).then_inc(zero_ready, 1)

            def placing():
                m = FILL["count"]
                wait_filled(dve, m)
                b = bank_of(m)
                link(dve.memset(place.rearrange("p a b -> p (a b)"), -1.0))
                link(dve.tensor_tensor(place[:, :, 0:EXPERTS], b[:, 0:2 * EXPERTS].rearrange("p (t e) -> p t e", t=NT),
                                       mark1, ALU.mult))
                link(dve.tensor_scalar(place[:, :, 0:EXPERTS], place[:, :, 0:EXPERTS], -1.0, None, ALU.add))
                dve.tensor_reduce(number[:, 0, :], b[:, 2 * EXPERTS:3 * EXPERTS], AX_X, ALU.max)\
                    .then_inc(drained[m % 4], 1)
                wait_drained(dve, m)
                dve.tensor_scalar(flag[:, :], number[:, 0, :], CAP + 0.5, None, ALU.is_lt).then_inc(flag_ready, 1)

            def gathered_experts():
                g0 = 2 * DEPTH * NF
                iota = konst[:, K_IOTA:K_IOTA + CAP]

                def at_(a, t, e):
                    return a[:, t, e:e + 1] if isinstance(e, int) else a[:, t, bass.ds(e, 1)]

                def choose(e):
                    for half in range(2):
                        for t in range(NT):
                            ins = dve.tensor_scalar(sel[:, t, half * CAP:(half + 1) * CAP], iota,
                                                    at_(place, t, e + half), None, ALU.is_equal)
                    ins.then_inc(sel_ready, 1)

                def weigh(e):
                    for half in range(2):
                        for t in range(NT):
                            ins = dve.tensor_scalar(selw[:, t, half * CAP:(half + 1) * CAP], iota,
                                                    at_(place, t, e + half), at_(comb, t, e + half),
                                                    ALU.is_equal, ALU.mult)
                    ins.then_inc(selw_ready, 1)

                def low(i, half, x):
                    wait_pair_split(dve, high_in, half, i, x)
                    s = (RING["moe"] + x) % SLOTS
                    dve.tensor_tensor(ring_low[:, s, :], ring[:, s, :], high_b[:, s, :].bitcast(F32), ALU.subtract)\
                        .then_inc(low_in[s], 1)

                def low_d(i, half, c):
                    wait_pair_split_d(dve, high_in_d, half, i, c)
                    s = (ROWD["moe"] + c) % SLOTS
                    dve.tensor_tensor(ring_d_low[:, s, :], ring_d[:, s, :], high_r[:, s, :].bitcast(F32),
                                      ALU.subtract).then_inc(low_in_d[s], 1)

                def products(i, half, j):
                    wait_pair_read(dve, half, i, 1)
                    dve.tensor_copy(both[:, 0, :, :].rearrange("p a b -> p (a b)"), bank_of(M0 + j))\
                        .then_inc(drained[(M0 + j) % 4], 1)

                def hidden_e(i, half):
                    j = JOINED[half]
                    hs = slice(half * CAP, (half + 1) * CAP)

                    def by_chunk(a):
                        return a.rearrange("p (a b) -> p a b", a=CPE)

                    dve.wait_ge(gate_ready, i * 2 + (g0 + half + 1))
                    dve.tensor_tensor(hid_e[:, :, hs], by_chunk(bank_of(M0 + j)[:, BLK:2 * BLK]),
                                      by_chunk(gate_e[:, half * BLK:(half + 1) * BLK]), ALU.mult)\
                        .then_inc(drained[(M0 + j) % 4], 1)
                    wait_pair_drained(dve, i, j)
                    dve.tensor_copy(heh[:, :, hs], hid_e[:, :, hs]).then_inc(hid_high, 1)
                    dve.wait_ge(hid_high, i * 2 + (g0 + half + 1))
                    dve.tensor_tensor(hel[:, :, hs], hid_e[:, :, hs], heh[:, :, hs].bitcast(F32), ALU.subtract)\
                        .then_inc(hid_low, 1)

                def tokens(i, groups):
                    for q in groups:
                        dve.wait_ge(ue_high, i * 4 + (4 + q + 1))
                        j = TOKENS[q]
                        dve.tensor_tensor(ue[:, 2 * q:2 * q + 2, :, CAP:2 * CAP],
                                          bank_of(M0 + j)[:, 0:2 * P].rearrange("p (a b c) -> p a b c", a=2, b=2),
                                          ue[:, 2 * q:2 * q + 2, :, 0:CAP].bitcast(F32), ALU.subtract)\
                            .then_inc(drained[(M0 + j) % 4], 1)

                def first_weights(i):
                    for x in range(4):
                        low(i, 0, x)
                    products(i, 0, 0)
                    for c in range(CPE):
                        low_d(i, 0, c)

                def pair(i, last):
                    i2 = i * 2
                    hidden_e(i, 0)
                    for x in range(2):
                        low(i, 1, x)
                    wait_pair_filled(dve, i, F_CHOICE[1])
                    choose(i2 + 2)
                    if not last:
                        weigh(i2 + 2)
                    for x in range(2, 4):
                        low(i, 1, x)
                    products(i, 1, 7)
                    for c in range(CPE):
                        low_d(i, 1, c)
                    tokens(i, range(2))
                    hidden_e(i, 1)
                    tokens(i, range(2, 4))
                    if not last:
                        first_weights(i + 1)

                choose(0)
                weigh(0)
                dve.memset(hid_e, 0.0).then_inc(zero_ready, 1)
                dve.wait_ge(zero_ready, 2)
                dve.tensor_copy(heh, hid_e).then_inc(zero_ready, 1)
                dve.tensor_copy(hel, hid_e).then_inc(zero_ready, 1)
                tokens(-1, range(4))
                wait_pair_drained(dve, 0, -9)
                dve.memset(selT, 0.0).then_inc(drained[(M0 - 5) % 4], 1)
                for c in range(2):
                    wait_pair_drained(dve, 0, c - 6)
                    dve.memset(out_e[:, c * 512:(c + 1) * 512], 0.0).then_inc(drained[(M0 + c - 2) % 4], 1)
                first_weights(0)
                with dve.Fori(0, EXPERTS // 2 - 1) as i:
                    pair(i, False)
                pair(EXPERTS // 2 - 1, True)
                dve.wait_ge(scattered, 1)
                for t in range(NT):
                    for c in range(2):
                        cs = slice(c * 512, (c + 1) * 512)
                        ins = dve.tensor_copy(y2[:, t, cs], acc[:, t, cs])
                ins.then_inc(y_ready, 1)

            def experts():
                m0, g0 = FILL["moe"], 2 * DEPTH * NF

                def hidden8(i, c):
                    dve.wait_ge(gate_ready, i * 8 + (g0 + c + 1))
                    if c >= 2:
                        half, cc = divmod((c - 2) % 8, CPE)
                        wait_pair_summed(dve, half, i + (c - 2) // 8, cc)
                    m = m0 + c
                    dve.tensor_tensor(hid[:, m % 2, :], bank_of(m)[:, SEQ:2 * SEQ], gate_s[:, m % 2, :], ALU.mult)\
                        .then_inc(drained[m % 4], 1)

                def add_expert(i, half):
                    dve.wait_ge(acc_free, i * 2 + (A1 + 1 + half))
                    wait_pair_summed(dve, half, i, CPE - 1)
                    for t in range(NT):
                        for c in range(2):
                            cs = slice(c * 512, (c + 1) * 512)
                            e = i * 2 + half
                            w = comb[:, t, e:e + 1] if isinstance(e, int) else comb[:, t, bass.ds(e, 1)]
                            ins = dve.scalar_tensor_tensor(out=y2[:, t, cs], in0=acc[:, t, cs], scalar=w,
                                                           in1=y2[:, t, cs], op0=ALU.mult, op1=ALU.add)
                    return ins

                dve.memset(y2.rearrange("p a b -> p (a b)"), 0.0).then_inc(zero_ready, 1)
                dve.wait_ge(zero_ready, 2)
                for c in range(CPE):
                    hidden8(0, c)
                with dve.Fori(0, EXPERTS // 2 - 1) as i:
                    for half in range(2):
                        hidden8(i, CPE * (half + 1))
                        add_expert(i, half).then_inc(acc_free, 1)
                        for j in range(1, CPE):
                            hidden8(i, CPE * (half + 1) + j)
                i = EXPERTS // 2 - 1
                hidden8(i, CPE)
                add_expert(i, 0).then_inc(acc_free, 1)
                for j in range(1, CPE):
                    hidden8(i, CPE + j)
                add_expert(i, 1).then_inc(y_ready, 1)

            def final():
                dve.wait_ge(y_ready, 1)
                for t in range(NT):
                    link(dve.tensor_tensor(y2[:, t, :], y2[:, t, :], rowf[:, 0, :], ALU.mult))
                    link(dve.tensor_tensor(x[:, t, :], x[:, t, :], y2[:, t, :], ALU.add))
                norm(U1 + 2, None)
                dve.wait_ge(xsc_ready, U1 + 3)
                for t in range(NT):
                    link(dve.tensor_tensor(xsc[:, t, :], xsc[:, t, :], rowf[:, 1, :], ALU.mult))
                    s = step(dve.tensor_tensor(x[:, t, :], xsc[:, t, :], rowf[:, 2, :], ALU.add))
                after_step(s)
                dve.nop().then_inc(y_final, 1)

            dve.memset(ones[:, :], 1.0).then_inc(ones_set, 1)
            for i, dst in enumerate((cola[:, 0, :], cola[:, 1, :], colb[:, :], colc[:, :])):
                wait_filled(dve, i)
                dve.tensor_copy(dst, bank_of(i)[:, 0:dst.shape[1]]).then_inc(drained[i], 1)
            for i in range(4):
                wait_drained(dve, i)
            dve.wait_ge(x_in, 16)
            for l in range(DEPTH):
                if not l:
                    for g in range(2):
                        low_block(RING["ffn", 0], 0, g)
                norm_low(3 * l, lambda k: cola[:, l, C_FFN1 + k:C_FFN1 + k + 1])
                ffn(2 * l, 5 * l)
                modulation(4 * l)
                norm(3 * l + 1, lambda k: cola[:, l, C_MIX + k:C_MIX + k + 1])
                w_in(l)
                modulation(4 * l + 1)
                ssd(l, 5 * l + 1)
                attention(l, 5 * l + 2)
                turned(FILL["yt", l], (1, 3), yT, 0, lambda k: cola[:, l, C_SSD + k:C_SSD + k + 1])
                turned(FILL["yt", l] + 4, (1, 3), yT, KD, lambda k: 1.0)
                for g in range(2):
                    low_block(RING["ffn", 2 * l + 1], 0, g)
                wait_slot_read(dve, RING["wout", l] + 7)
                add_x(1.0)
                modulation(4 * l + 2)
                norm_low(3 * l + 2, lambda k: cola[:, l, C_FFN2 + k:C_FFN2 + k + 1])
                ffn(2 * l + 1, 5 * l + 4)
                modulation(4 * l + 3)
            for i, (col, sc) in enumerate(((B_N1, SC1), (B_N2, SC2), (B_NF, SCF))):
                s = step(dve.scalar_tensor_tensor(out=gains[:, i, :], in0=mod[:, sc, :], scalar=1.0,
                                                  in1=colb[:, col:col + KD], op0=ALU.add, op1=ALU.mult))
            after_step(s)
            norm(U1, lambda k: gains[:, 0, k:k + 1], shift=lambda k: mod[:, SH1, k:k + 1])
            decays2()
            level(0)
            level(1)
            gated()
            gla()
            conv_branch()
            merge()
            norm(U1 + 1, lambda k: gains[:, 1, k:k + 1], shift=lambda k: mod[:, SH2, k:k + 1])
            routing()
            rows_and_tokens()
            placing()
            dve.wait_ge(flag_ready, 1)
            few = dve.value_load(flag[0:1, 0:1], min_val=0, max_val=1)
            with dve.If(few > 0):
                gathered_experts()
            with dve.Else():
                experts()
            final()




_INS = ["x", "ffn1_norm", "ffn1_w_gate", "ffn1_w_up", "ffn1_w_down", "mix_norm", "w_in", "conv_w", "conv_b",
        "dt_bias", "a_log", "d_skip", "ssd_norm", "q_norm", "k_norm", "w_out", "ffn2_norm", "ffn2_w_gate",
        "ffn2_w_up", "ffn2_w_down", "c_2", "w_ada_2", "b_ada_2", "g_norm1_2", "w_in_2", "w_dw_2", "b_dw_2",
        "g_conv_ln_2", "b_conv_ln_2", "w_conv_pw_2", "b_conv_pw_2", "w_a2_2", "b_a2_2", "g_gla_norm_2",
        "w_gla_o_2", "w_out_2", "g_norm2_2", "w_router_g_2", "b_router_g_2", "w_router_e_2", "b_router_e_2",
        "w1_2", "w3_2", "w2_2", "w_ada_f_2", "b_ada_f_2", "g_final_2"]
_OUTS = [((1, 256, 1024), "float32")]


def kernel(**inputs):
    import numpy as _np
    import concourse.bacc as _bacc
    from concourse import mybir as _mybir
    from concourse.bass_utils import run_bass_kernel_spmd as _run

    nc = _bacc.Bacc("TRN2", target_bir_lowering=False, num_devices=1)
    arrays, args = {}, {}
    for name in _INS:
        a = _np.ascontiguousarray(inputs[name])
        arrays[f"in_{name}_dram"] = a
        args[name] = nc.dram_tensor(f"in_{name}_dram", a.shape, _mybir.dt.from_np(a.dtype), kind="ExternalInput").ap()
    for name, table in (("consts", constants()), ("masks", pair_masks())):
        arrays[f"in_{name}_dram"] = table
        args[name] = nc.dram_tensor(f"in_{name}_dram", table.shape, F32, kind="ExternalInput").ap()
    (shape, dtype), = _OUTS
    out = nc.dram_tensor("out_0_dram", shape, _mybir.dt.from_np(_np.dtype(dtype)), kind="ExternalOutput").ap()
    two_blocks(nc, args, out)
    r = _run(nc, [arrays], core_ids=[0])
    return r.results[0]["out_0_dram"]
```
